# Optimizing a Trainium2 kernel written in Bass

```python
import math
import jax, jax.numpy as jnp
from jax import lax
import numpy as np
import jax
import jax.numpy as jnp

D_MODEL = 1024
BATCH = 1
SEQ = 256
DEPTH = 2

D_MIX = D_MODEL
D_A = D_MIX // 4
H_A = 4
HD_A = D_A // H_A
CHUNK = 128
D_B = D_MIX // 2
H_B = 4
DH_B = D_B // (2 * H_B)
D_C = D_MIX // 4
G_C = 4
GD_C = D_C // G_C
POOL_WINDOWS = (2, 4, 8, 16)
D_IN = 2 * D_A + 3 * D_B + D_C
Q_BLOCK = 128
NUM_BUCKETS = 32
MAX_EXACT = NUM_BUCKETS // 2
MAX_DISTANCE = 128
D_FF = 2816
N_EXPERTS = 8
TOP_K = 2
D_FF_EXPERT = 3584
N_DENSE = (DEPTH + 1) // 2
N_MOE = DEPTH // 2
ALPHA = (2 * DEPTH) ** 0.25
BETA = (8 * DEPTH) ** -0.25
EPS = 1e-5


F32 = jnp.float32

def layer_norm(x, g, b):
    xf = x.astype(F32)
    mu = jnp.mean(xf, axis=-1, keepdims=True)
    var = jnp.mean(jnp.square(xf - mu), axis=-1, keepdims=True)
    return ((xf - mu) * lax.rsqrt(var + EPS) * g.astype(F32) + b.astype(F32)).astype(x.dtype)

def rms_norm(x, g):
    xf = x.astype(F32)
    ms = jnp.mean(jnp.square(xf), axis=-1, keepdims=True)
    return (xf * lax.rsqrt(ms + EPS) * g.astype(F32)).astype(x.dtype)

def t5_bucket(dist):
    n = jnp.maximum(dist, 0)
    nf = jnp.maximum(n, 1).astype(F32)
    large = MAX_EXACT + (jnp.log(nf / MAX_EXACT) / math.log(MAX_DISTANCE / MAX_EXACT)
                         * (NUM_BUCKETS - MAX_EXACT)).astype(jnp.int32)
    large = jnp.minimum(large, NUM_BUCKETS - 1)
    return jnp.where(n < MAX_EXACT, n, large)

def gmlp_mixer(z, ws, bs):
    bn, s, _ = z.shape
    z = jax.nn.gelu(z, approximate=False)
    u, v = jnp.split(z, 2, axis=-1)
    v = v.reshape(bn, s // CHUNK, CHUNK, H_A, HD_A)
    vf = v.astype(F32)
    mu = jnp.mean(vf, axis=-1, keepdims=True)
    var = jnp.mean(jnp.square(vf - mu), axis=-1, keepdims=True)
    vn = ((vf - mu) * lax.rsqrt(var + EPS)).astype(z.dtype)
    mask = jnp.tril(jnp.ones((CHUNK, CHUNK), dtype=bool))
    w = jnp.where(mask[None], ws, jnp.zeros_like(ws))
    sg = jnp.einsum('hts,bcshd->bcthd', w, vn) + bs.T[None, None, :, :, None]
    return u * sg.reshape(bn, s, D_A)

def diff_attention(q, k, v, rel_bias, lam, subln_g, lam_init):
    bn, s, _ = q.shape
    q = q.reshape(bn, s, H_B, 2, DH_B).transpose(0, 2, 3, 1, 4)
    k = k.reshape(bn, s, H_B, 2, DH_B).transpose(0, 2, 3, 1, 4)
    v = v.reshape(bn, s, H_B, 2 * DH_B).transpose(0, 2, 1, 3)
    nb = s // Q_BLOCK
    qb = q.reshape(bn, H_B, 2, nb, Q_BLOCK, DH_B).transpose(3, 0, 1, 2, 4, 5)
    kpos = jnp.arange(s)
    scale = DH_B ** -0.5

    def block(args):
        i, qblk = args
        qpos = i * Q_BLOCK + jnp.arange(Q_BLOCK)
        dist = qpos[:, None] - kpos[None, :]
        bias = jnp.transpose(rel_bias[t5_bucket(dist)].astype(F32), (2, 0, 1))
        logits = jnp.einsum('bhmqd,bhmkd->bhmqk', qblk, k).astype(F32) * scale
        logits = logits + bias[None, :, None]
        logits = jnp.where(dist >= 0, logits, -jnp.inf)
        p = jax.nn.softmax(logits, axis=-1)
        a = p[:, :, 0] - lam * p[:, :, 1]
        return jnp.einsum('bhqk,bhkv->bhqv', a.astype(v.dtype), v)

    o = lax.map(block, (jnp.arange(nb), qb))
    o = o.transpose(1, 2, 0, 3, 4).reshape(bn, H_B, s, 2 * DH_B)
    o = rms_norm(o, subln_g) * (1.0 - lam_init)
    return o.transpose(0, 2, 1, 3).reshape(bn, s, D_B)

def pool_mixer(c, w_pool, pool_scale):
    bn, s, _ = c.shape
    cf = c.astype(F32).reshape(bn, s, G_C, GD_C)
    cs = jnp.concatenate([jnp.zeros((bn, 1, G_C, GD_C), F32), jnp.cumsum(cf, axis=1)], axis=1)
    t = jnp.arange(s)[:, None]
    win = jnp.array(POOL_WINDOWS, dtype=jnp.int32)[None, :]
    start = jnp.maximum(t + 1 - win, 0)
    count = (t + 1 - start).astype(F32)
    gidx = jnp.arange(G_C)[None, :]
    window_sum = cs[:, 1:] - cs[:, start, gidx]
    y = (window_sum / count[None, :, :, None] - cf).astype(c.dtype)
    y = jnp.einsum('bsgc,gcd->bsgd', y, w_pool).reshape(bn, s, D_C)
    return y * pool_scale

def swiglu(x, w1, w3, w2):
    return (jax.nn.silu(x @ w1) * (x @ w3)) @ w2

def moe_ffn(x, router_w, w1, w3, w2):
    bn, s, d = x.shape
    xt = x.reshape(bn * s, d)
    logits = (xt @ router_w).astype(F32)
    top_v, top_i = lax.top_k(logits, TOP_K)
    top_w = jax.nn.softmax(top_v, axis=-1)
    gates = jnp.sum(jax.nn.one_hot(top_i, N_EXPERTS, dtype=F32) * top_w[..., None], axis=1)
    y = jnp.zeros_like(xt)
    for e in range(N_EXPERTS):
        y = y + gates[:, e:e + 1].astype(x.dtype) * swiglu(xt, w1[e], w3[e], w2[e])
    return y.reshape(bn, s, d)

def first_inputs(seed: int = 0) -> dict:
    key = jax.random.key(seed)
    ks = jax.random.split(key, 24)
    nrm = lambda k, shape, sc: jax.random.normal(k, shape, F32) * sc
    return {
        "x": nrm(ks[0], (BATCH, SEQ, D_MODEL), 1.0),
        "w_in": nrm(ks[1], (DEPTH, D_MODEL, D_IN), D_MODEL ** -0.5),
        "w_out": nrm(ks[2], (DEPTH, D_MIX, D_MODEL), BETA * D_MIX ** -0.5),
        "gmlp_ws": nrm(ks[3], (DEPTH, H_A, CHUNK, CHUNK), CHUNK ** -0.5),
        "gmlp_bs": 1.0 + nrm(ks[4], (DEPTH, H_A, CHUNK), 0.02),
        "lam_q1": nrm(ks[5], (DEPTH, DH_B), 0.1),
        "lam_k1": nrm(ks[6], (DEPTH, DH_B), 0.1),
        "lam_q2": nrm(ks[7], (DEPTH, DH_B), 0.1),
        "lam_k2": nrm(ks[8], (DEPTH, DH_B), 0.1),
        "diff_subln_g": 1.0 + nrm(ks[9], (DEPTH, 2 * DH_B), 0.02),
        "rel_bias": nrm(ks[10], (NUM_BUCKETS, H_B), 0.5),
        "pool_w": nrm(ks[11], (DEPTH, G_C, GD_C, GD_C), GD_C ** -0.5),
        "pool_scale": 1.0 + nrm(ks[12], (DEPTH, D_C), 0.1),
        "ln1_g": 1.0 + nrm(ks[13], (DEPTH, D_MODEL), 0.02),
        "ln1_b": nrm(ks[14], (DEPTH, D_MODEL), 0.02),
        "ln2_g": 1.0 + nrm(ks[15], (DEPTH, D_MODEL), 0.02),
        "ln2_b": nrm(ks[16], (DEPTH, D_MODEL), 0.02),
        "ffn_w1": nrm(ks[17], (N_DENSE, D_MODEL, D_FF), D_MODEL ** -0.5),
        "ffn_w3": nrm(ks[18], (N_DENSE, D_MODEL, D_FF), D_MODEL ** -0.5),
        "ffn_w2": nrm(ks[19], (N_DENSE, D_FF, D_MODEL), BETA * D_FF ** -0.5),
        "router_w": nrm(ks[20], (N_MOE, D_MODEL, N_EXPERTS), D_MODEL ** -0.5),
        "moe_w1": nrm(ks[21], (N_MOE, N_EXPERTS, D_MODEL, D_FF_EXPERT), D_MODEL ** -0.5),
        "moe_w3": nrm(ks[22], (N_MOE, N_EXPERTS, D_MODEL, D_FF_EXPERT), D_MODEL ** -0.5),
        "moe_w2": nrm(ks[23], (N_MOE, N_EXPERTS, D_FF_EXPERT, D_MODEL), BETA * D_FF_EXPERT ** -0.5),
    }

def first_block(x, w_in, w_out, gmlp_ws, gmlp_bs, lam_q1, lam_k1, lam_q2, lam_k2,
              diff_subln_g, rel_bias, pool_w, pool_scale, ln1_g, ln1_b, ln2_g, ln2_b,
              ffn_w1, ffn_w3, ffn_w2, router_w, moe_w1, moe_w3, moe_w2):
    o_a = 2 * D_A
    o_q = o_a + D_B
    o_k = o_q + D_B
    o_v = o_k + D_B
    for l in range(DEPTH):
        p = x @ w_in[l]
        lam_init = 0.8 - 0.6 * math.exp(-0.3 * l)
        lam = (jnp.exp(jnp.sum(lam_q1[l].astype(F32) * lam_k1[l].astype(F32)))
               - jnp.exp(jnp.sum(lam_q2[l].astype(F32) * lam_k2[l].astype(F32))) + lam_init)
        y_a = gmlp_mixer(p[..., :o_a], gmlp_ws[l], gmlp_bs[l])
        y_b = diff_attention(p[..., o_a:o_q], p[..., o_q:o_k], p[..., o_k:o_v],
                             rel_bias, lam, diff_subln_g[l], lam_init)
        y_c = pool_mixer(p[..., o_v:], pool_w[l], pool_scale[l])
        h = jnp.concatenate([y_a, y_b, y_c], axis=-1) @ w_out[l]
        x = layer_norm(ALPHA * x + h, ln1_g[l], ln1_b[l])
        if l % 2 == 0:
            i = l // 2
            f = swiglu(x, ffn_w1[i], ffn_w3[i], ffn_w2[i])
        else:
            i = l // 2
            f = moe_ffn(x, router_w[i], moe_w1[i], moe_w3[i], moe_w2[i])
        x = layer_norm(ALPHA * x + f, ln2_g[l], ln2_b[l])
    return x


BRANCH_W = D_MODEL // 2
N_BRANCH = 3
NSA_HEADS = 8
NSA_GROUPS = 2
NSA_HPG = NSA_HEADS // NSA_GROUPS
NSA_DH = BRANCH_W // NSA_HEADS
NSA_KV = NSA_GROUPS * NSA_DH
CMP_BLOCK = 32
CMP_STRIDE = 16
CMP_HIDDEN = 2 * NSA_DH
SEL_BLOCK = 64
SEL_TOPK = 8
WINDOW = 512
RET_HEADS = 4
RET_DV = BRANCH_W // RET_HEADS
RET_DK = RET_DV // 2
RET_CHUNK = 128
ROPE_BASE = 10000.0
CONV_CH = BRANCH_W
CONV_WIDTH = 31
REL_BUCKETS = 32
REL_MAX_DIST = 128
D_FF_2 = 4 * D_MODEL
EPS_2 = 1e-6
IN_WIDTHS = (NSA_HEADS * NSA_DH, NSA_KV, NSA_KV, NSA_KV, NSA_KV, NSA_KV, NSA_KV, 3 * NSA_HEADS,
             RET_HEADS * RET_DK, RET_HEADS * RET_DK, RET_HEADS * RET_DV, RET_HEADS * RET_DV,
             CONV_CH, CONV_CH, N_BRANCH * D_MODEL)
IN_TOTAL = sum(IN_WIDTHS)


def _rmsnorm(x, g):
    x32 = x.astype(jnp.float32)
    y = x32 * lax.rsqrt(jnp.mean(x32 * x32, axis=-1, keepdims=True) + EPS_2)
    return (y * g.astype(jnp.float32)).astype(x.dtype)

def _layernorm(x, g, b=None):
    x32 = x.astype(jnp.float32)
    mu = jnp.mean(x32, axis=-1, keepdims=True)
    var = jnp.mean(jnp.square(x32 - mu), axis=-1, keepdims=True)
    y = (x32 - mu) * lax.rsqrt(var + EPS_2) * g.astype(jnp.float32)
    if b is not None:
        y = y + b.astype(jnp.float32)
    return y

def _split_cols(z):
    parts = []
    start = 0
    for w in IN_WIDTHS:
        parts.append(z[..., start:start + w])
        start += w
    return parts

def _rel_bucket(dist):
    n = jnp.maximum(dist, 0)
    max_exact = REL_BUCKETS // 2
    nf = jnp.maximum(n, 1).astype(jnp.float32)
    large = max_exact + (jnp.log(nf / max_exact) / math.log(REL_MAX_DIST / max_exact)
                         * (REL_BUCKETS - max_exact)).astype(jnp.int32)
    large = jnp.minimum(large, REL_BUCKETS - 1)
    return jnp.where(n < max_exact, n, large)

def _masked_softmax(s, mask):
    s = jnp.where(mask, s, -1e30)
    m = jnp.max(s, axis=-1, keepdims=True)
    p = jnp.exp(s - m) * mask
    den = jnp.sum(p, axis=-1, keepdims=True)
    return p / jnp.maximum(den, 1e-30)

def _rotary(x, pos):
    half = x.shape[-1] // 2
    inv = ROPE_BASE ** (-jnp.arange(half, dtype=jnp.float32) / half)
    ang = pos[:, None] * inv[None, :]
    cos = jnp.cos(ang)[:, None, :]
    sin = jnp.sin(ang)[:, None, :]
    x32 = x.astype(jnp.float32)
    x1, x2 = x32[..., :half], x32[..., half:]
    return jnp.concatenate([x1 * cos - x2 * sin, x1 * sin + x2 * cos], axis=-1).astype(x.dtype)

def _compress(x, pe, w1, w2):
    B, S, G, DH = x.shape
    n_ch = S // CMP_STRIDE
    r = CMP_BLOCK // CMP_STRIDE
    n_c = n_ch - r + 1
    ch = x.reshape(B, n_ch, CMP_STRIDE, G, DH)
    blocks = jnp.concatenate([ch[:, i:i + n_c] for i in range(r)], axis=2) + pe[None, None, :, None, :]
    hid = jax.nn.gelu(jnp.einsum('bnlgd,ldf->bngf', blocks, w1))
    return jnp.einsum('bngf,fd->bngd', hid, w2)

def _nsa(q, kc, vc, ks, vs, kw, vw, gl, pe_k, w1_k, w2_k, pe_v, w1_v, w2_v, rel_table):
    B, S, _ = q.shape
    G, HPG, DH = NSA_GROUPS, NSA_HPG, NSA_DH
    dt = q.dtype
    q = q.reshape(B, S, G, HPG, DH) * (DH ** -0.5)
    kc, vc, ks, vs, kw, vw = [a.reshape(B, S, G, DH) for a in (kc, vc, ks, vs, kw, vw)]
    k_cmp = _compress(kc, pe_k, w1_k, w2_k)
    v_cmp = _compress(vc, pe_v, w1_v, w2_v)
    n_c = k_cmp.shape[1]
    cmp_start = jnp.arange(n_c) * CMP_STRIDE
    cmp_end = cmp_start + (CMP_BLOCK - 1)
    n_s = S // SEL_BLOCK
    k_eff = min(SEL_TOPK, n_s)
    sel_start = jnp.arange(n_s) * SEL_BLOCK
    overlap = ((cmp_start[:, None] <= sel_start[None, :] + SEL_BLOCK - 1)
               & (cmp_end[:, None] >= sel_start[None, :])).astype(jnp.float32)
    ks_blk = ks.reshape(B, n_s, SEL_BLOCK, G, DH).transpose(0, 3, 1, 2, 4)
    vs_blk = vs.reshape(B, n_s, SEL_BLOCK, G, DH).transpose(0, 3, 1, 2, 4)
    kw_pad = jnp.pad(kw, ((0, 0), (WINDOW, 0), (0, 0), (0, 0)))
    vw_pad = jnp.pad(vw, ((0, 0), (WINDOW, 0), (0, 0), (0, 0)))
    tb = rel_table.reshape(REL_BUCKETS, G, HPG).transpose(1, 0, 2)
    b_idx = jnp.arange(B)[:, None, None, None]
    g_idx = jnp.arange(G)[None, :, None, None]
    sb_ar = jnp.arange(SEL_BLOCK)

    def head_bias(dist):
        bias = rel_table[_rel_bucket(dist)]
        return jnp.transpose(bias, (2, 0, 1)).reshape(G, HPG, dist.shape[0], dist.shape[1]).astype(jnp.float32)

    def block_fn(args):
        c, qb, gb = args
        t = c * Q_BLOCK + jnp.arange(Q_BLOCK)
        dist_c = t[:, None] - cmp_end[None, :]
        s_c = jnp.einsum('bqghd,bngd->bghqn', qb, k_cmp).astype(jnp.float32) + head_bias(dist_c)
        p_c = _masked_softmax(s_c, dist_c >= 0)
        o_c = jnp.einsum('bghqn,bngd->bqghd', p_c, v_cmp)
        imp = jnp.einsum('bghqn,ns->bgqs', p_c, overlap)
        jb = jnp.arange(n_s)[None, :]
        cur = (t // SEL_BLOCK)[:, None]
        valid = jb <= cur
        forced = (jb == 0) | (jb == cur) | (jb == cur - 1)
        score = jnp.where(forced, imp + 1e4, jnp.where(valid, imp, -1e4))
        _, idx = lax.top_k(score, k_eff)
        kg = ks_blk[b_idx, g_idx, idx]
        vg = vs_blk[b_idx, g_idx, idx]
        pos_s = idx[..., None] * SEL_BLOCK + sb_ar
        dist_s = t[None, None, :, None, None] - pos_s
        bias_s = tb[g_idx[..., None], _rel_bucket(dist_s)]
        s_s = jnp.einsum('bqghd,bgqkld->bghqkl', qb, kg).astype(jnp.float32) + jnp.moveaxis(bias_s, -1, 2).astype(jnp.float32)
        mask_s = (dist_s >= 0)[:, :, None]
        p_s = _masked_softmax(s_s.reshape(B, G, HPG, Q_BLOCK, k_eff * SEL_BLOCK),
                              mask_s.reshape(B, G, 1, Q_BLOCK, k_eff * SEL_BLOCK))
        p_s = p_s.reshape(B, G, HPG, Q_BLOCK, k_eff, SEL_BLOCK)
        o_s = jnp.einsum('bghqkl,bgqkld->bqghd', p_s, vg)
        start = c * Q_BLOCK
        kwb = lax.dynamic_slice_in_dim(kw_pad, start, WINDOW + Q_BLOCK, axis=1)
        vwb = lax.dynamic_slice_in_dim(vw_pad, start, WINDOW + Q_BLOCK, axis=1)
        pos_w = start - WINDOW + jnp.arange(WINDOW + Q_BLOCK)
        dist_w = t[:, None] - pos_w[None, :]
        mask_w = (dist_w >= 0) & (dist_w < WINDOW) & (pos_w[None, :] >= 0)
        s_w = jnp.einsum('bqghd,bkgd->bghqk', qb, kwb).astype(jnp.float32) + head_bias(dist_w)
        p_w = _masked_softmax(s_w, mask_w)
        o_w = jnp.einsum('bghqk,bkgd->bqghd', p_w, vwb)
        gs = jax.nn.sigmoid(gb.astype(jnp.float32)).reshape(B, Q_BLOCK, G, HPG, 3)
        o = gs[..., 0:1] * o_c + gs[..., 1:2] * o_s + gs[..., 2:3] * o_w
        return o.astype(dt)

    n_qb = S // Q_BLOCK
    q_blocks = q.reshape(B, n_qb, Q_BLOCK, G, HPG, DH).transpose(1, 0, 2, 3, 4, 5)
    g_blocks = gl.reshape(B, n_qb, Q_BLOCK, NSA_HEADS, 3).transpose(1, 0, 2, 3, 4)
    out = lax.map(block_fn, (jnp.arange(n_qb), q_blocks, g_blocks))
    return out.transpose(1, 0, 2, 3, 4, 5).reshape(B, S, NSA_HEADS * DH)

def _retention(q, k, v, g, gn_gain):
    B, S, _ = q.shape
    H, DK, DV, C = RET_HEADS, RET_DK, RET_DV, RET_CHUNK
    dt = q.dtype
    pos = jnp.arange(S, dtype=jnp.float32)
    q = _rotary(q.reshape(B, S, H, DK), pos)
    k = _rotary(k.reshape(B, S, H, DK), pos) * (DK ** -0.5)
    v = v.reshape(B, S, H, DV)
    log_g = jnp.log1p(-jnp.exp2(-5.0 - jnp.arange(H, dtype=jnp.float32)))
    N = S // C
    qc = q.reshape(B, N, C, H, DK)
    kc = k.reshape(B, N, C, H, DK)
    vc = v.reshape(B, N, C, H, DV)
    ar = jnp.arange(C)
    diff = ar[:, None] - ar[None, :]
    decay = jnp.where(diff >= 0, jnp.exp(log_g[:, None, None] * jnp.maximum(diff, 0).astype(jnp.float32)), 0.0)
    inner = jnp.einsum('bnchd,bnehd->bnhce', qc, kc).astype(jnp.float32) * decay
    o_inner = jnp.einsum('bnhce,bnehv->bnchv', inner, vc)
    zeta = jnp.exp(log_g[:, None] * (C - 1 - ar).astype(jnp.float32))
    xi = jnp.exp(log_g[:, None] * (ar + 1).astype(jnp.float32))
    kv = jnp.einsum('bnchd,hc,bnchv->bnhdv', kc, zeta, vc)
    g_chunk = jnp.exp(log_g * C)[None, :, None, None]

    def step(state, kv_n):
        return g_chunk * state + kv_n, state

    init = jnp.zeros((B, H, DK, DV), kv.dtype)
    _, prev = lax.scan(step, init, kv.transpose(1, 0, 2, 3, 4))
    prev = prev.transpose(1, 0, 2, 3, 4)
    o_cross = jnp.einsum('bnchd,hc,bnhdv->bnchv', qc, xi, prev)
    o = (o_inner + o_cross).reshape(B, S, H, DV)
    o = _layernorm(o, jnp.ones((DV,), jnp.float32)).reshape(B, S, H * DV) * gn_gain.astype(jnp.float32)
    return (jax.nn.silu(g.astype(jnp.float32)) * o).astype(dt)

def _conv_module(a, b, dw_w, dw_b, ln_g, ln_b):
    u = a * jax.nn.sigmoid(b)
    kern = dw_w[:, None, :].astype(u.dtype)
    y = lax.conv_general_dilated(u, kern, window_strides=(1,), padding=[(CONV_WIDTH - 1, 0)],
                                 dimension_numbers=('NWC', 'WIO', 'NWC'), feature_group_count=CONV_CH)
    y = y + dw_b
    y = _layernorm(y, ln_g, ln_b)
    return jax.nn.silu(y).astype(a.dtype)

def second_inputs(seed: int = 0) -> dict:
    key = jax.random.key(seed)
    k = jax.random.split(key, 21)
    f32 = jnp.float32

    def nrm(kk, shape, scale):
        return jax.random.normal(kk, shape, f32) * scale

    return {
        'x': nrm(k[0], (BATCH, SEQ, D_MODEL), 1.0),
        'rel_table': nrm(k[1], (REL_BUCKETS, NSA_HEADS), 0.5),
        'norm_mix': 1.0 + nrm(k[2], (DEPTH, D_MODEL), 0.05),
        'w_in': nrm(k[3], (DEPTH, D_MODEL, IN_TOTAL), D_MODEL ** -0.5),
        'cmp_pe_k': nrm(k[4], (DEPTH, CMP_BLOCK, NSA_DH), 0.5),
        'cmp_w1_k': nrm(k[5], (DEPTH, CMP_BLOCK, NSA_DH, CMP_HIDDEN), (CMP_BLOCK * NSA_DH) ** -0.5),
        'cmp_w2_k': nrm(k[6], (DEPTH, CMP_HIDDEN, NSA_DH), CMP_HIDDEN ** -0.5),
        'cmp_pe_v': nrm(k[7], (DEPTH, CMP_BLOCK, NSA_DH), 0.5),
        'cmp_w1_v': nrm(k[8], (DEPTH, CMP_BLOCK, NSA_DH, CMP_HIDDEN), (CMP_BLOCK * NSA_DH) ** -0.5),
        'cmp_w2_v': nrm(k[9], (DEPTH, CMP_HIDDEN, NSA_DH), CMP_HIDDEN ** -0.5),
        'ret_gn': 1.0 + nrm(k[10], (DEPTH, RET_HEADS * RET_DV), 0.05),
        'conv_w': nrm(k[11], (DEPTH, CONV_WIDTH, CONV_CH), CONV_WIDTH ** -0.5),
        'conv_b': nrm(k[12], (DEPTH, CONV_CH), 0.02),
        'conv_ln_g': 1.0 + nrm(k[13], (DEPTH, CONV_CH), 0.05),
        'conv_ln_b': nrm(k[14], (DEPTH, CONV_CH), 0.02),
        'w_branch': nrm(k[15], (DEPTH, N_BRANCH, BRANCH_W, D_MODEL), BRANCH_W ** -0.5),
        'w_out': nrm(k[16], (DEPTH, D_MODEL, D_MODEL), D_MODEL ** -0.5),
        'norm_mlp': 1.0 + nrm(k[17], (DEPTH, D_MODEL), 0.05),
        'w_ff1': nrm(k[18], (DEPTH, D_MODEL, D_FF_2), D_MODEL ** -0.5),
        'w_ff2': nrm(k[19], (DEPTH, D_FF_2, D_MODEL), D_FF_2 ** -0.5),
        'norm_final': 1.0 + nrm(k[20], (D_MODEL,), 0.05),
    }

def second_block(x, rel_table, norm_mix, w_in, cmp_pe_k, cmp_w1_k, cmp_w2_k, cmp_pe_v, cmp_w1_v, cmp_w2_v,
              ret_gn, conv_w, conv_b, conv_ln_g, conv_ln_b, w_branch, w_out, norm_mlp, w_ff1, w_ff2,
              norm_final):
    B, S, _ = x.shape
    for l in range(DEPTH):
        h = _rmsnorm(x, norm_mix[l])
        z = h @ w_in[l]
        (q_n, kc, vc, ks, vs, kw, vw, g_n, q_r, k_r, v_r, g_r, c_a, c_b, m_g) = _split_cols(z)
        o_nsa = _nsa(q_n, kc, vc, ks, vs, kw, vw, g_n, cmp_pe_k[l], cmp_w1_k[l], cmp_w2_k[l],
                     cmp_pe_v[l], cmp_w1_v[l], cmp_w2_v[l], rel_table)
        o_ret = _retention(q_r, k_r, v_r, g_r, ret_gn[l])
        o_conv = _conv_module(c_a, c_b, conv_w[l], conv_b[l], conv_ln_g[l], conv_ln_b[l])
        br = jnp.stack([o_nsa.astype(x.dtype), o_ret.astype(x.dtype), o_conv.astype(x.dtype)], axis=2)
        proj = jnp.einsum('bsnc,ncd->bsnd', br, w_branch[l])
        gate = jax.nn.sigmoid(m_g.astype(jnp.float32)).reshape(B, S, N_BRANCH, D_MODEL)
        merged = jnp.sum(gate * proj, axis=2).astype(x.dtype)
        x = x + merged @ w_out[l]
        h2 = _rmsnorm(x, norm_mlp[l])
        x = x + jnp.square(jax.nn.relu(h2 @ w_ff1[l])) @ w_ff2[l]
    return _rmsnorm(x, norm_final)


def setup_inputs(seed=0):
    out = dict(first_inputs(seed))
    for name, value in second_inputs(seed + 1).items():
        if name != "x":
            out[name + "_2"] = value
    return out


def reference(
    x, w_in, w_out, gmlp_ws, gmlp_bs, lam_q1, lam_k1, lam_q2, lam_k2, diff_subln_g, rel_bias,
    pool_w, pool_scale, ln1_g, ln1_b, ln2_g, ln2_b, ffn_w1, ffn_w3, ffn_w2, router_w, moe_w1,
    moe_w3, moe_w2, rel_table_2, norm_mix_2, w_in_2, cmp_pe_k_2, cmp_w1_k_2, cmp_w2_k_2,
    cmp_pe_v_2, cmp_w1_v_2, cmp_w2_v_2, ret_gn_2, conv_w_2, conv_b_2, conv_ln_g_2, conv_ln_b_2,
    w_branch_2, w_out_2, norm_mlp_2, w_ff1_2, w_ff2_2, norm_final_2,
):
    x = first_block(
        x, w_in, w_out, gmlp_ws, gmlp_bs, lam_q1, lam_k1, lam_q2, lam_k2, diff_subln_g,
        rel_bias, pool_w, pool_scale, ln1_g, ln1_b, ln2_g, ln2_b, ffn_w1, ffn_w3, ffn_w2,
        router_w, moe_w1, moe_w3, moe_w2,
    )
    return second_block(
        x, rel_table_2, norm_mix_2, w_in_2, cmp_pe_k_2, cmp_w1_k_2, cmp_w2_k_2, cmp_pe_v_2,
        cmp_w1_v_2, cmp_w2_v_2, ret_gn_2, conv_w_2, conv_b_2, conv_ln_g_2, conv_ln_b_2,
        w_branch_2, w_out_2, norm_mlp_2, w_ff1_2, w_ff2_2, norm_final_2,
    )


_drawn_inputs = setup_inputs


def setup_inputs(seed=0):
    import zlib

    import numpy as np

    out = dict(_drawn_inputs(seed))
    spreads = {}
    factors = {'gmlp_bs': 6.241,
     'diff_subln_g': 4.886,
     'cmp_pe_k_2': 3.604,
     'ret_gn_2': 2.932,
     'conv_b_2': 2.988,
     'conv_ln_b_2': 6.472}
    for name, (base, spread) in spreads.items():
        noise = np.random.default_rng([zlib.crc32(name.encode()), seed]).standard_normal(out[name].shape)
        drawn = base * np.exp(spread * noise) if base else spread * noise
        out[name] = jnp.asarray(drawn.astype(out[name].dtype))
    for name, factor in factors.items():
        out[name] = (out[name] * factor).astype(out[name].dtype)
    return out
```

```python
import math

import numpy as np

import concourse.bass as bass
from concourse import mybir
from contextlib import ExitStack

F32 = mybir.dt.float32
I32 = mybir.dt.int32
U32 = mybir.dt.uint32
ALU = mybir.AluOpType
ACT = mybir.ActivationFunctionType
AX = mybir.AxisListType

P = 128
SEQ, D = 256, 1024
TB = SEQ // P
KC = D // P
DEPTH = 2
HEADS1, DH1 = 4, 64
D_FF, N_EXP, D_FFE = 2816, 8, 3584
NSA_H, NSA_G, DH2 = 8, 2, 64
RET_H, RET_DK, RET_DV = 4, 64, 128
CONV_CH, CONV_W = 512, 31
CMP_BLOCK, CMP_STRIDE = 32, 16
N_CMP = SEQ // CMP_STRIDE - CMP_BLOCK // CMP_STRIDE + 1
D_FF2 = 4096
BUCKETS, MAX_DIST = 32, 128
WINDOWS = (2, 4, 8, 16)
ALPHA = (2 * DEPTH) ** 0.25
EPS1, EPS2 = 1e-5, 1e-6
QSCALE = DH1 ** -0.5
NEG = -1e30
UNITS = 7
REACH = SEQ + P
CAP = P
EXTRA = 2 * SEQ // (CAP + 1)
ROUNDS = N_EXP + EXTRA
assert SEQ <= 2 * CAP

TILES1 = [(0, 512), (512, 512), (1024, 512), (1536, 512), (2048, 256)]
TILES2 = [(0, 512), (512, 512), (1024, 280), (1304, 512), (1816, 512), (2328, 512), (2840, 512),
          (3352, 512)] + [(3864 + 512 * i, 512) for i in range(6)]
FF_TILES = [(c, min(512, D_FF - c)) for c in range(0, D_FF, 512)]
MOE_TILES = D_FFE // 512


def lam_init(layer):
    return 0.8 - 0.6 * math.exp(-0.3 * layer)


class Tally:

    def __init__(self):
        self.n, self.i, self.per = 0, None, 0

    def at(self, n):
        return n if self.i is None else n + self.i * self.per

    def take(self, k=1):
        self.n += k
        return self.n - k


class Signals:

    def __init__(self, sem, suffix=""):
        self.unit_loaded = [sem(f"unit_loaded{i}{suffix}") for i in range(UNITS)]
        self.unit_started = sem("unit_started" + suffix)
        self.tile_full = sem("tile_full" + suffix)
        self.tile_evac = sem("tile_evac" + suffix)
        self.aux_full = sem("aux_full" + suffix)
        self.aux_evac = sem("aux_evac" + suffix)
        self.gated = sem("gated" + suffix)
        self.picked = sem("picked" + suffix)


class Counts:

    def __init__(self):
        self.unit, self.tile, self.aux = Tally(), Tally(), Tally()
        self.gated, self.picked, self.own = Tally(), Tally(), Tally()

    def all(self):
        return [self.unit, self.tile, self.aux, self.gated, self.picked, self.own]


PARAMS1, PARAMS2, FILLS = 3 + 9 * DEPTH, 12, 5
NORM_STAGE = [1, 2, 4, 5, 6, 9, 10, 13, 14]

MOE_UNITS = MOE_TILES * 4 + D_FFE // 256
MOE_PER = (MOE_UNITS, MOE_TILES * 2 + 2, 16, MOE_TILES, 1, 0)


def rolled(eng, C, body, routed, extra):
    begun = [t.n for t in C.all()]

    def turn(e, expert):
        for t, n, per in zip(C.all(), begun, MOE_PER):
            t.n, t.i, t.per = n, e, per
        body(e, expert)
        for t, n, per in zip(C.all(), begun, MOE_PER):
            assert t.n - n in (0, per), (t.n - n, per)

    with eng.Fori(0, N_EXP) as e:
        turn(e, e)
    eng.wait_ge(routed, 2)
    with eng.Fori(N_EXP, ROUNDS) as e:
        active = eng.value_load(extra[0:1, bass.ds(e - N_EXP, 1)], min_val=0, max_val=1)
        with eng.If(active):
            turn(e, eng.value_load(extra[0:1, bass.ds(e - N_EXP + EXTRA, 1)], min_val=0, max_val=N_EXP - 1))


def wait(eng, sem, value):
    if not isinstance(value, int) or value > 0:
        eng.wait_ge(sem, value)


def build(nc, A, out):
    ctx = ExitStack()
    with ctx:
        def sb(name, shape, dt=F32, where=ctx):
            return where.enter_context(nc.sbuf_tensor(name, shape, dt))

        def sem(name):
            return ctx.enter_context(nc.semaphore(name))

        ring = [sb(f"unit{i}", [P, 2048]) for i in range(UNITS)]
        x = sb("x_sb", [P, TB, D])
        nat = sb("nat", [P, TB, D])
        act_t = sb("act_t", [P, KC, SEQ])
        acc = sb("acc", [P, TB, D])
        zbuf = sb("zbuf", [P, 8192])
        z = zbuf[:, :].rearrange("p (t b n) -> p t b n", t=8, b=TB)
        hid_t = zbuf[:, :].rearrange("p (c t) -> p c t", t=SEQ)
        gbuf = sb("gbuf", [P, 4096])
        hs = gbuf[:, 0:2048].rearrange("p (i b n) -> p i b n", i=2, b=TB)
        hu = gbuf[:, 2048:4096].rearrange("p (i b n) -> p i b n", i=2, b=TB)
        br_t = gbuf[:, 0:3072].rearrange("p (r c t) -> p r c t", r=3, c=4)
        cmp_w1 = gbuf[:, :].rearrange("p (k l f) -> p k l f", k=2, l=CMP_BLOCK // 2)
        q_buf = sb("q_buf", [P, 8 * SEQ])
        q_t = q_buf[0:64, :].rearrange("p (h t) -> p h t", h=8)
        k_t = sb("k_t", [64, 8, SEQ])
        sc = sb("sc", [P, 2, 2, SEQ])
        p_t = sb("p_t", [P, 2, 512])
        gain = sb("gain", [P, 2, D])
        bias2 = sb("bias2", [P, NSA_H, SEQ])
        bias_c = sb("bias_c", [P, TB, N_CMP, NSA_H])
        consts = sb("consts_sb", [P, 640])
        ident, triu, before, iota = (consts[:, i * P:(i + 1) * P] for i in range(4))
        rope_cos = consts[:, 512:576].rearrange("p (b d) -> p b d", b=TB)
        rope_sin = consts[:, 576:640].rearrange("p (b d) -> p b d", b=TB)
        ones = sb("ones", [P, P])
        half = sb("half", [P, 8])
        rs_in = sb("rs_in", [P, 8])
        rs_out = sb("rs_out", [P, 8])
        stats = sb("stats", [P, 8, 2, 6])
        mv = sb("mv", [P, 8, 2])
        negm = sb("negm", [P, 2, 2])
        den = sb("den", [P, 2, 2])
        coef = sb("coef", [P, 2, 4])
        small = sb("small", [P, 65])
        biasrow = acc[0:8, 0, :].rearrange("p (i n) -> p i n", i=2)
        rel1 = sb("rel1", [BUCKETS + 1, HEADS1])
        rel2 = sb("rel2", [BUCKETS + 1, NSA_H])
        extra = sb("extra", [P, 2 * EXTRA], I32)

        one = ExitStack()
        with one:
            gm_ws = sb("gm_ws", [P, DEPTH, 4, P], where=one)
            gm_bs = sb("gm_bs", [P, DEPTH, 4], where=one)
            lamv = sb("lamv", [P, 4, DEPTH, 64], where=one)
            subln = sb("subln", [P, DEPTH, P], where=one)
            pool_w = sb("pool_w_sb", [64, DEPTH, 4, 64], where=one)
            pool_s = sb("pool_s", [P, DEPTH, 256], where=one)
            bias1 = sb("bias1", [P, HEADS1, SEQ], where=one)
            gm_wt = sb("gm_wt", [P, 4, P], where=one)
            router = sb("router", [P, KC, N_EXP], where=one)
            lam = sb("lam", [P, 8], where=one)
            logits = sb("logits", [P, TB, 8], where=one)
            top = sb("top", [P, TB, 8], where=one)
            topi = sb("topi", [P, TB, 8], U32, where=one)
            topf = sb("topf", [P, TB, 8], where=one)
            pick = sb("pick", [P, TB, 3, 8], where=one)
            gates = sb("gates", [P, TB, ROUNDS + 1], where=one)
            rank = sb("rank", [P, TB, ROUNDS + 1], where=one)
            mask = sb("mask", [P, TB, N_EXP], where=one)
            excess = sb("excess", [P, 5, N_EXP], where=one)
        poolT = p_t[0:64, :, :].rearrange("p i (a t) -> p (i a) t", a=2)
        pool_a = z[:, 6:8, :, :].rearrange("p t b (g n) -> p (t b g) n", g=2)
        onehot = zbuf[0:BUCKETS + 1, 0:512]
        onehot_c = zbuf[0:BUCKETS + 1, 512:512 + TB * N_CMP * P].rearrange(
            "p (b n q) -> p b n q", b=TB, n=N_CMP)
        xg_t = act_t[:, 0:4, :].rearrange("p c (h n) -> p (c h) n", h=2)
        sel = act_t[:, 4, :].rearrange("p (b n) -> p b n", b=TB)
        sel_g = act_t[:, 5, :].rearrange("p (b n) -> p b n", b=TB)
        sel_gt = act_t[:, 6, :].rearrange("p (b n) -> p b n", b=TB)
        ye = gbuf[:, 1024:2048]
        hs_e = gbuf[:, 0:1024].rearrange("p (i n) -> p i n", i=2)
        hu_e = gbuf[:, 2048:3072].rearrange("p (i n) -> p i n", i=2)
        hide_t = zbuf[:, 0:D_FFE].rearrange("p (c n) -> p c n", n=CAP)

        two = ExitStack()
        with two:
            decay = sb("decay", [P, RET_H, 384], where=two)
            ret_gn = sb("ret_gn", [P, 512], where=two)
            conv_nat = sb("conv_nat", [CONV_W + 1, CONV_CH], where=two)
            conv_ln = sb("conv_ln", [P, 2, CONV_CH], where=two)
            cmp_w2 = sb("cmp_w2", [P, 2, 64], where=two)
            pe_nat = sb("pe_nat", [CMP_BLOCK, 2, 64], where=two)
            taps = sb("taps", [P, 4, CONV_W + 1], where=two)
            cbuf = sb("cbuf", [P, 6 * SEQ], where=two)
            hidp = sb("hidp", [P, 2, 45], where=two)
            hidc = sb("hidc", [P, 2, 2 * N_CMP], where=two)
            kcmp = sb("kcmp", [64, 2, N_CMP], where=two)
            vcmp = sb("vcmp", [N_CMP, 2, 64], where=two)
            sc_c = sb("sc_c", [P, TB, NSA_H, N_CMP], where=two)
            gates2 = sb("gates2", [P, TB, 24], where=two)
        pc_t = p_t[0:N_CMP, :, :].rearrange("p i (h q) -> p (i h) q", q=P)
        c_t = cbuf[:, :].rearrange("p (s t) -> p s t", s=6)
        PAD = CONV_W - 1
        u_t = cbuf[:, 0:4 * (PAD + SEQ)].rearrange("p (c t) -> p c t", c=4)
        y_t = z[:, 6, :, :].rearrange("p b (c t) -> p (b c) t", t=SEQ)
        o_cmp = acc[:, 0, :].rearrange("p (b n) -> p b n", b=TB)
        rot = acc[:, 1, :].rearrange("p (b h d) -> p b h d", b=TB, h=8)
        sig = [z[:, 0:2, :, :].rearrange("p t b n -> p (t b n)").rearrange("p (b n) -> p b n", b=TB),
               z[:, 2:4, :, :].rearrange("p t b n -> p (t b n)").rearrange("p (b n) -> p b n", b=TB),
               q_buf[:, :].rearrange("p (b n) -> p b n", b=TB)]

        tiles = [ctx.enter_context(nc.psum_tensor(f"tile{i}", [P, 512], F32)) for i in range(4)]
        aux = [ctx.enter_context(nc.psum_tensor(f"aux{i}", [P, 512], F32)) for i in range(4)]
        rows = nc.dram_tensor("bias_rows", (HEADS1 + NSA_H, P, REACH), F32)

        S = Signals(sem)
        S2 = Signals(sem, "_2")
        x_loaded = sem("x_loaded")
        consts_loaded = sem("consts_loaded")
        filled = sem("filled")
        params_loaded = sem("params_loaded")
        cmp_loaded = sem("cmp_loaded")
        params_used = sem("params_used")
        gain_loaded = sem("gain_loaded")
        gain_used = sem("gain_used")
        rows_ready = sem("rows_ready")
        rows_stored = sem("rows_stored")
        bias_loaded = sem("bias_loaded")
        nat_ready = sem("nat_ready")
        var_ready = sem("var_ready")
        rstd_ready = sem("rstd_ready")
        scores_ready = sem("scores_ready")
        probs_ready = sem("probs_ready")
        attn_ready = sem("attn_ready")
        vn_ready = sem("vn_ready")
        lam_dots = sem("lam_dots")
        lam_exp = sem("lam_exp")
        route_dif = sem("route_dif")
        route_exp = sem("route_exp")
        route_mask = sem("route_mask")
        merged = sem("merged")
        hidc_in = sem("hidc_in")
        hidc_ready = sem("hidc_ready")
        cmp_scores = sem("cmp_scores")
        cmp_exp = sem("cmp_exp")
        cmp_probs = sem("cmp_probs")
        rot_ready = sem("rot_ready")
        conv_in = sem("conv_in")
        conv_out = sem("conv_out")
        conv_norm = sem("conv_norm")
        conv_act = sem("conv_act")
        out_stored = sem("out_stored")
        gated2 = sem("gated2")
        vec = sem("vec")

        gains = ([("ln1_g", 0, "ln1_b"), ("ln2_g", 0, "ln2_b"), ("ln1_g", 1, "ln1_b"), ("ln2_g", 1, "ln2_b")]
                 + [(n, l, None) for l in range(DEPTH) for n in ("norm_mix_2", "norm_mlp_2")]
                 + [("norm_final_2", None, None)])
        block = ctx.enter_context(nc.Block())

        @block.sync
        def _(sp):
            C = Counts()

            def unit(sig_, dst, src):
                n = C.unit.take()
                wait(sp, sig_.unit_started, C.unit.at(n - UNITS + 2))
                sp.dma_start(dst(ring[n % UNITS]), src).then_inc(sig_.unit_loaded[n % UNITS], 16)

            def narrow(sig_, w, c0, width):
                for h in range(2):
                    unit(sig_, lambda r: r[:, 0:4 * width].rearrange("p (c n) -> p c n", c=4),
                         w[h * 512:(h + 1) * 512, c0:c0 + width].rearrange("(c p) n -> p c n", p=P))

            def wide(sig_, w, rows_):
                for r0 in range(0, rows_, 256):
                    unit(sig_, lambda r: r[:, :].rearrange("p (c n) -> p c n", c=2),
                         w[r0:r0 + 256, :].rearrange("(c p) n -> p c n", p=P))

            def expert(sig_, e):
                w1, w3, w2 = (A[n][0, bass.ds(e, 1)].rearrange("o k n -> (o k) n")
                              for n in ("moe_w1", "moe_w3", "moe_w2"))
                for t in range(MOE_TILES):
                    narrow(sig_, w1, t * 512, 512)
                    narrow(sig_, w3, t * 512, 512)
                wide(sig_, w2, D_FFE)

            sp.dma_start(x[:, :, :], A["x"][0].rearrange("(b p) d -> p b d", p=P)).then_inc(x_loaded, 16)
            sp.dma_start(consts[:, :], A["c_small"]).then_inc(consts_loaded, 16)
            sp.dma_start(zbuf[0:BUCKETS + 1, 0:512 + TB * N_CMP * P], A["c_onehot"]).then_inc(consts_loaded, 16)
            sp.dma_start(zbuf[:, 6 * 1024:8 * 1024], A["c_pool"]).then_inc(consts_loaded, 16)
            for l in range(DEPTH):
                for c0, width in TILES1:
                    narrow(S, A["w_in"][l], c0, width)
                wide(S, A["w_out"][l], D)
                if l == 0:
                    for c0, width in FF_TILES:
                        narrow(S, A["ffn_w1"][0], c0, width)
                        narrow(S, A["ffn_w3"][0], c0, width)
                    wide(S, A["ffn_w2"][0], D_FF)
                else:
                    rolled(sp, C, lambda _, e: expert(S, e), route_mask, extra)
            sp.wait_ge(params_used, 1)
            C = Counts()
            for l in range(DEPTH):
                for c0, width in TILES2:
                    narrow(S2, A["w_in_2"][l], c0, width)
                for r in range(3):
                    wide(S2, A["w_branch_2"][l, r], 512)
                wide(S2, A["w_out_2"][l], D)
                for t in range(D_FF2 // 512):
                    narrow(S2, A["w_ff1_2"][l], t * 512, 512)
                wide(S2, A["w_ff2_2"][l], D_FF2)
            sp.wait_ge(nat_ready, TB * (NORM_STAGE[-1] + 1))
            sp.dma_start(out[0].rearrange("(b p) d -> p b d", p=P), nat[:, :, :]).then_inc(out_stored, 16)
            sp.wait_ge(out_stored, 16)

        @block.tensor
        def _(pe):
            C = Counts()
            SG = [S]

            def unit():
                n = C.unit.take()
                value = 16 * (n // UNITS + 1)
                if C.unit.i is not None:
                    value = value + C.unit.i * (16 * C.unit.per // UNITS)
                pe.wait_ge(SG[0].unit_loaded[n % UNITS], value)
                return ring[n % UNITS]

            def tile_bank():
                n = C.tile.take()
                wait(pe, SG[0].tile_evac, C.tile.at(n - 3))
                return tiles[n % 4]

            def aux_bank():
                n = C.aux.take()
                wait(pe, SG[0].aux_evac, C.aux.at(n - 3))
                return aux[n % 4]

            def aux_done():
                wait(pe, SG[0].aux_evac, C.aux.at(C.aux.n))

            def narrow(width, lhs, blocks=TB):
                banks = {}
                for h in range(2):
                    w = unit()[:, 0:4 * width].rearrange("p (c n) -> p c n", c=4)
                    for b in range(blocks):
                        if h == 0:
                            banks[b] = tile_bank()
                        for c in range(4):
                            mm = nc.tensor.matmul(banks[b][:, 0:width], lhs(4 * h + c, b), w[:, c, :],
                                                  start=(h == 0 and c == 0), stop=(h == 1 and c == 3))
                            if b == 0 and c == 0:
                                mm.then_inc(SG[0].unit_started, 1)
                        if h == 1:
                            mm.then_inc(SG[0].tile_full, 1)

            def wide(units, lhs, blocks=TB, between=None):
                banks = None
                for k in range(units):
                    if between and between[0] == k:
                        between[1]()
                    w = unit()[:, :].rearrange("p (c n) -> p c n", c=2)
                    if banks is None:
                        banks = [tile_bank() for _ in range(2 * blocks)]
                    for c in range(2):
                        for b in range(blocks):
                            for h in range(2):
                                mm = nc.tensor.matmul(banks[2 * b + h][:, :], lhs(2 * k + c, b),
                                                      w[:, c, h * 512:(h + 1) * 512],
                                                      start=(k == 0 and c == 0),
                                                      stop=(k == units - 1 and c == 1))
                                if c == 0 and b == 0 and h == 0:
                                    mm.then_inc(SG[0].unit_started, 1)
                                if k == units - 1 and c == 1:
                                    mm.then_inc(SG[0].tile_full, 1)

            def turn(sources):
                bank = aux_bank()
                for i, src in enumerate(sources):
                    k, m = src.shape
                    mm = nc.tensor.transpose(bank[0:m, i * k:(i + 1) * k], src, ident[0:k, 0:k])
                mm.then_inc(SG[0].aux_full, 1)

            def turn_all(src, stage=None):
                for b in range(TB):
                    if stage is not None:
                        pe.wait_ge(nat_ready, 2 * stage + b + 1)
                    for h in range(2):
                        turn([src[:, b, (4 * h + i) * P:(4 * h + i + 1) * P] for i in range(4)])

            def lhs_act(c, b):
                return act_t[:, c, b * P:(b + 1) * P]

            def pipelined(n, scores, turned, values):
                scores(0)
                scores(1)
                for u in range(n):
                    turned(u)
                    if u + 2 < n:
                        scores(u + 2)
                    values(u)

            pe.wait_ge(consts_loaded, 48)
            pe.wait_ge(filled, FILLS)
            pe.wait_ge(params_loaded, 16 * PARAMS1)
            for rel, heads in ((rel1, HEADS1), (rel2, NSA_H)):
                nc.tensor.matmul(aux_bank()[0:heads, :], rel[:, :], onehot, start=True,
                                 stop=True).then_inc(S.aux_full, 1)
            bank = aux_bank()
            for b in range(TB):
                for n in range(N_CMP):
                    at = (b * N_CMP + n) * NSA_H
                    mm = nc.tensor.matmul(bank[:, at:at + NSA_H], onehot_c[:, b, n, :], rel2[:, :],
                                          start=True, stop=True)
            mm.then_inc(S.aux_full, 1)

            pe.wait_ge(x_loaded, 16)
            for l in range(DEPTH):
                turn_all(x, None if l == 0 else 2)
                aux_done()
                t0 = C.tile.n
                for _, width in TILES1:
                    narrow(width, lhs_act)
                turn([gm_ws[:, l, h, :] for h in range(4)])
                wait(pe, S.tile_evac, t0 + 6)
                for t in (1, 2):
                    for b in range(TB):
                        for h in range(2):
                            turn([z[:, t, b, (4 * h + i) * 64:(4 * h + i + 1) * 64] for i in range(4)])
                for b in range(TB):
                    pe.wait_ge(vn_ready, 2 * l + b + 1)
                    bank = aux_bank()
                    for h in range(4):
                        mm = nc.tensor.matmul(bank[:, h * 64:(h + 1) * 64], gm_wt[:, h, :],
                                              z[:, 0, b, 256 + h * 64:256 + (h + 1) * 64],
                                              start=True, stop=True)
                    mm.then_inc(S.aux_full, 1)
                wait(pe, S.tile_evac, t0 + 10)
                for g2 in range(2):
                    bank = aux_bank()
                    for i in range(2):
                        g = 2 * g2 + i
                        for s in range(TB):
                            mm = nc.tensor.matmul(bank[0:64, i * SEQ:(i + 1) * SEQ],
                                                  z[:, 4, s, g * 64:(g + 1) * 64], pool_a[:, s * 4 + g, :],
                                                  start=(s == 0), stop=(s == 1))
                    mm.then_inc(S.aux_full, 1)
                aux_done()
                for b in range(TB):
                    bank = aux_bank()
                    for g in range(4):
                        mm = nc.tensor.matmul(bank[:, g * 64:(g + 1) * 64], poolT[:, g, b * P:(b + 1) * P],
                                              pool_w[:, l, g, :], start=True, stop=True)
                    mm.then_inc(S.aux_full, 1)
                aux_done()
                turned_at = {}

                def scores(u):
                    h, b = divmod(u, TB)
                    nk = (b + 1) * P
                    bank = aux_bank()
                    for m in range(2):
                        mm = nc.tensor.matmul(bank[:, m * SEQ:m * SEQ + nk],
                                              q_t[:, 2 * h + m, b * P:(b + 1) * P],
                                              k_t[:, 2 * h + m, 0:nk], start=True, stop=True)
                    mm.then_inc(S.aux_full, 1)

                def turned(u):
                    pe.wait_ge(attn_ready, l * HEADS1 * TB + u + 1)
                    turn([sc[:, u % 2, 0, k * P:(k + 1) * P] for k in range(u % TB + 1)])
                    turned_at[u] = C.aux.n

                def values(u):
                    h, b = divmod(u, TB)
                    pe.wait_ge(S.aux_evac, turned_at[u])
                    bank = aux_bank()
                    for k in range(b + 1):
                        mm = nc.tensor.matmul(bank[:, 0:P], p_t[:, u % 2, k * P:(k + 1) * P],
                                              z[:, 3, k, h * P:(h + 1) * P], start=(k == 0), stop=(k == b))
                    mm.then_inc(S.aux_full, 1)

                pipelined(HEADS1 * TB, scores, turned, values)
                turn_all(nat, 3 * l)
                aux_done()
                wide(D // 256, lhs_act)
                turn_all(x, 3 * l + 1)
                aux_done()
                if l == 0:
                    def turn_hidden(t):
                        pe.wait_ge(S.gated, t + 1)
                        C.gated.n = t + 1
                        for b in range(TB):
                            turn([hs[:, t % 2, b, i * P:(i + 1) * P] for i in range(FF_TILES[t][1] // P)])

                    for t, (_, width) in enumerate(FF_TILES):
                        narrow(width, lhs_act)
                        narrow(width, lhs_act)
                        if t > 0:
                            turn_hidden(t - 1)
                    turn_hidden(len(FF_TILES) - 1)
                    aux_done()
                    wide(D_FF // 256, lambda c, b: hid_t[:, c, b * P:(b + 1) * P])
                else:
                    for b in range(TB):
                        bank = aux_bank()
                        for c in range(KC):
                            mm = nc.tensor.matmul(bank[:, 0:N_EXP], lhs_act(c, b), router[:, c, :],
                                                  start=(c == 0), stop=(c == KC - 1))
                        mm.then_inc(S.aux_full, 1)
                    pe.wait_ge(route_mask, 1)
                    bank = aux_bank()
                    for to, parts in enumerate([[(before, 0)], [(ones, 0), (before, 1)], [(ones, 0), (ones, 1)]]):
                        for i, (m, b) in enumerate(parts):
                            mm = nc.tensor.matmul(bank[:, to * 8:to * 8 + 8], m[:, :], mask[:, b, :],
                                                  start=(i == 0), stop=(i == len(parts) - 1))
                    mm.then_inc(S.aux_full, 1)

                    def gather():
                        n = C.picked.take()
                        pe.wait_ge(SG[0].picked, C.picked.at(n) + 1)
                        for j in range(4):
                            bank = aux_bank()
                            for i in range(2):
                                for b in range(TB):
                                    mm = nc.tensor.matmul(bank[:, i * P:(i + 1) * P],
                                                          x[:, b, (2 * j + i) * P:(2 * j + i + 1) * P],
                                                          sel[:, b, :], start=(b == 0), stop=(b == TB - 1))
                            mm.then_inc(SG[0].aux_full, 1)

                    def turn_gates():
                        turn([sel_g[:, b, :] for b in range(TB)])

                    def expert(*_):
                        def turn_hidden(t):
                            n = C.gated.take()
                            pe.wait_ge(SG[0].gated, C.gated.at(n) + 1)
                            turn([hs_e[:, t % 2, i * P:(i + 1) * P] for i in range(4)])

                        wait(pe, SG[0].aux_evac, C.aux.at(C.aux.n))
                        for t in range(MOE_TILES):
                            narrow(512, lambda c, b: xg_t[:, c, :], 1)
                            narrow(512, lambda c, b: xg_t[:, c, :], 1)
                            if t > 0:
                                turn_hidden(t - 1)
                        aux_done()

                        def last():
                            turn_hidden(MOE_TILES - 1)
                            aux_done()

                        wide(D_FFE // 256, lambda c, b: hide_t[:, c, :], 1, (D_FFE // 256 - 2, last))
                        out_tile = C.tile.n
                        gather()
                        wait(pe, SG[0].tile_evac, C.tile.at(out_tile))
                        for b in range(TB):
                            for h in range(2):
                                nc.tensor.matmul(aux_bank()[:, :], sel_gt[:, b, :], ye[:, h * 512:(h + 1) * 512],
                                                 start=True, stop=True).then_inc(SG[0].aux_full, 1)
                        turn_gates()

                    gather()
                    turn_gates()
                    rolled(pe, C, expert, route_mask, extra)

            C, SG[0] = Counts(), S2
            for l in range(DEPTH):
                turn_all(nat, 6 + 4 * l)
                aux_done()
                t0 = C.tile.n
                for _, width in TILES2[0:8]:
                    narrow(width, lhs_act)
                pe.wait_ge(S2.tile_evac, t0 + 16)
                pe.wait_ge(params_loaded, 16 * (PARAMS1 + PARAMS2 * (l + 1)))
                turn([conv_nat[:, c * P:(c + 1) * P] for c in range(4)])
                turn([pe_nat[:, k, :] for k in range(2)])
                for b in range(TB):
                    turn([z[:, 1, b, i * 64:(i + 1) * 64] for i in range(4)])
                    turn([z[:, 1, b, 256 + i * 64:256 + (i + 1) * 64] for i in range(2)]
                         + [z[:, 2, b, i * 64:(i + 1) * 64] for i in range(2)])
                    for h in range(2):
                        turn([z[:, 0, b, (4 * h + i) * 64:(4 * h + i + 1) * 64] for i in range(4)])
                aux_done()
                for k in range(2):
                    bank = aux_bank()
                    for i in range(CMP_BLOCK // 2):
                        last_col = 2 * i + CMP_STRIDE * (N_CMP - 1) + 1
                        mm = nc.tensor.matmul(bank[:, 0:3 * N_CMP], cmp_w1[:, k, i, :],
                                              c_t[:, 3 * k:3 * k + 3, 2 * i:last_col:CMP_STRIDE],
                                              start=(i == 0), stop=(i == CMP_BLOCK // 2 - 1))
                    mm.then_inc(S2.aux_full, 1)
                pe.wait_ge(hidc_ready, 2 * l + 2)
                nc.tensor.matmul(aux_bank()[0:64, 0:2 * N_CMP], cmp_w2[:, 0, :], hidc[:, 0, :], start=True,
                                 stop=True).then_inc(S2.aux_full, 1)
                bank = aux_bank()
                for g in range(NSA_G):
                    mm = nc.tensor.matmul(bank[0:N_CMP, g * 64:(g + 1) * 64],
                                          hidc[:, 1, g * N_CMP:(g + 1) * N_CMP], cmp_w2[:, 1, :],
                                          start=True, stop=True)
                mm.then_inc(S2.aux_full, 1)
                aux_done()
                bank = aux_bank()
                for b in range(TB):
                    for h in range(NSA_H):
                        at = (b * NSA_H + h) * N_CMP
                        mm = nc.tensor.matmul(bank[:, at:at + N_CMP], q_t[:, h, b * P:(b + 1) * P],
                                              kcmp[:, h // 4, :], start=True, stop=True)
                mm.then_inc(S2.aux_full, 1)
                pe.wait_ge(cmp_probs, l + 1)
                for b in range(TB):
                    for h2 in range(2):
                        turn([sc_c[:, b, 4 * h2 + i, :] for i in range(4)])
                    aux_done()
                    bank = aux_bank()
                    for h in range(NSA_H):
                        mm = nc.tensor.matmul(bank[:, h * 64:(h + 1) * 64], pc_t[:, h, :], vcmp[:, h // 4, :],
                                              start=True, stop=True)
                    mm.then_inc(S2.aux_full, 1)

                turned_at = {}

                def scores(u):
                    h, b = divmod(u, TB)
                    nk = (b + 1) * P
                    g = h // 4
                    nc.tensor.matmul(aux_bank()[:, 0:2 * nk].rearrange("p (r k) -> p r k", r=2),
                                     q_t[:, h, b * P:(b + 1) * P], k_t[:, g:g + 3:2, 0:nk],
                                     start=True, stop=True).then_inc(S2.aux_full, 1)

                def turned(u):
                    pe.wait_ge(probs_ready, (DEPTH * HEADS1 + l * NSA_H) * TB + u + 1)
                    turn([sc[:, u % 2, r, k * P:(k + 1) * P] for r in range(2) for k in range(u % TB + 1)])
                    turned_at[u] = C.aux.n

                def values(u):
                    h, b = divmod(u, TB)
                    g = h // 4
                    pe.wait_ge(S2.aux_evac, turned_at[u])
                    bank = aux_bank()
                    for r in range(2):
                        for k in range(b + 1):
                            v = (z[:, 1, k, 384 + g * 64:384 + (g + 1) * 64] if r == 0 else
                                 z[:, 2, k, 128 + g * 64:128 + (g + 1) * 64])
                            at = (r * (b + 1) + k) * P
                            mm = nc.tensor.matmul(bank[:, r * 64:(r + 1) * 64], p_t[:, u % 2, at:at + P], v,
                                                  start=(k == 0), stop=(k == b))
                    mm.then_inc(S2.aux_full, 1)

                pipelined(NSA_H * TB, scores, turned, values)

                pe.wait_ge(rot_ready, l + 1)
                for b in range(TB):
                    for h in range(2):
                        turn([rot[:, b, 4 * h + i, :] for i in range(4)])
                aux_done()
                decayed = {}

                def ret_scores(h):
                    bank = aux_bank()
                    nc.tensor.matmul(bank[:, 0:SEQ], q_t[:, 4 + h, 0:P], q_t[:, h, 0:SEQ], start=True, stop=True)
                    nc.tensor.matmul(bank[:, SEQ:SEQ + P], q_t[:, 4 + h, P:SEQ], q_t[:, h, P:SEQ],
                                     start=True, stop=True).then_inc(S2.aux_full, 1)
                    decayed[h] = C.aux.n

                def ret_values(h):
                    pe.wait_ge(S2.aux_evac, decayed[h])
                    bank = aux_bank()
                    for b, at, k in ((0, 0, 0), (1, P, 0), (1, 2 * P, 1)):
                        mm = nc.tensor.matmul(bank[:, b * P:(b + 1) * P], p_t[:, h % 2, at:at + P],
                                              z[:, 4, k, h * P:(h + 1) * P], start=(k == 0), stop=(k == b))
                    mm.then_inc(S2.aux_full, 1)

                ret_scores(0)
                for h in range(RET_H):
                    if h + 1 < RET_H:
                        ret_scores(h + 1)
                    ret_values(h)
                for b in range(TB):
                    pe.wait_ge(conv_in, 2 * l + b + 1)
                    turn([z[:, 6, b, c * P:(c + 1) * P] for c in range(4)])
                for t in range(8, 14):
                    narrow(512, lhs_act)
                    if t == 8:
                        turn_all(nat, 6 + 4 * l + 1)
                    if t == 12:
                        for b in range(TB):
                            pe.wait_ge(conv_out, l + 1)
                            turn([y_t[:, c, b * P:(b + 1) * P] for c in range(4)])
                for b in range(TB):
                    pe.wait_ge(conv_act, 2 * l + b + 1)
                    turn([nat[:, b, 512 + c * P:512 + (c + 1) * P] for c in range(4)])
                aux_done()
                for r in range(3):
                    wide(2, lambda c, b: br_t[:, r, c, b * P:(b + 1) * P])
                turn_all(nat, 6 + 4 * l + 2)
                aux_done()
                wide(D // 256, lhs_act)
                turn_all(nat, 6 + 4 * l + 3)
                aux_done()

                def turn_hidden2(t):
                    pe.wait_ge(gated2, l * (D_FF2 // 512) + t + 1)
                    for b in range(TB):
                        turn([hs[:, t % 2, b, i * P:(i + 1) * P] for i in range(4)])

                for t in range(D_FF2 // 512):
                    narrow(512, lhs_act)
                    if t > 0:
                        turn_hidden2(t - 1)
                turn_hidden2(D_FF2 // 512 - 1)
                aux_done()
                wide(D_FF2 // 256, lambda c, b: hid_t[:, c, b * P:(b + 1) * P])

        @block.scalar
        def _(act):
            C = Counts()
            SG = [S]

            def evac(dst, func=ACT.Copy, width=512, scale=1.0, also=None):
                n = C.tile.take()
                act.wait_ge(SG[0].tile_full, C.tile.at(n) + 1)
                if also:
                    also(tiles[n % 4])
                nc.scalar.activation(dst, tiles[n % 4][:, 0:width], func, scale=scale).then_inc(SG[0].tile_evac, 1)

            def evac_wide(before_block=None):
                for b in range(TB):
                    if before_block:
                        before_block(b)
                    for h in range(2):
                        evac(acc[:, b, h * 512:(h + 1) * 512])

            def exps(count, base, width):
                for u in range(count):
                    nk = width(u)
                    act.wait_ge(scores_ready, base + u + 1)
                    for m in range(2):
                        e = nc.scalar.activation(sc[:, u % 2, m, 0:nk], sc[:, u % 2, m, 0:nk], ACT.Exp,
                                                 bias=negm[:, u % 2, m:m + 1],
                                                 accum_out=den[:, u % 2, m:m + 1])
                    e.then_inc(probs_ready, 1)

            act.wait_ge(lam_dots, 1)
            nc.scalar.activation(lam[:, 0:4], lam[:, 4:8], ACT.Exp).then_inc(lam_exp, 1)
            for l in range(DEPTH):
                for t, (_, width) in enumerate(TILES1):
                    for b in range(TB):
                        evac(z[:, t, b, 0:width], ACT.Gelu if t == 0 else ACT.Copy, width,
                             QSCALE if t == 1 else 1.0)
                exps(HEADS1 * TB, l * HEADS1 * TB, lambda u: (u % TB + 1) * P)
                evac_wide()
                if l == 0:
                    for t, (_, width) in enumerate(FF_TILES):
                        for b in range(TB):
                            evac(hs[:, t % 2, b, 0:width], ACT.Silu, width)
                        for b in range(TB):
                            evac(hu[:, t % 2, b, 0:width], ACT.Copy, width)
                    evac_wide()
                else:
                    act.wait_ge(route_dif, 1)
                    nc.scalar.activation(small[:, 8:10], small[:, 0:2], ACT.Exp).then_inc(route_exp, 1)

                    def expert(*_):
                        for t in range(MOE_TILES):
                            evac(hs_e[:, t % 2, :], ACT.Silu)
                            evac(hu_e[:, t % 2, :])
                        for h in range(2):
                            evac(ye[:, h * 512:(h + 1) * 512])

                    rolled(act, C, expert, route_mask, extra)
            C, SG[0] = Counts(), S2
            for l in range(DEPTH):
                for t in range(8):
                    for b in range(TB):
                        if t == 2:
                            evac(z[:, t, b, 0:256], ACT.Copy, 256, also=lambda bank: nc.scalar.activation(
                                gates2[:, b, :], bank[:, 256:280], ACT.Sigmoid))
                        else:
                            evac(z[:, t, b, :], {5: ACT.Silu, 7: ACT.Sigmoid}.get(t, ACT.Copy),
                                 scale=QSCALE if t == 0 else 1.0)
                for k in range(2):
                    act.wait_ge(hidc_in, 2 * l + k + 1)
                    nc.scalar.activation(hidc[:, k, :], hidp[:, k, 0:2 * N_CMP], ACT.Gelu_apprx_tanh,
                                         bias=hidp[:, k, 2 * N_CMP:2 * N_CMP + 1]).then_inc(hidc_ready, 1)
                act.wait_ge(cmp_scores, l + 1)
                nc.scalar.activation(sc_c[:, :, :, :], sc_c[:, :, :, :], ACT.Exp).then_inc(cmp_exp, 1)
                exps(NSA_H * TB, (DEPTH * HEADS1 + l * NSA_H) * TB, lambda u: (u % TB + 1) * P)
                for t in range(8, 14):
                    r, h = divmod(t - 8, 2)
                    for b in range(TB):
                        evac(sig[r][:, b, h * 512:(h + 1) * 512], ACT.Sigmoid)
                for b in range(TB):
                    act.wait_ge(conv_norm, 2 * l + b + 1)
                    nc.scalar.activation(nat[:, b, 512:1024], nat[:, b, 0:512], ACT.Silu).then_inc(conv_act, 1)
                for r in range(3):
                    evac_wide(lambda b: wait(act, merged, (2 * l + r - 1) * TB + b + 1 if r else 0))
                evac_wide(lambda b: act.wait_ge(nat_ready, 2 * (6 + 4 * l + 2) + b + 1))
                for t in range(D_FF2 // 512):
                    for b in range(TB):
                        evac(hs[:, t % 2, b, :], ACT.Relu)
                evac_wide()

        @block.gpsimd
        def _(pool):
            pows = Tally()
            loads = Tally()

            nc.gpsimd.memset(ones[:, :], 1.0).then_inc(filled, 1)
            nc.gpsimd.memset(half[:, :], -0.5).then_inc(filled, 1)
            nc.gpsimd.memset(rs_in[:, :], 1.0).then_inc(filled, 1)

            def load(dst, src, scattered=False):
                pool.dma_start(dst, src, allow_slow_non_contiguous=scattered).then_inc(params_loaded, 16)

            def row(src, width):
                return src.rearrange("(o n) -> o n", o=1).to_broadcast([P, width])

            def load_params2(l):
                pool.wait_ge(params_used, l + 1)
                load(decay[:, :, :], A["c_decay"].rearrange("p (h t) -> p h t", h=RET_H))
                load(ret_gn[:, :], row(A["ret_gn_2"][l], 512))
                load(conv_nat[0:CONV_W, :], A["conv_w_2"][l])
                load(conv_nat[CONV_W:CONV_W + 1, :], A["conv_b_2"][l:l + 1, :])
                load(conv_ln[:, 0, :], row(A["conv_ln_g_2"][l], CONV_CH))
                load(conv_ln[:, 1, :], row(A["conv_ln_b_2"][l], CONV_CH))
                for k, kind in enumerate("kv"):
                    load(cmp_w1[:, k, :, :], A[f"cmp_w1_{kind}_2"][l].rearrange("(i a) d f -> (a d) i f", a=2))
                    load(cmp_w2[:, k, :], A[f"cmp_w2_{kind}_2"][l])
                    load(pe_nat[:, k, :], A[f"cmp_pe_{kind}_2"][l])

            def load_gain(norm):
                g, l, b = gains[norm]
                if norm > 0:
                    pool.wait_ge(nat_ready, 2 * NORM_STAGE[norm - 1] + TB)
                pool.dma_start(gain[:, 0, :], row(A[g] if l is None else A[g][l], D)).then_inc(gain_loaded, 16)
                if b is not None:
                    pool.dma_start(gain[:, 1, :], row(A[b][l], D)).then_inc(gain_loaded, 16)

            def power():
                n = pows.take()
                pool.wait_ge(var_ready, n + 1)
                if n == 0:
                    pool.wait_ge(filled, FILLS)
                nc.gpsimd.tensor_tensor(rs_out[:, :], rs_in[:, :], half[:, :], ALU.pow).then_inc(rstd_ready, 1)

            load(rel1[0:BUCKETS, :], A["rel_bias"])
            load(rel2[0:BUCKETS, :], A["rel_table_2"])
            for l in range(DEPTH):
                load(gm_ws[:, l, :, :], A["gmlp_ws"][l].rearrange("h t s -> t h s"))
                load(gm_bs[:, l, :], A["gmlp_bs"][l].rearrange("h t -> t h"), scattered=True)
                load(subln[:, l, :], row(A["diff_subln_g"][l], P))
                load(pool_w[:, l, :, :], A["pool_w"][l].rearrange("g c d -> c g d"))
                load(pool_s[:, l, :], row(A["pool_scale"][l], 256))
                for i, name in enumerate(("lam_q1", "lam_k1", "lam_q2", "lam_k2")):
                    load(lamv[:, i, l, :], row(A[name][l], 64))
            load(router[:, :, :], A["router_w"][0].rearrange("(c p) e -> p c e", p=P))
            load_gain(0)
            pool.wait_ge(rows_ready, 1)
            stacks = ((bias1, 0, HEADS1), (bias2, HEADS1, NSA_H))
            for i, (_, first, heads) in enumerate(stacks):
                pool.dma_start(rows.ap()[first:first + heads],
                               biasrow[0:heads, i, 0:REACH].unsqueeze(1).broadcast_to([heads, P, REACH])
                               ).then_inc(rows_stored, 16)
            pool.wait_ge(rows_stored, 32)
            for dst, first, heads in stacks:
                src = bass.AP(rows, first * P * REACH + P - 1, [[REACH - 1, P], [P * REACH, heads], [1, SEQ]])
                pool.dma_start(dst[:, :, :], src).then_inc(bias_loaded, 16)
            norm = 0
            for l in range(DEPTH):
                for _ in range(3):
                    power()
                for _ in range(2):
                    if l == 1 and norm == 3:
                        load_params2(0)
                    power()
                    norm += 1
                    load_gain(norm)
            for l in range(DEPTH):
                if l > 0:
                    load_params2(l)
                power()
                norm += 1
                load_gain(norm)
                for _ in range(4):
                    power()
                norm += 1
                load_gain(norm)
            power()

        @block.vector
        def _(dve):
            C = Counts()
            SG = [S]
            own = Tally()
            asked = Tally()
            V = nc.vector

            def step(ins):
                own.n += 1
                ins.then_inc(vec, 1)
                dve.wait_ge(vec, own.n)

            def aux_in():
                n = C.aux.take()
                dve.wait_ge(SG[0].aux_full, C.aux.at(n) + 1)
                return aux[n % 4]

            def evac(ins):
                ins.then_inc(SG[0].aux_evac, 1)

            def read_back():
                dve.wait_ge(SG[0].aux_evac, C.aux.at(C.aux.n))

            def turn_in(dst):
                p, n, m = dst.shape
                bank = aux_in()
                evac(V.tensor_copy(dst, bank[0:p, 0:n * m].rearrange("p (n m) -> p n m", n=n)))

            def turn_all_in():
                for b in range(TB):
                    for h in range(2):
                        turn_in(act_t[:, 4 * h:4 * h + 4, b * P:(b + 1) * P])

            def rstd(groups, value, scale, eps):
                n = asked.take()
                V.tensor_scalar(rs_in[:, 0:groups], value, scale, eps, ALU.mult, ALU.add).then_inc(var_ready, 1)
                dve.wait_ge(rstd_ready, n + 1)

            def moments(src, eps):
                _, groups, width = src.shape
                parts = max(1, width // 512)
                for g in range(groups):
                    for i in range(parts):
                        ins = V.bn_stats(stats[:, g, i, :], src[:, g, i * 512:min(width, (i + 1) * 512)])
                step(ins)
                for g in range(groups):
                    ins = V.bn_aggr(mv[:, g, :], stats[:, g, 0:parts, :].rearrange("p i s -> p (i s)"))
                step(ins)
                rstd(groups, mv[:, 0:groups, 1], 1.0, eps)

            def spread(v, width):
                return v.unsqueeze(2).broadcast_to([P, v.shape[1], width])

            def over(v, n):
                return v.unsqueeze(1).broadcast_to([P, n, v.shape[1]])

            def standardise(dst, src, eps, signal=None):
                _, groups, width = src.shape
                moments(src, eps)
                step(V.tensor_tensor(dst, src, spread(mv[:, 0:groups, 0], width), ALU.subtract))
                ins = V.tensor_tensor(dst, dst, spread(rs_out[:, 0:groups], width), ALU.mult)
                if signal is None:
                    step(ins)
                else:
                    ins.then_inc(signal, 1)

            def gain_in(norm):
                dve.wait_ge(gain_loaded, 16 * sum(1 if g[2] is None else 2 for g in gains[0:norm + 1]))

            def add_products(factor):
                for b in range(TB):
                    C.tile.n += 2
                    dve.wait_ge(SG[0].tile_evac, C.tile.n)
                    step(V.scalar_tensor_tensor(x[:, b, :], x[:, b, :], factor, acc[:, b, :], ALU.mult, ALU.add))

            def layer_norm(norm):
                moments(x[:, :, :], EPS1)
                gain_in(norm)
                for b in range(TB):
                    step(V.tensor_scalar(x[:, b, :], x[:, b, :], mv[:, b, 0:1], rs_out[:, b:b + 1],
                                         ALU.subtract, ALU.mult))
                    step(V.tensor_tensor(x[:, b, :], x[:, b, :], gain[:, 0, :], ALU.mult))
                    V.tensor_tensor(x[:, b, :], x[:, b, :], gain[:, 1, :], ALU.add).then_inc(nat_ready, 1)

            def rms_norm(norm):
                for b in range(TB):
                    ins = V.tensor_tensor_reduce(out=nat[:, b, :], in0=x[:, b, :], in1=x[:, b, :], scale=1.0,
                                                 scalar=0.0, op0=ALU.mult, op1=ALU.add,
                                                 accum_out=mv[:, b, 1:2])
                step(ins)
                rstd(TB, mv[:, 0:TB, 1], 1.0 / D, EPS2)
                gain_in(norm)
                for b in range(TB):
                    V.scalar_tensor_tensor(nat[:, b, :], x[:, b, :], rs_out[:, b:b + 1], gain[:, 0, :],
                                           ALU.mult, ALU.mult).then_inc(nat_ready, 1)

            def score_rows(bank, s, bias, nk, at):
                for m in range(2):
                    ins = V.tensor_tensor_reduce(out=sc[:, s, m, 0:nk], in0=bank[:, at(m):at(m) + nk],
                                                 in1=bias[:, SEQ - nk:SEQ], scale=1.0, scalar=-3e38,
                                                 op0=ALU.add, op1=ALU.max,
                                                 accum_out=small[:, 2 * s + m:2 * s + m + 1])
                evac(ins)
                read_back()
                V.tensor_scalar(negm[:, s, :], small[:, 2 * s:2 * s + 2], -1.0, None, ALU.mult).then_inc(scores_ready, 1)

            def pipelined(n, scores, turned, values):
                scores(0)
                scores(1)
                for u in range(n):
                    turned(u)
                    if u + 2 < n:
                        scores(u + 2)
                    values(u)

            V.memset(rel1[BUCKETS:BUCKETS + 1, :], 1.0).then_inc(filled, 1)
            V.memset(rel2[BUCKETS:BUCKETS + 1, :], 1.0).then_inc(filled, 1)
            for i, heads in enumerate((HEADS1, NSA_H)):
                V.tensor_copy(biasrow[0:heads, i, :], aux_in()[0:heads, :]).then_inc(S.aux_evac, 1)
            read_back()
            V.memset(small[:, 64:65], 0.0).then_inc(rows_ready, 1)
            bank = aux_in()
            evac(V.tensor_copy(bias_c[:, :, :, :].rearrange("p b n h -> p (b n h)"), bank[:, 0:TB * N_CMP * NSA_H]))
            dve.wait_ge(params_loaded, 16 * PARAMS1)
            for l in range(DEPTH):
                for i in range(2):
                    ins = V.tensor_tensor_reduce(out=small[:, 0:64], in0=lamv[:, 2 * i, l, :],
                                                 in1=lamv[:, 2 * i + 1, l, :], scale=1.0, scalar=0.0,
                                                 op0=ALU.mult, op1=ALU.add,
                                                 accum_out=lam[:, 4 + 2 * l + i:5 + 2 * l + i])
                    if l == DEPTH - 1 and i == 1:
                        ins.then_inc(lam_dots, 1)
                    else:
                        step(ins)
            dve.wait_ge(lam_exp, 1)
            for l in range(DEPTH):
                step(V.tensor_tensor(lam[:, 2 * l:2 * l + 1], lam[:, 2 * l + 1:2 * l + 2], lam[:, 2 * l:2 * l + 1],
                                     ALU.subtract))
                step(V.tensor_scalar(lam[:, 2 * l:2 * l + 1], lam[:, 2 * l:2 * l + 1], -lam_init(l), None, ALU.add))

            for l in range(DEPTH):
                turn_all_in()
                t0 = C.tile.n
                C.tile.n += 2 * len(TILES1)
                dve.wait_ge(consts_loaded, 48)
                dve.wait_ge(S.tile_evac, t0 + 2)
                values_ = z[:, 0, :, 256:512]
                for b in range(TB):
                    v = values_[:, b, :].rearrange("p (h d) -> p h d", h=4)
                    standardise(v, v, EPS1, vn_ready)
                bank = aux_in()
                evac(V.tensor_tensor(gm_wt[:, :, :], bank[:, :].rearrange("p (h t) -> p h t", h=4), over(triu, 4),
                                     ALU.mult))
                for dst in (q_t, k_t):
                    for b in range(TB):
                        for h in range(2):
                            turn_in(dst[:, 4 * h:4 * h + 4, b * P:(b + 1) * P])
                for b in range(TB):
                    bank = aux_in()
                    for h in range(4):
                        ins = V.scalar_tensor_tensor(nat[:, b, h * 64:(h + 1) * 64], bank[:, h * 64:(h + 1) * 64],
                                                     gm_bs[:, l, h:h + 1], z[:, 0, b, h * 64:(h + 1) * 64],
                                                     ALU.add, ALU.mult)
                    evac(ins)
                for g2 in range(2):
                    bank = aux_in()
                    evac(V.tensor_copy(poolT[:, 2 * g2:2 * g2 + 2, :],
                                       bank[0:64, :].rearrange("p (i t) -> p i t", i=2)))
                for b in range(TB):
                    bank = aux_in()
                    evac(V.tensor_tensor(nat[:, b, 768:1024], bank[:, 0:256], pool_s[:, l, :], ALU.mult))
                dve.wait_ge(bias_loaded, 32)

                def scores(u):
                    score_rows(aux_in(), u % 2, bias1[:, u // TB, :], (u % TB + 1) * P, lambda m: m * SEQ)

                def turned(u):
                    s, nk = u % 2, (u % TB + 1) * P
                    dve.wait_ge(probs_ready, l * HEADS1 * TB + u + 1)
                    step(V.reciprocal(coef[:, s, 0:2], den[:, s, :]))
                    step(V.tensor_tensor(coef[:, s, 2:3], coef[:, s, 1:2], lam[:, 2 * l:2 * l + 1], ALU.mult))
                    step(V.tensor_scalar(sc[:, s, 0, 0:nk], sc[:, s, 0, 0:nk], coef[:, s, 0:1], None, ALU.mult))
                    V.scalar_tensor_tensor(sc[:, s, 0, 0:nk], sc[:, s, 1, 0:nk], coef[:, s, 2:3],
                                           sc[:, s, 0, 0:nk], ALU.mult, ALU.add).then_inc(attn_ready, 1)
                    turn_in(p_t[:, s, 0:nk].rearrange("p (k q) -> p k q", q=P))

                def values(u):
                    h, b = divmod(u, TB)
                    evac(V.tensor_copy(nat[:, b, 256 + h * P:256 + (h + 1) * P], aux_in()[:, 0:P]))

                pipelined(HEADS1 * TB, scores, turned, values)
                read_back()
                for b in range(TB):
                    o = nat[:, b, 256:768].rearrange("p (h d) -> p h d", h=HEADS1)
                    for h in range(HEADS1):
                        ins = V.tensor_tensor_reduce(out=sc[:, 0, 0, 0:P], in0=o[:, h, :], in1=o[:, h, :],
                                                     scale=1.0, scalar=0.0, op0=ALU.mult, op1=ALU.add,
                                                     accum_out=mv[:, b * HEADS1 + h, 1:2])
                        step(ins)
                rstd(TB * HEADS1, mv[:, 0:TB * HEADS1, 1], 1.0 / P, EPS1)
                for b in range(TB):
                    for h in range(HEADS1):
                        g = b * HEADS1 + h
                        o = nat[:, b, 256 + h * P:256 + (h + 1) * P]
                        ins = V.scalar_tensor_tensor(o, o, rs_out[:, g:g + 1], subln[:, l, :], ALU.mult, ALU.mult)
                    step(ins)
                    o = nat[:, b, 256:768]
                    V.tensor_scalar(o, o, 1.0 - lam_init(l), None, ALU.mult).then_inc(nat_ready, 1)
                turn_all_in()
                add_products(ALPHA)
                layer_norm(2 * l)
                turn_all_in()
                if l == 0:
                    def hidden_in(t):
                        for b in range(TB):
                            turn_in(hid_t[:, 4 * t:4 * t + FF_TILES[t][1] // P, b * P:(b + 1) * P])

                    for t, (_, width) in enumerate(FF_TILES):
                        C.tile.n += 4
                        dve.wait_ge(S.tile_evac, C.tile.n)
                        g = hs[:, t % 2, :, 0:width]
                        V.tensor_tensor(g, g, hu[:, t % 2, :, 0:width], ALU.mult).then_inc(S.gated, 1)
                        C.gated.n += 1
                        if t > 0:
                            hidden_in(t - 1)
                    hidden_in(len(FF_TILES) - 1)
                    add_products(ALPHA)
                    layer_norm(1)
            for b in range(TB):
                evac(V.tensor_copy(logits[:, b, :], aux_in()[:, 0:N_EXP]))
            read_back()
            for b in range(TB):
                ins = V.max(top[:, b, :], logits[:, b, :])
            step(ins)
            for b in range(TB):
                ins = V.max_index(topi[:, b, :], top[:, b, :], logits[:, b, :])
            step(ins)
            step(V.tensor_copy(topf[:, :, :], topi[:, :, :]))
            V.tensor_tensor(small[:, 0:2], top[:, :, 1], top[:, :, 0], ALU.subtract).then_inc(route_dif, 1)
            dve.wait_ge(route_exp, 1)
            step(V.tensor_scalar(small[:, 10:12], small[:, 8:10], 1.0, None, ALU.add))
            step(V.reciprocal(small[:, 12:14], small[:, 10:12]))
            step(V.tensor_tensor(small[:, 14:16], small[:, 8:10], small[:, 12:14], ALU.mult))
            step(V.memset(gates[:, :, :], 0.0))
            step(V.memset(rank[:, :, :], -1000.0))
            for b in range(TB):
                for i in range(2):
                    V.tensor_scalar(pick[:, b, i, :], iota[:, 0:8], topf[:, b, i:i + 1],
                                    small[:, 12 + 2 * i + b:13 + 2 * i + b], ALU.is_equal, ALU.mult)
                    step(V.tensor_scalar(pick[:, b, 2, :] if i else mask[:, b, :], iota[:, 0:8],
                                         topf[:, b, i:i + 1], None, ALU.is_equal))
                step(V.tensor_tensor(gates[:, b, 0:8], pick[:, b, 0, :], pick[:, b, 1, :], ALU.add))
                ins = V.tensor_tensor(mask[:, b, :], mask[:, b, :], pick[:, b, 2, :], ALU.add)
                if b == TB - 1:
                    ins.then_inc(route_mask, 1)
                    dve.wait_ge(route_mask, 1)
                else:
                    step(ins)
            bank = aux_in()
            for b in range(TB):
                ins = V.scalar_tensor_tensor(rank[:, b, 0:8], bank[:, b * 8:b * 8 + 8], 1000.0, mask[:, b, :],
                                             ALU.add, ALU.mult)
            step(ins)
            over_cap, place, mine, junk, seen = (excess[:, k, :] for k in range(5))
            evac(V.tensor_scalar(over_cap, bank[:, 16:24], float(CAP), None, ALU.is_gt))
            read_back()
            step(V.tensor_scalar(rank[:, :, 0:8], rank[:, :, 0:8], -1000.0, None, ALU.add))

            def find_extra():
                step(V.memset(place, 0.0))
                for i in range(1, N_EXP):
                    step(V.tensor_tensor(place[:, i:i + 1], place[:, i - 1:i], over_cap[:, i - 1:i], ALU.add))
                for j in range(EXTRA):
                    step(V.scalar_tensor_tensor(mine, place, float(j), over_cap, ALU.is_equal, ALU.mult))
                    step(V.tensor_reduce(seen[:, 0:1], mine, AX.X, ALU.add))
                    for b in range(TB):
                        for src, dst in ((rank, rank), (gates, gates)):
                            step(V.tensor_tensor(junk, mine, src[:, b, 0:8], ALU.mult))
                            step(V.tensor_reduce(dst[:, b, N_EXP + j:N_EXP + j + 1], junk, AX.X, ALU.add))
                        at = rank[:, b, N_EXP + j:N_EXP + j + 1]
                        step(V.scalar_tensor_tensor(at, seen[:, 0:1], 1000.0, at, ALU.mult, ALU.add))
                        step(V.tensor_scalar(at, at, -1000.0 - CAP, None, ALU.add))
                    step(V.tensor_copy(extra[:, j:j + 1], seen[:, 0:1]))
                    step(V.tensor_tensor(junk, mine, iota[:, 0:8], ALU.mult))
                    step(V.tensor_reduce(seen[:, 1:2], junk, AX.X, ALU.add))
                    ins = V.tensor_copy(extra[:, EXTRA + j:EXTRA + j + 1], seen[:, 1:2])
                    if j == EXTRA - 1:
                        ins.then_inc(route_mask, 1)
                        dve.wait_ge(route_mask, 2)
                    else:
                        step(ins)

            step(V.memset(acc[:, :, :], 0.0))

            def choose(e):
                col = (lambda v, b: v[:, b, e:e + 1]) if isinstance(e, int) else (
                    lambda v, b: v[:, b, bass.ds(e, 1)])
                for b in range(TB):
                    V.tensor_scalar(sel[:, b, :], iota, col(rank, b), None, ALU.is_equal)
                    ins = V.tensor_scalar(sel_g[:, b, :], iota, col(rank, b), col(gates, b), ALU.is_equal, ALU.mult)
                ins.then_inc(SG[0].picked, 1)

            def gathered():
                for j in range(4):
                    turn_in(xg_t[:, 2 * j:2 * j + 2, :])

            def gates_in():
                turn_in(sel_gt)

            def expert(e, _):
                def hidden_in(t):
                    turn_in(hide_t[:, 4 * t:4 * t + 4, :])

                for t in range(MOE_TILES):
                    n = C.tile.take(2)
                    dve.wait_ge(SG[0].tile_evac, C.tile.at(n) + 2)
                    V.tensor_tensor(hs_e[:, t % 2, :], hs_e[:, t % 2, :], hu_e[:, t % 2, :],
                                    ALU.mult).then_inc(SG[0].gated, 1)
                    C.gated.n += 1
                    if t > 0:
                        hidden_in(t - 1)
                C.tile.take(2)
                C.picked.take()
                choose(e + 1)
                hidden_in(MOE_TILES - 1)
                gathered()
                for b in range(TB):
                    for h in range(2):
                        y = acc[:, b, h * 512:(h + 1) * 512]
                        evac(V.tensor_tensor(y, y, aux_in()[:, :], ALU.add))
                read_back()
                gates_in()

            choose(0)
            C.picked.n += 1
            find_extra()
            gathered()
            gates_in()
            rolled(dve, C, expert, route_mask, extra)
            V.memset(small[:, 21:22], 0.0).then_inc(params_used, 1)
            C, SG[0] = Counts(), S2
            for b in range(TB):
                step(V.scalar_tensor_tensor(x[:, b, :], x[:, b, :], ALPHA, acc[:, b, :], ALU.mult, ALU.add))
            layer_norm(3)

            for l in range(DEPTH):
                if l == 0:
                    dve.wait_ge(nat_ready, TB * (NORM_STAGE[3] + 1))
                rms_norm(4 + 2 * l)
                turn_all_in()
                C.tile.n += 16
                dve.wait_ge(S2.tile_evac, C.tile.n)
                dve.wait_ge(params_loaded, 16 * (PARAMS1 + PARAMS2 * (l + 1)))
                turn_in(taps[:, :, :])
                step(V.memset(cbuf[:, :], 0.0))
                bank = aux_in()
                for k in range(2):
                    V.tensor_copy(c_t[0:64, 3 * k + 2, 0:CMP_BLOCK], bank[0:64, k * 32:(k + 1) * 32])
                    ins = V.tensor_copy(c_t[64:128, 3 * k + 2, 0:CMP_BLOCK - 1],
                                        bank[0:64, k * 32 + 1:(k + 1) * 32])
                evac(ins)
                for b in range(TB):
                    bank = aux_in()
                    src = bank[0:64, :].rearrange("p (k g t) -> p k g t", k=2, g=2)
                    lo = 1 if b == 0 else 0
                    for k in range(2):
                        V.tensor_copy(c_t[0:64, 3 * k:3 * k + 2, b * P:(b + 1) * P], src[:, k, :, :])
                        ins = V.tensor_copy(c_t[64:128, 3 * k:3 * k + 2, b * P - 1 + lo:(b + 1) * P - 1],
                                            src[:, k, :, lo:P])
                    evac(ins)
                    turn_in(k_t[:, 0:4, b * P:(b + 1) * P])
                    for h in range(2):
                        turn_in(q_t[:, 4 * h:4 * h + 4, b * P:(b + 1) * P])
                for k in range(2):
                    bank = aux_in()
                    evac(V.tensor_copy(hidp[:, k, :], bank[:, 0:45]))
                    read_back()
                    V.memset(small[:, 22:23], 0.0).then_inc(hidc_in, 1)
                bank = aux_in()
                evac(V.tensor_copy(kcmp[:, :, :], bank[0:64, 0:2 * N_CMP].rearrange("p (g n) -> p g n", g=2)))
                bank = aux_in()
                evac(V.tensor_copy(vcmp[:, :, :], bank[0:N_CMP, 0:128].rearrange("p (g d) -> p g d", g=2)))
                bank = aux_in()
                for b in range(TB):
                    n = NSA_H * N_CMP
                    ins = V.tensor_tensor(sc_c[:, b, :, :],
                                          bank[:, b * n:(b + 1) * n].rearrange("p (h n) -> p h n", h=NSA_H),
                                          bias_c[:, b, :, :].rearrange("p n h -> p h n"), ALU.add)
                evac(ins)
                read_back()
                s2 = sc_c[:, :, :, :].rearrange("p b h n -> p (b h) n")
                step(V.tensor_reduce(small[:, 0:16], s2, AX.X, ALU.max))
                step(V.tensor_scalar(small[:, 0:16], small[:, 0:16], -1e29, None, ALU.max))
                V.tensor_tensor(s2, s2, spread(small[:, 0:16], N_CMP), ALU.subtract).then_inc(cmp_scores, 1)
                dve.wait_ge(cmp_exp, l + 1)
                step(V.tensor_reduce(small[:, 0:16], s2, AX.X, ALU.add))
                step(V.tensor_scalar(small[:, 0:16], small[:, 0:16], 1e-30, None, ALU.max))
                step(V.reciprocal(small[:, 16:32], small[:, 0:16]))
                step(V.tensor_tensor(small[:, 0:16].rearrange("p (b h) -> p b h", b=TB),
                                     small[:, 16:32].rearrange("p (b h) -> p b h", b=TB),
                                     gates2[:, :, 0:24:3], ALU.mult))
                V.tensor_tensor(s2, s2, spread(small[:, 0:16], N_CMP), ALU.mult).then_inc(cmp_probs, 1)
                for b in range(TB):
                    for h2 in range(2):
                        turn_in(pc_t[:, 4 * h2:4 * h2 + 4, :])
                    evac(V.tensor_copy(o_cmp[:, b, :], aux_in()[:, :]))

                def scores(u):
                    nk = (u % TB + 1) * P
                    score_rows(aux_in(), u % 2, bias2[:, u // TB, :], nk, lambda m: m * nk)

                def turned(u):
                    h, b = divmod(u, TB)
                    s, nk = u % 2, (b + 1) * P
                    dve.wait_ge(probs_ready, (DEPTH * HEADS1 + l * NSA_H) * TB + u + 1)
                    step(V.reciprocal(coef[:, s, 0:2], den[:, s, :]))
                    step(V.tensor_tensor(coef[:, s, 2:4], coef[:, s, 0:2], gates2[:, b, 3 * h + 1:3 * h + 3], ALU.mult))
                    turn_in(p_t[:, s, 0:2 * nk].rearrange("p (k q) -> p k q", q=P))

                def values(u):
                    h, b = divmod(u, TB)
                    s = u % 2
                    bank = aux_in()
                    o = nat[:, b, h * 64:(h + 1) * 64]
                    step(V.scalar_tensor_tensor(o, bank[:, 0:64], coef[:, s, 2:3], o_cmp[:, b, h * 64:(h + 1) * 64],
                                                ALU.mult, ALU.add))
                    evac(V.scalar_tensor_tensor(o, bank[:, 64:128], coef[:, s, 3:4], o, ALU.mult, ALU.add))

                pipelined(NSA_H * TB, scores, turned, values)

                t1 = sc[:, 0, 0, :].rearrange("p (h d) -> p h d", h=8)
                t2 = sc[:, 1, 0, :].rearrange("p (h d) -> p h d", h=8)
                for b in range(TB):
                    qk = z[:, 3, b, :].rearrange("p (h d) -> p h d", h=8)
                    lo, hi = qk[:, :, 0:32], qk[:, :, 32:64]
                    cos, sin = over(rope_cos[:, b, :], 8), over(rope_sin[:, b, :], 8)
                    V.tensor_tensor(t1, hi, sin, ALU.mult)
                    V.tensor_tensor(t2, lo, sin, ALU.mult)
                    V.tensor_tensor(rot[:, b, :, 0:32], lo, cos, ALU.mult)
                    step(V.tensor_tensor(rot[:, b, :, 32:64], hi, cos, ALU.mult))
                    V.tensor_tensor(rot[:, b, :, 0:32], rot[:, b, :, 0:32], t1, ALU.subtract)
                    ins = V.tensor_tensor(rot[:, b, :, 32:64], rot[:, b, :, 32:64], t2, ALU.add)
                    if b == TB - 1:
                        ins.then_inc(rot_ready, 1)
                    else:
                        step(ins)
                for b in range(TB):
                    for h in range(2):
                        turn_in(q_t[:, 4 * h:4 * h + 4, b * P:(b + 1) * P])

                def ret_scores(h):
                    bank = aux_in()
                    evac(V.tensor_tensor(p_t[:, h % 2, 0:3 * P], bank[:, 0:3 * P], decay[:, h, :], ALU.mult))

                def ret_values(h):
                    bank = aux_in()
                    evac(V.tensor_copy(nat[:, :, 512 + h * P:512 + (h + 1) * P],
                                       bank[:, 0:2 * P].rearrange("p (b d) -> p b d", b=TB)))

                ret_scores(0)
                for h in range(RET_H):
                    if h + 1 < RET_H:
                        ret_scores(h + 1)
                    ret_values(h)
                for b in range(TB):
                    V.tensor_tensor(z[:, 6, b, :], z[:, 6, b, :], z[:, 7, b, :], ALU.mult).then_inc(conv_in, 1)
                step(V.memset(u_t[:, :, 0:PAD], 0.0))
                for b in range(TB):
                    turn_in(u_t[:, :, PAD + b * P:PAD + (b + 1) * P])
                for b in range(TB):
                    o = nat[:, b, 512:1024].rearrange("p (h d) -> p h d", h=RET_H)
                    standardise(o, o, EPS2)
                    o = nat[:, b, 512:1024]
                    step(V.tensor_tensor(o, o, ret_gn[:, :], ALU.mult))
                    V.tensor_tensor(o, o, z[:, 5, b, :], ALU.mult).then_inc(nat_ready, 1)
                for b in range(TB):
                    for r in range(2):
                        turn_in(br_t[:, r, :, b * P:(b + 1) * P])
                read_back()
                for j in range(CONV_W):
                    for c in range(4):
                        if j == 0:
                            own.n += 1
                            V.tensor_scalar(y_t[:, c, :], u_t[:, c, j:j + SEQ], taps[:, c, j:j + 1],
                                            taps[:, c, CONV_W:CONV_W + 1], ALU.mult, ALU.add).then_inc(vec, 1)
                            continue
                        dve.wait_ge(vec, own.n - 3)
                        ins = V.scalar_tensor_tensor(y_t[:, c, :], u_t[:, c, j:j + SEQ], taps[:, c, j:j + 1],
                                                     y_t[:, c, :], ALU.mult, ALU.add)
                        if j == CONV_W - 1 and c == 3:
                            ins.then_inc(conv_out, 1)
                        else:
                            own.n += 1
                            ins.then_inc(vec, 1)
                for b in range(TB):
                    turn_in(nat[:, b, 0:512].rearrange("p (c d) -> p c d", c=4))
                read_back()
                standardise(nat[:, :, 0:512], nat[:, :, 0:512], EPS2)
                for b in range(TB):
                    o = nat[:, b, 0:512]
                    step(V.tensor_tensor(o, o, conv_ln[:, 0, :], ALU.mult))
                    V.tensor_tensor(o, o, conv_ln[:, 1, :], ALU.add).then_inc(conv_norm, 1)
                for b in range(TB):
                    turn_in(br_t[:, 2, :, b * P:(b + 1) * P])
                C.tile.n += 12
                for r in range(3):
                    for b in range(TB):
                        C.tile.n += 2
                        dve.wait_ge(S2.tile_evac, C.tile.n)
                        if r == 0:
                            V.tensor_tensor(nat[:, b, :], sig[0][:, b, :], acc[:, b, :], ALU.mult).then_inc(merged, 1)
                            continue
                        g = sig[r][:, b, :]
                        ins = V.tensor_tensor(g, g, acc[:, b, :], ALU.mult)
                        if r == 1:
                            ins.then_inc(merged, 1)
                            dve.wait_ge(merged, (2 * l + 1) * TB + b + 1)
                            step(V.tensor_tensor(nat[:, b, :], nat[:, b, :], g, ALU.add))
                        else:
                            step(ins)
                            V.tensor_tensor(nat[:, b, :], nat[:, b, :], g, ALU.add).then_inc(nat_ready, 1)
                turn_all_in()
                add_products(1.0)
                rms_norm(5 + 2 * l)
                turn_all_in()

                def hidden_in(t):
                    for b in range(TB):
                        turn_in(hid_t[:, 4 * t:4 * t + 4, b * P:(b + 1) * P])

                for t in range(D_FF2 // 512):
                    C.tile.n += 2
                    dve.wait_ge(S2.tile_evac, C.tile.n)
                    g = hs[:, t % 2, :, :]
                    V.tensor_tensor(g, g, g, ALU.mult).then_inc(gated2, 1)
                    if t > 0:
                        hidden_in(t - 1)
                hidden_in(D_FF2 // 512 - 1)
                read_back()
                V.memset(small[:, 21:22], 0.0).then_inc(params_used, 1)
                add_products(1.0)
            rms_norm(8)


def buckets(dist):
    n = np.maximum(dist, 0)
    exact = BUCKETS // 2
    far = np.maximum(n, 1).astype(np.float32)
    large = exact + (np.log(far / np.float32(exact)) / np.float32(math.log(MAX_DIST / exact))
                     * np.float32(BUCKETS - exact)).astype(np.int32)
    return np.where(n < exact, n, np.minimum(large, BUCKETS - 1))


def one_hot_buckets(dist):
    rows = (np.arange(BUCKETS).reshape(-1, *[1] * dist.ndim) == buckets(dist)) & (dist >= 0)
    return np.concatenate([rows.astype(np.float32), np.where(dist < 0, NEG, 0.0).astype(np.float32)[None]])


def tables():
    i = np.arange(P)
    half = RET_DK // 2
    inv = 10000.0 ** (-np.arange(half, dtype=np.float32) / np.float32(half))
    ang = (np.arange(SEQ, dtype=np.float32)[:, None] * inv[None, :].astype(np.float32)).astype(np.float32)
    trig = [f(ang.astype(np.float64)).reshape(TB, P, half).transpose(1, 0, 2).reshape(P, TB * half)
            for f in (np.cos, np.sin)]
    small = np.concatenate([np.eye(P), i[:, None] <= i[None, :], i[:, None] < i[None, :],
                            np.broadcast_to(i, (P, P)), *trig], axis=1)
    rows = one_hot_buckets(SEQ - 1 - np.arange(512))
    block_end = CMP_STRIDE * np.arange(N_CMP) + CMP_BLOCK - 1
    dist_c = np.arange(SEQ).reshape(TB, 1, P) - block_end.reshape(1, N_CMP, 1)
    onehot = np.concatenate([rows, one_hot_buckets(dist_c).reshape(BUCKETS + 1, -1)], axis=1)
    t = np.arange(SEQ)
    pool = []
    for w in WINDOWS:
        inside = (t[:, None] <= t[None, :]) & (t[:, None] > t[None, :] - w)
        pool.append(inside / np.minimum(t + 1, w)[None, :] - np.eye(SEQ))
    pool = np.stack(pool).reshape(4, TB, P, SEQ).transpose(2, 1, 0, 3).reshape(P, -1)
    log_g = np.log1p(-np.exp2(-5.0 - np.arange(RET_H)))
    diff = t[None, :] - i[:, None]
    decay = np.where(diff >= 0, np.exp(log_g[:, None, None] * np.maximum(diff, 0)), 0.0) * RET_DK ** -0.5
    decay = np.concatenate([decay, decay[:, :, 0:P]], axis=2).transpose(1, 0, 2).reshape(P, -1)
    named = {"c_small": small, "c_onehot": onehot, "c_pool": pool, "c_decay": decay}
    return {n: np.ascontiguousarray(v, dtype=np.float32) for n, v in named.items()}


def kernel(**inputs):
    import concourse.bacc as bacc
    from concourse.bass_utils import run_bass_kernel_spmd

    nc = bacc.Bacc("TRN2", target_bir_lowering=False, num_devices=1)
    arrays, aps = {}, {}
    for name, a in {**inputs, **tables()}.items():
        a = np.ascontiguousarray(a)
        arrays[f"in_{name}"] = a
        aps[name] = nc.dram_tensor(f"in_{name}", a.shape, mybir.dt.from_np(a.dtype), kind="ExternalInput").ap()
    out = nc.dram_tensor("out_x", (1, SEQ, D), F32, kind="ExternalOutput").ap()
    build(nc, aps, out)
    r = run_bass_kernel_spmd(nc, [arrays], core_ids=[0])
    return r.results[0]["out_x"]
```

```python
import math

import numpy as np

import concourse.bass as bass
from concourse import mybir
from contextlib import ExitStack

F32 = mybir.dt.float32
F32R = mybir.dt.float32r
I32 = mybir.dt.int32
U32 = mybir.dt.uint32
ALU = mybir.AluOpType
ACT = mybir.ActivationFunctionType
AX = mybir.AxisListType

P = 128
SEQ, D = 256, 1024
TB = SEQ // P
KC = D // P
DEPTH = 2
HEADS1, DH1 = 4, 64
D_FF, N_EXP, D_FFE = 2816, 8, 3584
NSA_H, NSA_G, DH2 = 8, 2, 64
RET_H, RET_DK, RET_DV = 4, 64, 128
CONV_CH, CONV_W = 512, 31
CMP_BLOCK, CMP_STRIDE = 32, 16
N_CMP = SEQ // CMP_STRIDE - CMP_BLOCK // CMP_STRIDE + 1
D_FF2 = 4096
BUCKETS, MAX_DIST = 32, 128
WINDOWS = (2, 4, 8, 16)
ALPHA = (2 * DEPTH) ** 0.25
EPS1, EPS2 = 1e-5, 1e-6
QSCALE = DH1 ** -0.5
NEG = -1e30
UNITS = 7
HIGHS = 4
MOE_LOW = 640
REACH = SEQ + P
CAP = P
EXTRA = 2 * SEQ // (CAP + 1)
ROUNDS = N_EXP + EXTRA
assert SEQ <= 2 * CAP

TILES1 = [(0, 512), (512, 512), (1024, 512), (1536, 512), (2048, 256)]
TILES2 = [(0, 512), (512, 512), (1024, 280), (1304, 512), (1816, 512), (2328, 512), (2840, 512),
          (3352, 512)] + [(3864 + 512 * i, 512) for i in range(6)]
FF_PARTS = [[(c, min(512, D_FF - c)) for c in range(a, min(a + 1536, D_FF), 512)] for a in (0, 1536)]
FF2_PARTS = [[(c, 512) for c in range(a, a + 2048, 512)] for a in (0, 2048)]
MOE_TILES = D_FFE // 512


def lam_init(layer):
    return 0.8 - 0.6 * math.exp(-0.3 * layer)


def narrow_units(tiles):
    return [2 * width for _, width in tiles for _ in range(KC // 2)]


def wide_units(rows):
    return [D] * (rows // P)


def part_units(parts, matrices):
    return sum([narrow_units([t for t in part for _ in range(matrices)])
                + wide_units(sum(width for _, width in part)) for part in parts], [])


IN1, OUT1, FF1 = narrow_units(TILES1), wide_units(D), part_units(FF_PARTS, 2)
IN2, GATE2 = narrow_units(TILES2[0:8]), narrow_units(TILES2[8:14])
BRANCH2, OUT2, FF2 = 3 * wide_units(512), wide_units(D), part_units(FF2_PARTS, 1)
STREAM1 = IN1 + OUT1 + FF1 + IN1 + OUT1
STREAM2 = DEPTH * (IN2 + GATE2 + BRANCH2 + OUT2 + FF2)


class Tally:

    def __init__(self):
        self.n, self.i, self.per = 0, None, 0

    def at(self, n):
        return n if self.i is None else n + self.i * self.per

    def take(self, k=1):
        self.n += k
        return self.n - k


class Signals:

    def __init__(self, sem, suffix=""):
        self.unit_loaded = [sem(f"unit_loaded{i}{suffix}") for i in range(UNITS)]
        self.high_ready = sem("high_ready" + suffix)
        self.low_pool = sem("low_pool" + suffix)
        self.low_vec = sem("low_vec" + suffix)
        self.unit_done = sem("unit_done" + suffix)
        self.tile_full = sem("tile_full" + suffix)
        self.tile_evac = sem("tile_evac" + suffix)
        self.aux_full = sem("aux_full" + suffix)
        self.aux_evac = sem("aux_evac" + suffix)
        self.vec = sem("vec" + suffix)
        self.gated = sem("gated" + suffix)
        self.picked = sem("picked" + suffix)


class Counts:

    def __init__(self):
        self.unit, self.split, self.tile, self.full = Tally(), Tally(), Tally(), Tally()
        self.aux, self.gated, self.picked, self.low, self.own = (Tally() for _ in range(5))

    def all(self):
        return [self.unit, self.split, self.tile, self.full, self.aux, self.gated, self.picked, self.low,
                self.own]


PARAMS1, PARAMS2, FILLS = 3 + 9 * DEPTH, 12, 5
NORM_STAGE = [1, 2, 4, 5, 6, 9, 10, 13, 14]

GATHER_AT = 4
MOE_UNITS = (2 * MOE_TILES * KC) // 2 + D_FFE // P
assert MOE_UNITS % UNITS == 0 and MOE_UNITS % HIGHS == 0
MOE_PER = (MOE_UNITS, MOE_UNITS, MOE_TILES * 2 + 2, 1, 16, MOE_TILES, 1, MOE_UNITS, MOE_TILES + 4)


def rolled(eng, C, body, routed, extra):
    begun = [t.n for t in C.all()]

    def turn(e, expert):
        for t, n, per in zip(C.all(), begun, MOE_PER):
            t.n, t.i, t.per = n, e, per
        body(e, expert)
        for t, n, per in zip(C.all(), begun, MOE_PER):
            assert t.n - n in (0, per), (t.n - n, per)

    with eng.Fori(0, N_EXP) as e:
        turn(e, e)
    eng.wait_ge(routed, 2)
    with eng.Fori(N_EXP, ROUNDS) as e:
        active = eng.value_load(extra[0:1, bass.ds(e - N_EXP, 1)], min_val=0, max_val=1)
        with eng.If(active):
            turn(e, eng.value_load(extra[0:1, bass.ds(e - N_EXP + EXTRA, 1)], min_val=0, max_val=N_EXP - 1))


def wait(eng, sem, value):
    if not isinstance(value, int) or value > 0:
        eng.wait_ge(sem, value)


def build(nc, A, out):
    ctx = ExitStack()
    with ctx:
        def sb(name, shape, dt=F32, where=ctx):
            return where.enter_context(nc.sbuf_tensor(name, shape, dt))

        def shared(name, shape):
            with ExitStack() as first:
                plain = sb(name, shape, F32, first)
            return plain, sb(name + "_parts", shape, F32R)

        def sem(name):
            return ctx.enter_context(nc.semaphore(name))

        ring, lows = zip(*(shared(f"unit{i}", [P, 1024]) for i in range(UNITS)))
        highs = [sb(f"high{i}", [P, 1024], F32R) for i in range(HIGHS)]
        x = sb("x_sb", [P, TB, D])
        nat = sb("nat", [P, TB, D])
        acts = sb("acts", [P, 2, KC, SEQ], F32R)
        act_t = [acts[:, i, :, :] for i in range(2)]
        acc = sb("acc", [P, TB, D])
        zbuf, zparts = shared("zbuf", [P, 8192])
        z = zbuf[:, :].rearrange("p (t b n) -> p t b n", t=8, b=TB)

        def hidden_parts(chunks):
            return [zparts[:, i * chunks * SEQ:(i + 1) * chunks * SEQ].rearrange("p (c t) -> p c t", t=SEQ)
                    for i in range(2)]

        hid1_t, hid2_t = hidden_parts(12), hidden_parts(16)
        gbuf, gparts = shared("gbuf", [P, 4096])
        hs = gbuf[:, 0:2048].rearrange("p (i b n) -> p i b n", i=2, b=TB)
        hu = gbuf[:, 2048:4096].rearrange("p (i b n) -> p i b n", i=2, b=TB)
        br_high = gparts[:, 0:3072].rearrange("p (r c t) -> p r c t", r=3, c=4)
        br_low = [zparts[:, t * 1024:(t + 1) * 1024].rearrange("p (c t) -> p c t", t=SEQ)
                  for t in (4, 5, 7)]
        br_t = [[br_high[:, r, :, :], br_low[r]] for r in range(3)]
        cmp_w1 = gbuf[:, :].rearrange("p (k l f) -> p k l f", k=2, l=CMP_BLOCK // 2)
        q_buf = sb("q_buf", [P, 8 * SEQ])
        q_t = q_buf[0:64, :].rearrange("p (h t) -> p h t", h=8)
        k_t = sb("k_t", [64, 8, SEQ])
        sc = sb("sc", [P, 2, 2, SEQ])
        p_t = sb("p_t", [P, 2, 512])
        gain = sb("gain", [P, 2, D])
        bias2 = sb("bias2", [P, NSA_H, SEQ])
        bias_c = sb("bias_c", [P, TB, N_CMP, NSA_H])
        consts = sb("consts_sb", [P, 640])
        ident, triu, before, iota = (consts[:, i * P:(i + 1) * P] for i in range(4))
        rope_cos = consts[:, 512:576].rearrange("p (b d) -> p b d", b=TB)
        rope_sin = consts[:, 576:640].rearrange("p (b d) -> p b d", b=TB)
        ones = sb("ones", [P, P])
        half = sb("half", [P, 8])
        rs_in = sb("rs_in", [P, 8])
        rs_out = sb("rs_out", [P, 8])
        stats = sb("stats", [P, 8, 2, 6])
        mv = sb("mv", [P, 8, 2])
        negm = sb("negm", [P, 2, 2])
        den = sb("den", [P, 2, 2])
        coef = sb("coef", [P, 2, 4])
        small = sb("small", [P, 65])
        biasrow = acc[0:8, 0, :].rearrange("p (i n) -> p i n", i=2)
        rel1 = sb("rel1", [BUCKETS + 1, HEADS1])
        rel2 = sb("rel2", [BUCKETS + 1, NSA_H])
        extra = sb("extra", [P, 2 * EXTRA], I32)

        one = ExitStack()
        with one:
            gm_ws = sb("gm_ws", [P, DEPTH, 4, P], where=one)
            gm_bs = sb("gm_bs", [P, DEPTH, 4], where=one)
            lamv = sb("lamv", [P, 4, DEPTH, 64], where=one)
            subln = sb("subln", [P, DEPTH, P], where=one)
            pool_w = sb("pool_w_sb", [64, DEPTH, 4, 64], where=one)
            pool_s = sb("pool_s", [P, DEPTH, 256], where=one)
            bias1 = sb("bias1", [P, HEADS1, SEQ], where=one)
            gm_wt = sb("gm_wt", [P, 4, P], where=one)
            router = sb("router", [P, KC, N_EXP], where=one)
            lam = sb("lam", [P, 8], where=one)
            logits = sb("logits", [P, TB, 8], where=one)
            top = sb("top", [P, TB, 8], where=one)
            topi = sb("topi", [P, TB, 8], U32, where=one)
            topf = sb("topf", [P, TB, 8], where=one)
            pick = sb("pick", [P, TB, 3, 8], where=one)
            gates = sb("gates", [P, TB, ROUNDS + 1], where=one)
            rank = sb("rank", [P, TB, ROUNDS + 1], where=one)
            mask = sb("mask", [P, TB, N_EXP], where=one)
            excess = sb("excess", [P, 5, N_EXP], where=one)
        poolT = p_t[0:64, :, :].rearrange("p i (a t) -> p (i a) t", a=2)
        pool_a = z[:, 6:8, :, :].rearrange("p t b (g n) -> p (t b g) n", g=2)
        onehot = acc[0:BUCKETS + 1, 1, 0:512]
        onehot_c = gbuf[0:BUCKETS + 1, 0:TB * N_CMP * P].rearrange(
            "p (b n q) -> p b n q", b=TB, n=N_CMP)
        xg_t = [act_t[i][:, 0:4, :].rearrange("p c (h n) -> p (c h) n", h=2) for i in range(2)]
        sel, sel_g = (sc[:, i, :, 0:P] for i in range(2))
        sel_gt = sc[:, 0, :, P:2 * P]
        ye = gbuf[:, 1024:2048]
        hs_e = gbuf[:, 0:1024].rearrange("p (i n) -> p i n", i=2)
        hu_e = gbuf[:, 2048:3072].rearrange("p (i n) -> p i n", i=2)
        hide_t = [zparts[:, i * 4096:i * 4096 + D_FFE].rearrange("p (c n) -> p c n", n=CAP) for i in range(2)]

        two = ExitStack()
        with two:
            decay = sb("decay", [P, RET_H, 384], where=two)
            ret_gn = sb("ret_gn", [P, 512], where=two)
            conv_nat = sb("conv_nat", [CONV_W + 1, CONV_CH], where=two)
            conv_ln = sb("conv_ln", [P, 2, CONV_CH], where=two)
            cmp_w2 = sb("cmp_w2", [P, 2, 64], where=two)
            pe_nat = sb("pe_nat", [CMP_BLOCK, 2, 64], where=two)
            taps = sb("taps", [P, 4, CONV_W + 1], where=two)
            cbuf = sb("cbuf", [P, 6 * SEQ], where=two)
            hidp = sb("hidp", [P, 2, 45], where=two)
            hidc = sb("hidc", [P, 2, 2 * N_CMP], where=two)
            kcmp = sb("kcmp", [64, 2, N_CMP], where=two)
            vcmp = sb("vcmp", [N_CMP, 2, 64], where=two)
            sc_c = sb("sc_c", [P, TB, NSA_H, N_CMP], where=two)
            gates2 = sb("gates2", [P, TB, 24], where=two)
        pc_t = p_t[0:N_CMP, :, :].rearrange("p i (h q) -> p (i h) q", q=P)
        c_t = cbuf[:, :].rearrange("p (s t) -> p s t", s=6)
        PAD = CONV_W - 1
        u_t = cbuf[:, 0:4 * (PAD + SEQ)].rearrange("p (c t) -> p c t", c=4)
        y_t = z[:, 6, :, :].rearrange("p b (c t) -> p (b c) t", t=SEQ)
        o_cmp = acc[:, 0, :].rearrange("p (b n) -> p b n", b=TB)
        rot = acc[:, 1, :].rearrange("p (b h d) -> p b h d", b=TB, h=8)
        sig = [z[:, 0:2, :, :].rearrange("p t b n -> p (t b n)").rearrange("p (b n) -> p b n", b=TB),
               z[:, 2:4, :, :].rearrange("p t b n -> p (t b n)").rearrange("p (b n) -> p b n", b=TB),
               q_buf[:, :].rearrange("p (b n) -> p b n", b=TB)]

        tiles = [ctx.enter_context(nc.psum_tensor(f"tile{i}", [P, 512], F32)) for i in range(4)]
        aux = [ctx.enter_context(nc.psum_tensor(f"aux{i}", [P, 512], F32)) for i in range(4)]
        rows = nc.dram_tensor("bias_rows", (HEADS1 + NSA_H, P, REACH), F32)

        S = Signals(sem)
        S2 = Signals(sem, "_2")
        x_loaded = sem("x_loaded")
        small_loaded = sem("small_loaded")
        consts_loaded = sem("consts_loaded")
        filled = sem("filled")
        params_loaded = sem("params_loaded")
        layer_loaded = sem("layer_loaded")
        cmp_loaded = sem("cmp_loaded")
        params_used = sem("params_used")
        gain_loaded = sem("gain_loaded")
        gain_used = sem("gain_used")
        rows_ready = sem("rows_ready")
        rows_stored = sem("rows_stored")
        bias_loaded = sem("bias_loaded")
        nat_ready = sem("nat_ready")
        var_ready = sem("var_ready")
        rstd_ready = sem("rstd_ready")
        scores_ready = sem("scores_ready")
        probs_ready = sem("probs_ready")
        attn_ready = sem("attn_ready")
        vn_ready = sem("vn_ready")
        lam_dots = sem("lam_dots")
        lam_exp = sem("lam_exp")
        route_dif = sem("route_dif")
        route_exp = sem("route_exp")
        route_mask = sem("route_mask")
        merged = sem("merged")
        hidc_in = sem("hidc_in")
        hidc_ready = sem("hidc_ready")
        cmp_scores = sem("cmp_scores")
        cmp_exp = sem("cmp_exp")
        cmp_probs = sem("cmp_probs")
        rot_ready = sem("rot_ready")
        conv_in = sem("conv_in")
        conv_out = sem("conv_out")
        conv_norm = sem("conv_norm")
        conv_act = sem("conv_act")
        out_stored = sem("out_stored")
        gated2 = sem("gated2")

        gains = ([("ln1_g", 0, "ln1_b"), ("ln2_g", 0, "ln2_b"), ("ln1_g", 1, "ln1_b"), ("ln2_g", 1, "ln2_b")]
                 + [(n, l, None) for l in range(DEPTH) for n in ("norm_mix_2", "norm_mlp_2")]
                 + [("norm_final_2", None, None)])
        def row(src, width):
            return src.rearrange("(o n) -> o n", o=1).to_broadcast([P, width])

        block = ctx.enter_context(nc.Block())

        @block.sync
        def _(sp):
            C = Counts()

            def unit(sig_, dst, src):
                n = C.unit.take()
                wait(sp, sig_.unit_done, C.unit.at(n - UNITS + 1))
                sp.dma_start(dst(ring[n % UNITS]), src).then_inc(sig_.unit_loaded[n % UNITS], 16)

            def narrow(sig_, w, c0, width):
                for r0 in range(0, D, 256):
                    unit(sig_, lambda r: r[:, 0:2 * width].rearrange("p (c n) -> p c n", c=2),
                         w[r0:r0 + 256, c0:c0 + width].rearrange("(c p) n -> p c n", p=P))

            def wide(sig_, w, first, rows_):
                for r0 in range(first, first + rows_, P):
                    unit(sig_, lambda r: r[:, :], w[r0:r0 + P, :])

            def hidden(sig_, parts, w1s, w2):
                for part in parts:
                    for c0, width in part:
                        for w1 in w1s:
                            narrow(sig_, w1, c0, width)
                    wide(sig_, w2, part[0][0], sum(width for _, width in part))

            def expert(sig_, e):
                w1, w3, w2 = (A[n][0, bass.ds(e, 1)].rearrange("o k n -> (o k) n")
                              for n in ("moe_w1", "moe_w3", "moe_w2"))
                for t in range(MOE_TILES):
                    narrow(sig_, w1, t * 512, 512)
                    narrow(sig_, w3, t * 512, 512)
                wide(sig_, w2, 0, D_FFE)

            sp.dma_start(x[:, :, :], A["x"][0].rearrange("(b p) d -> p b d", p=P)).then_inc(x_loaded, 16)
            sp.dma_start(consts[:, :], A["c_small"]).then_inc(small_loaded, 16)
            for l in range(DEPTH):
                for c0, width in TILES1:
                    narrow(S, A["w_in"][l], c0, width)
                wide(S, A["w_out"][l], 0, D)
                if l == 0:
                    hidden(S, FF_PARTS, (A["ffn_w1"][0], A["ffn_w3"][0]), A["ffn_w2"][0])
                else:
                    rolled(sp, C, lambda _, e: expert(S, e), route_mask, extra)
            sp.wait_ge(params_used, 1)
            C = Counts()
            for l in range(DEPTH):
                for c0, width in TILES2:
                    narrow(S2, A["w_in_2"][l], c0, width)
                for r in range(3):
                    wide(S2, A["w_branch_2"][l, r], 0, 512)
                wide(S2, A["w_out_2"][l], 0, D)
                hidden(S2, FF2_PARTS, (A["w_ff1_2"][l],), A["w_ff2_2"][l])
            sp.wait_ge(nat_ready, TB * (NORM_STAGE[-1] + 1))
            sp.dma_start(out[0].rearrange("(b p) d -> p b d", p=P), nat[:, :, :]).then_inc(out_stored, 16)
            sp.wait_ge(out_stored, 16)

        @block.tensor
        def _(pe):
            C = Counts()
            SG = [S]

            def unit(shared):
                n = C.unit.take()
                pe.wait_ge(SG[0].low_pool, C.unit.at(n) + 1)
                if shared:
                    pe.wait_ge(SG[0].low_vec, C.low.at(C.low.take()) + 1)
                return highs[n % HIGHS][:, :], lows[n % UNITS][:, :]

            def products(bank, lhs, high, low, start, stop):
                nc.tensor.matmul(bank, lhs[0], high, start=start, stop=False)
                nc.tensor.matmul(bank, lhs[0], low, start=False, stop=False)
                return nc.tensor.matmul(bank, lhs[1], high, start=False, stop=stop)

            def tile_bank():
                n = C.tile.take()
                wait(pe, SG[0].tile_evac, C.tile.at(n - 3))
                return tiles[n % 4]

            def aux_bank():
                n = C.aux.take()
                wait(pe, SG[0].aux_evac, C.aux.at(n - 3))
                return aux[n % 4]

            def aux_done():
                wait(pe, SG[0].aux_evac, C.aux.at(C.aux.n))

            def narrow(width, lhs, blocks=TB, shared=False, when=None):
                banks = {}
                for k in range(KC // 2):
                    high, low = (v[:, 0:2 * width].rearrange("p (c n) -> p c n", c=2) for v in unit(shared))
                    for b in range(blocks):
                        if k == 0:
                            banks[b] = tile_bank()
                        if when and k % 2 == 0:
                            when(b, k // 2)
                        for c in range(2):
                            mm = products(banks[b][:, 0:width], lhs(2 * k + c, b), high[:, c, :], low[:, c, :],
                                          k == 0 and c == 0, k == KC // 2 - 1 and c == 1)
                        if k == KC // 2 - 1 and b < blocks - 1:
                            mm.then_inc(SG[0].tile_full, 1)
                    mm.then_inc(SG[0].unit_done, 1)

            def wide(units, lhs, blocks=TB, shared=False, between={}, when=None):
                banks = None
                for k in range(units):
                    if k in between:
                        between[k]()
                    high, low = unit(shared)
                    if banks is None:
                        banks = [tile_bank() for _ in range(2 * blocks)]
                    for b in range(blocks):
                        if when and k % 4 == 0:
                            when(b, k // 4)
                        for h in range(2):
                            at = slice(h * 512, (h + 1) * 512)
                            mm = products(banks[2 * b + h][:, :], lhs(k, b), high[:, at], low[:, at],
                                          k == 0, k == units - 1)
                            if k == units - 1 and (b, h) != (blocks - 1, 1):
                                mm.then_inc(SG[0].tile_full, 1)
                    mm.then_inc(SG[0].unit_done, 1)

            def turn(sources):
                bank = aux_bank()
                for i, src in enumerate(sources):
                    k, m = src.shape
                    mm = nc.tensor.transpose(bank[0:m, i * k:(i + 1) * k], src, ident[0:k, 0:k])
                mm.then_inc(SG[0].aux_full, 1)

            def turn_all(src, stage=None):
                for b in range(TB):
                    if stage is not None:
                        pe.wait_ge(nat_ready, 2 * stage + b + 1)
                    for h in range(2):
                        turn([src[:, b, (4 * h + i) * P:(4 * h + i + 1) * P] for i in range(4)])

            def block_of(v):
                return lambda c, b: [part[:, c, b * P:(b + 1) * P] for part in v]

            lhs_act = block_of(act_t)

            def arriving():
                n = C.aux.n - 2 * TB
                return lambda b, h: pe.wait_ge(SG[0].aux_evac, n + 2 * b + h + 1)

            def pipelined(n, scores, turned, values):
                scores(0)
                scores(1)
                for u in range(n):
                    turned(u)
                    if u + 2 < n:
                        scores(u + 2)
                    values(u)

            def tables_of_bias():
                pe.wait_ge(consts_loaded, 48)
                pe.wait_ge(filled, FILLS)
                pe.wait_ge(params_loaded, 16 * PARAMS1)
                for rel, heads in ((rel1, HEADS1), (rel2, NSA_H)):
                    nc.tensor.matmul(aux_bank()[0:heads, :], rel[:, :], onehot, start=True,
                                     stop=True).then_inc(S.aux_full, 1)
                bank = aux_bank()
                for b in range(TB):
                    for n in range(N_CMP):
                        at = (b * N_CMP + n) * NSA_H
                        mm = nc.tensor.matmul(bank[:, at:at + NSA_H], onehot_c[:, b, n, :], rel2[:, :],
                                              start=True, stop=True)
                mm.then_inc(S.aux_full, 1)

            pe.wait_ge(x_loaded, 16)
            pe.wait_ge(small_loaded, 16)
            for l in range(DEPTH):
                turn_all(x, None if l == 0 else 2)
                t0 = C.tile.n
                for t, (_, width) in enumerate(TILES1):
                    narrow(width, lhs_act, when=arriving() if t == 0 else None)
                    if l == 0 and t == 0:
                        tables_of_bias()
                turn([gm_ws[:, l, h, :] for h in range(4)])
                wait(pe, S.tile_evac, t0 + 6)
                for t in (1, 2):
                    for b in range(TB):
                        for h in range(2):
                            turn([z[:, t, b, (4 * h + i) * 64:(4 * h + i + 1) * 64] for i in range(4)])
                for b in range(TB):
                    pe.wait_ge(vn_ready, 2 * l + b + 1)
                    bank = aux_bank()
                    for h in range(4):
                        mm = nc.tensor.matmul(bank[:, h * 64:(h + 1) * 64], gm_wt[:, h, :],
                                              z[:, 0, b, 256 + h * 64:256 + (h + 1) * 64],
                                              start=True, stop=True)
                    mm.then_inc(S.aux_full, 1)
                wait(pe, S.tile_evac, t0 + 10)
                for g2 in range(2):
                    bank = aux_bank()
                    for i in range(2):
                        g = 2 * g2 + i
                        for s in range(TB):
                            mm = nc.tensor.matmul(bank[0:64, i * SEQ:(i + 1) * SEQ],
                                                  z[:, 4, s, g * 64:(g + 1) * 64], pool_a[:, s * 4 + g, :],
                                                  start=(s == 0), stop=(s == 1))
                    mm.then_inc(S.aux_full, 1)
                aux_done()
                for b in range(TB):
                    bank = aux_bank()
                    for g in range(4):
                        mm = nc.tensor.matmul(bank[:, g * 64:(g + 1) * 64], poolT[:, g, b * P:(b + 1) * P],
                                              pool_w[:, l, g, :], start=True, stop=True)
                    mm.then_inc(S.aux_full, 1)
                aux_done()
                turned_at = {}

                def scores(u):
                    h, b = divmod(u, TB)
                    nk = (b + 1) * P
                    bank = aux_bank()
                    for m in range(2):
                        mm = nc.tensor.matmul(bank[:, m * SEQ:m * SEQ + nk],
                                              q_t[:, 2 * h + m, b * P:(b + 1) * P],
                                              k_t[:, 2 * h + m, 0:nk], start=True, stop=True)
                    mm.then_inc(S.aux_full, 1)

                def turned(u):
                    pe.wait_ge(attn_ready, l * HEADS1 * TB + u + 1)
                    turn([sc[:, u % 2, 0, k * P:(k + 1) * P] for k in range(u % TB + 1)])
                    turned_at[u] = C.aux.n

                def values(u):
                    h, b = divmod(u, TB)
                    pe.wait_ge(S.aux_evac, turned_at[u])
                    bank = aux_bank()
                    for k in range(b + 1):
                        mm = nc.tensor.matmul(bank[:, 0:P], p_t[:, u % 2, k * P:(k + 1) * P],
                                              z[:, 3, k, h * P:(h + 1) * P], start=(k == 0), stop=(k == b))
                    mm.then_inc(S.aux_full, 1)

                pipelined(HEADS1 * TB, scores, turned, values)
                turn_all(nat, 3 * l)
                wide(KC, lhs_act, when=arriving())
                turn_all(x, 3 * l + 1)
                if l == 0:
                    def turn_hidden(t, width):
                        pe.wait_ge(S.gated, C.gated.take() + 1)
                        for b in range(TB):
                            turn([hs[:, t % 2, b, i * P:(i + 1) * P] for i in range(width // P)])

                    when = arriving()
                    for part in FF_PARTS:
                        for t, (_, width) in enumerate(part):
                            narrow(width, lhs_act, when=when)
                            when = None
                            narrow(width, lhs_act)
                            if t > 0:
                                turn_hidden(t - 1, part[t - 1][1])
                        turn_hidden(t, width)
                        aux_done()
                        wide(sum(width for _, width in part) // P, block_of(hid1_t))
                else:
                    aux_done()
                    for b in range(TB):
                        bank = aux_bank()
                        for c in range(KC):
                            for i, part in enumerate(lhs_act(c, b)):
                                mm = nc.tensor.matmul(bank[:, 0:N_EXP], part.bitcast(F32), router[:, c, :],
                                                      start=(c == 0 and i == 0), stop=(c == KC - 1 and i == 1))
                        mm.then_inc(S.aux_full, 1)
                    pe.wait_ge(route_mask, 1)
                    bank = aux_bank()
                    for to, parts in enumerate([[(before, 0)], [(ones, 0), (before, 1)], [(ones, 0), (ones, 1)]]):
                        for i, (m, b) in enumerate(parts):
                            mm = nc.tensor.matmul(bank[:, to * 8:to * 8 + 8], m[:, :], mask[:, b, :],
                                                  start=(i == 0), stop=(i == len(parts) - 1))
                    mm.then_inc(S.aux_full, 1)

                    def gather():
                        n = C.picked.take()
                        pe.wait_ge(SG[0].picked, C.picked.at(n) + 1)
                        for j in range(4):
                            bank = aux_bank()
                            for i in range(2):
                                for b in range(TB):
                                    mm = nc.tensor.matmul(bank[:, i * P:(i + 1) * P],
                                                          x[:, b, (2 * j + i) * P:(2 * j + i + 1) * P],
                                                          sel[:, b, :], start=(b == 0), stop=(b == TB - 1))
                            mm.then_inc(SG[0].aux_full, 1)

                    def turn_gates():
                        turn([sel_g[:, b, :] for b in range(TB)])

                    def expert(*_):
                        def turn_hidden(t):
                            n = C.gated.take()
                            pe.wait_ge(SG[0].gated, C.gated.at(n) + 1)
                            turn([hs_e[:, t % 2, i * P:(i + 1) * P] for i in range(4)])

                        wait(pe, SG[0].aux_evac, C.aux.at(C.aux.n))
                        for t in range(MOE_TILES):
                            for _ in range(2):
                                narrow(512, lambda c, b: [part[:, c, :] for part in xg_t], 1, True)
                            if t > 0:
                                turn_hidden(t - 1)
                        aux_done()

                        def last():
                            turn_hidden(MOE_TILES - 1)
                            aux_done()

                        wide(D_FFE // P, lambda c, b: [part[:, c, :] for part in hide_t], 1, True,
                             {GATHER_AT: gather, D_FFE // P - 4: last})
                        out_tile = C.tile.n
                        wait(pe, SG[0].tile_evac, C.tile.at(out_tile))
                        for b in range(TB):
                            for h in range(2):
                                nc.tensor.matmul(aux_bank()[:, :], sel_gt[:, b, :], ye[:, h * 512:(h + 1) * 512],
                                                 start=True, stop=True).then_inc(SG[0].aux_full, 1)
                        turn_gates()

                    gather()
                    turn_gates()
                    rolled(pe, C, expert, route_mask, extra)

            C, SG[0] = Counts(), S2
            for l in range(DEPTH):
                turn_all(nat, 6 + 4 * l)
                t0 = C.tile.n
                for t, (_, width) in enumerate(TILES2[0:8]):
                    narrow(width, lhs_act, when=arriving() if t == 0 else None)
                pe.wait_ge(S2.tile_evac, t0 + 16)
                pe.wait_ge(layer_loaded, 16 * PARAMS2 * (l + 1))
                turn([conv_nat[:, c * P:(c + 1) * P] for c in range(4)])
                turn([pe_nat[:, k, :] for k in range(2)])
                for b in range(TB):
                    turn([z[:, 1, b, i * 64:(i + 1) * 64] for i in range(4)])
                    turn([z[:, 1, b, 256 + i * 64:256 + (i + 1) * 64] for i in range(2)]
                         + [z[:, 2, b, i * 64:(i + 1) * 64] for i in range(2)])
                    for h in range(2):
                        turn([z[:, 0, b, (4 * h + i) * 64:(4 * h + i + 1) * 64] for i in range(4)])
                aux_done()
                for k in range(2):
                    bank = aux_bank()
                    for i in range(CMP_BLOCK // 2):
                        last_col = 2 * i + CMP_STRIDE * (N_CMP - 1) + 1
                        mm = nc.tensor.matmul(bank[:, 0:3 * N_CMP], cmp_w1[:, k, i, :],
                                              c_t[:, 3 * k:3 * k + 3, 2 * i:last_col:CMP_STRIDE],
                                              start=(i == 0), stop=(i == CMP_BLOCK // 2 - 1))
                    mm.then_inc(S2.aux_full, 1)
                pe.wait_ge(hidc_ready, 2 * l + 2)
                nc.tensor.matmul(aux_bank()[0:64, 0:2 * N_CMP], cmp_w2[:, 0, :], hidc[:, 0, :], start=True,
                                 stop=True).then_inc(S2.aux_full, 1)
                bank = aux_bank()
                for g in range(NSA_G):
                    mm = nc.tensor.matmul(bank[0:N_CMP, g * 64:(g + 1) * 64],
                                          hidc[:, 1, g * N_CMP:(g + 1) * N_CMP], cmp_w2[:, 1, :],
                                          start=True, stop=True)
                mm.then_inc(S2.aux_full, 1)
                aux_done()
                bank = aux_bank()
                for b in range(TB):
                    for h in range(NSA_H):
                        at = (b * NSA_H + h) * N_CMP
                        mm = nc.tensor.matmul(bank[:, at:at + N_CMP], q_t[:, h, b * P:(b + 1) * P],
                                              kcmp[:, h // 4, :], start=True, stop=True)
                mm.then_inc(S2.aux_full, 1)
                pe.wait_ge(cmp_probs, l + 1)
                for b in range(TB):
                    for h2 in range(2):
                        turn([sc_c[:, b, 4 * h2 + i, :] for i in range(4)])
                    aux_done()
                    bank = aux_bank()
                    for h in range(NSA_H):
                        mm = nc.tensor.matmul(bank[:, h * 64:(h + 1) * 64], pc_t[:, h, :], vcmp[:, h // 4, :],
                                              start=True, stop=True)
                    mm.then_inc(S2.aux_full, 1)

                turned_at = {}

                def scores(u):
                    h, b = divmod(u, TB)
                    nk = (b + 1) * P
                    g = h // 4
                    nc.tensor.matmul(aux_bank()[:, 0:2 * nk].rearrange("p (r k) -> p r k", r=2),
                                     q_t[:, h, b * P:(b + 1) * P], k_t[:, g:g + 3:2, 0:nk],
                                     start=True, stop=True).then_inc(S2.aux_full, 1)

                def turned(u):
                    pe.wait_ge(probs_ready, (DEPTH * HEADS1 + l * NSA_H) * TB + u + 1)
                    turn([sc[:, u % 2, r, k * P:(k + 1) * P] for r in range(2) for k in range(u % TB + 1)])
                    turned_at[u] = C.aux.n

                def values(u):
                    h, b = divmod(u, TB)
                    g = h // 4
                    pe.wait_ge(S2.aux_evac, turned_at[u])
                    bank = aux_bank()
                    for r in range(2):
                        for k in range(b + 1):
                            v = (z[:, 1, k, 384 + g * 64:384 + (g + 1) * 64] if r == 0 else
                                 z[:, 2, k, 128 + g * 64:128 + (g + 1) * 64])
                            at = (r * (b + 1) + k) * P
                            mm = nc.tensor.matmul(bank[:, r * 64:(r + 1) * 64], p_t[:, u % 2, at:at + P], v,
                                                  start=(k == 0), stop=(k == b))
                    mm.then_inc(S2.aux_full, 1)

                pipelined(NSA_H * TB, scores, turned, values)

                pe.wait_ge(rot_ready, l + 1)
                for b in range(TB):
                    for h in range(2):
                        turn([rot[:, b, 4 * h + i, :] for i in range(4)])
                aux_done()
                decayed = {}

                def ret_scores(h):
                    bank = aux_bank()
                    nc.tensor.matmul(bank[:, 0:SEQ], q_t[:, 4 + h, 0:P], q_t[:, h, 0:SEQ], start=True, stop=True)
                    nc.tensor.matmul(bank[:, SEQ:SEQ + P], q_t[:, 4 + h, P:SEQ], q_t[:, h, P:SEQ],
                                     start=True, stop=True).then_inc(S2.aux_full, 1)
                    decayed[h] = C.aux.n

                def ret_values(h):
                    pe.wait_ge(S2.aux_evac, decayed[h])
                    bank = aux_bank()
                    for b, at, k in ((0, 0, 0), (1, P, 0), (1, 2 * P, 1)):
                        mm = nc.tensor.matmul(bank[:, b * P:(b + 1) * P], p_t[:, h % 2, at:at + P],
                                              z[:, 4, k, h * P:(h + 1) * P], start=(k == 0), stop=(k == b))
                    mm.then_inc(S2.aux_full, 1)

                ret_scores(0)
                for h in range(RET_H):
                    if h + 1 < RET_H:
                        ret_scores(h + 1)
                    ret_values(h)
                for b in range(TB):
                    pe.wait_ge(conv_in, 2 * l + b + 1)
                    turn([z[:, 6, b, c * P:(c + 1) * P] for c in range(4)])
                for t in range(8, 14):
                    narrow(512, lhs_act)
                    if t == 8:
                        turn_all(nat, 6 + 4 * l + 1)
                    if t == 12:
                        for b in range(TB):
                            pe.wait_ge(conv_out, l + 1)
                            turn([y_t[:, c, b * P:(b + 1) * P] for c in range(4)])
                for b in range(TB):
                    pe.wait_ge(conv_act, 2 * l + b + 1)
                    turn([nat[:, b, 512 + c * P:512 + (c + 1) * P] for c in range(4)])
                aux_done()
                for r in range(3):
                    wide(4, block_of(br_t[r]))
                turn_all(nat, 6 + 4 * l + 2)
                wide(KC, lhs_act, when=arriving())
                turn_all(nat, 6 + 4 * l + 3)

                def turn_hidden2(t):
                    pe.wait_ge(gated2, C.gated.take() + 1)
                    for b in range(TB):
                        turn([hs[:, t % 2, b, i * P:(i + 1) * P] for i in range(4)])

                when = arriving()
                for part in FF2_PARTS:
                    for t in range(len(part)):
                        narrow(512, lhs_act, when=when)
                        when = None
                        if t > 0:
                            turn_hidden2(t - 1)
                    turn_hidden2(t)
                    aux_done()
                    wide(sum(width for _, width in part) // P, block_of(hid2_t))

        @block.scalar
        def _(act):
            C = Counts()
            SG = [S]

            def load(dst, src, sig_=params_loaded, scattered=False):
                act.dma_start(dst, src, allow_slow_non_contiguous=scattered).then_inc(sig_, 16)

            def ahead(limit):
                while C.split.n < limit:
                    n = C.split.take()
                    cols = STREAM[0][n] if n < len(STREAM[0]) else D
                    value = 16 * (n // UNITS + 1)
                    if C.split.i is not None:
                        value = value + C.split.i * (16 * C.split.per // UNITS)
                    act.wait_ge(SG[0].unit_loaded[n % UNITS], value)
                    wait(act, SG[0].unit_done, C.split.at(n - HIGHS + 1))
                    nc.scalar.activation(highs[n % HIGHS][:, 0:cols], ring[n % UNITS][:, 0:cols],
                                         ACT.Copy).then_inc(SG[0].high_ready, 1)

            def idle():
                ahead(min(C.unit.n + HIGHS, END[0]))

            def used(units):
                C.unit.take(units)
                ahead(min(C.unit.n + HIGHS - 1, END[0]))

            def evac(dst, closes, func=ACT.Copy, width=512, scale=1.0, also=None):
                n = C.tile.take()
                if closes:
                    act.wait_ge(SG[0].unit_done, C.unit.at(C.unit.n))
                else:
                    act.wait_ge(SG[0].tile_full, C.full.at(C.full.take()) + 1)
                if also:
                    also(tiles[n % 4])
                nc.scalar.activation(dst, tiles[n % 4][:, 0:width], func, scale=scale).then_inc(SG[0].tile_evac, 1)

            def evac_tile(dst, func=ACT.Copy, width=512, scale=1.0, also=None):
                used(KC // 2)
                for b in range(TB):
                    evac(dst(b), b == TB - 1, func, width, scale, also and also(b))

            def evac_wide(units, before_block=None):
                used(units)
                for b in range(TB):
                    if before_block:
                        before_block(b)
                    for h in range(2):
                        evac(acc[:, b, h * 512:(h + 1) * 512], (b, h) == (TB - 1, 1))

            def exps(count, base, width):
                for u in range(count):
                    nk = width(u)
                    act.wait_ge(scores_ready, base + u + 1)
                    for m in range(2):
                        e = nc.scalar.activation(sc[:, u % 2, m, 0:nk], sc[:, u % 2, m, 0:nk], ACT.Exp,
                                                 bias=negm[:, u % 2, m:m + 1],
                                                 accum_out=den[:, u % 2, m:m + 1])
                    e.then_inc(probs_ready, 1)

            load(rel1[0:BUCKETS, :], A["rel_bias"])
            load(rel2[0:BUCKETS, :], A["rel_table_2"])
            load(onehot, A["c_onehot"][:, 0:512], consts_loaded)
            load(gbuf[0:BUCKETS + 1, 0:TB * N_CMP * P], A["c_onehot"][:, 512:512 + TB * N_CMP * P], consts_loaded)
            load(zbuf[:, 6 * 1024:8 * 1024], A["c_pool"], consts_loaded)
            for l in range(DEPTH):
                load(gm_ws[:, l, :, :], A["gmlp_ws"][l].rearrange("h t s -> t h s"))
                load(gm_bs[:, l, :], A["gmlp_bs"][l].rearrange("h t -> t h"), scattered=True)
                load(subln[:, l, :], row(A["diff_subln_g"][l], P))
                load(pool_w[:, l, :, :], A["pool_w"][l].rearrange("g c d -> c g d"))
                load(pool_s[:, l, :], row(A["pool_scale"][l], 256))
                for i, name in enumerate(("lam_q1", "lam_k1", "lam_q2", "lam_k2")):
                    load(lamv[:, i, l, :], row(A[name][l], 64))
            load(router[:, :, :], A["router_w"][0].rearrange("(c p) e -> p c e", p=P))

            STREAM, END = [STREAM1], [len(STREAM1)]
            bias_by_stack = ((bias1, 0, HEADS1), (bias2, HEADS1, NSA_H))
            for l in range(DEPTH):
                for t, (_, width) in enumerate(TILES1):
                    evac_tile(lambda b: z[:, t, b, 0:width], ACT.Gelu if t == 0 else ACT.Copy, width,
                              QSCALE if t == 1 else 1.0)
                    if l == 0 and t == 1:
                        act.wait_ge(rows_ready, 1)
                        for i, (_, first, heads) in enumerate(bias_by_stack):
                            load(rows.ap()[first:first + heads],
                                 biasrow[0:heads, i, 0:REACH].unsqueeze(1).broadcast_to([heads, P, REACH]), rows_stored)
                    if l == 0 and t == 3:
                        act.wait_ge(rows_stored, 32)
                        for dst, first, heads in bias_by_stack:
                            load(dst[:, :, :], bass.AP(rows, first * P * REACH + P - 1,
                                                       [[REACH - 1, P], [P * REACH, heads], [1, SEQ]]), bias_loaded)
                idle()
                if l == 0:
                    act.wait_ge(lam_dots, 1)
                    nc.scalar.activation(lam[:, 0:4], lam[:, 4:8], ACT.Exp).then_inc(lam_exp, 1)
                exps(HEADS1 * TB, l * HEADS1 * TB, lambda u: (u % TB + 1) * P)
                evac_wide(KC)
                if l == 0:
                    for part in FF_PARTS:
                        for t, (_, width) in enumerate(part):
                            evac_tile(lambda b: hs[:, t % 2, b, 0:width], ACT.Silu, width)
                            evac_tile(lambda b: hu[:, t % 2, b, 0:width], ACT.Copy, width)
                        evac_wide(sum(width for _, width in part) // P)
                else:
                    act.wait_ge(route_dif, 1)
                    nc.scalar.activation(small[:, 8:10], small[:, 0:2], ACT.Exp).then_inc(route_exp, 1)
                    END[0] += MOE_UNITS

                    def expert(*_):
                        for t in range(MOE_TILES):
                            used(KC // 2)
                            evac(hs_e[:, t % 2, :], True, ACT.Silu)
                            used(KC // 2)
                            evac(hu_e[:, t % 2, :], True)
                        used(D_FFE // P)
                        for h in range(2):
                            evac(ye[:, h * 512:(h + 1) * 512], h == 1)

                    rolled(act, C, expert, route_mask, extra)
            C, SG[0] = Counts(), S2
            STREAM[0], END[0] = STREAM2, len(STREAM2)
            for l in range(DEPTH):
                for t in range(8):
                    if t == 2:
                        evac_tile(lambda b: z[:, t, b, 0:256], ACT.Copy, 256,
                                  also=lambda b: lambda bank: nc.scalar.activation(
                                      gates2[:, b, :], bank[:, 256:280], ACT.Sigmoid))
                    else:
                        evac_tile(lambda b: z[:, t, b, :], {5: ACT.Silu, 7: ACT.Sigmoid}.get(t, ACT.Copy),
                                  scale=QSCALE if t == 0 else 1.0)
                idle()
                for k in range(2):
                    act.wait_ge(hidc_in, 2 * l + k + 1)
                    nc.scalar.activation(hidc[:, k, :], hidp[:, k, 0:2 * N_CMP], ACT.Gelu_apprx_tanh,
                                         bias=hidp[:, k, 2 * N_CMP:2 * N_CMP + 1]).then_inc(hidc_ready, 1)
                act.wait_ge(cmp_scores, l + 1)
                nc.scalar.activation(sc_c[:, :, :, :], sc_c[:, :, :, :], ACT.Exp).then_inc(cmp_exp, 1)
                exps(NSA_H * TB, (DEPTH * HEADS1 + l * NSA_H) * TB, lambda u: (u % TB + 1) * P)
                for t in range(8, 14):
                    r, h = divmod(t - 8, 2)
                    evac_tile(lambda b: sig[r][:, b, h * 512:(h + 1) * 512], ACT.Sigmoid)
                idle()
                for b in range(TB):
                    act.wait_ge(conv_norm, 2 * l + b + 1)
                    nc.scalar.activation(nat[:, b, 512:1024], nat[:, b, 0:512], ACT.Silu).then_inc(conv_act, 1)
                for r in range(3):
                    evac_wide(4, lambda b: wait(act, merged, (2 * l + r - 1) * TB + b + 1 if r else 0))
                evac_wide(KC, lambda b: act.wait_ge(nat_ready, 2 * (6 + 4 * l + 2) + b + 1))
                for part in FF2_PARTS:
                    for t in range(len(part)):
                        evac_tile(lambda b: hs[:, t % 2, b, :], ACT.Relu)
                    evac_wide(sum(width for _, width in part) // P)

        @block.gpsimd
        def _(pool):
            C = Counts()
            SG = [S]
            pows = Tally()

            nc.gpsimd.memset(ones[:, :], 1.0).then_inc(filled, 1)
            nc.gpsimd.memset(half[:, :], -0.5).then_inc(filled, 1)
            nc.gpsimd.memset(rs_in[:, :], 1.0).then_inc(filled, 1)

            def load(dst, src):
                pool.dma_start(dst, src).then_inc(layer_loaded, 16)

            def split(limit, first=0):
                while C.split.n < limit:
                    n = C.split.take()
                    cols = STREAM[0][n] if n < len(STREAM[0]) else D
                    pool.wait_ge(SG[0].high_ready, C.split.at(n) + 1)
                    nc.gpsimd.tensor_tensor(lows[n % UNITS][:, first:cols], ring[n % UNITS][:, first:cols],
                                            highs[n % HIGHS][:, first:cols], ALU.subtract).then_inc(SG[0].low_pool, 1)

            def load_params2(l):
                pool.wait_ge(params_used, l + 1)
                load(decay[:, :, :], A["c_decay"].rearrange("p (h t) -> p h t", h=RET_H))
                load(ret_gn[:, :], row(A["ret_gn_2"][l], 512))
                load(conv_nat[0:CONV_W, :], A["conv_w_2"][l])
                load(conv_nat[CONV_W:CONV_W + 1, :], A["conv_b_2"][l:l + 1, :])
                load(conv_ln[:, 0, :], row(A["conv_ln_g_2"][l], CONV_CH))
                load(conv_ln[:, 1, :], row(A["conv_ln_b_2"][l], CONV_CH))
                for k, kind in enumerate("kv"):
                    load(cmp_w1[:, k, :, :], A[f"cmp_w1_{kind}_2"][l].rearrange("(i a) d f -> (a d) i f", a=2))
                    load(cmp_w2[:, k, :], A[f"cmp_w2_{kind}_2"][l])
                    load(pe_nat[:, k, :], A[f"cmp_pe_{kind}_2"][l])

            def load_gain(norm):
                g, l, b = gains[norm]
                if norm > 0:
                    pool.wait_ge(nat_ready, 2 * NORM_STAGE[norm - 1] + TB)
                pool.dma_start(gain[:, 0, :], row(A[g] if l is None else A[g][l], D)).then_inc(gain_loaded, 16)
                if b is not None:
                    pool.dma_start(gain[:, 1, :], row(A[b][l], D)).then_inc(gain_loaded, 16)

            def power():
                n = pows.take()
                pool.wait_ge(var_ready, n + 1)
                if n == 0:
                    pool.wait_ge(filled, FILLS)
                nc.gpsimd.tensor_tensor(rs_out[:, :], rs_in[:, :], half[:, :], ALU.pow).then_inc(rstd_ready, 1)

            def stage(units, slack=HIGHS):
                C.unit.take(units)
                split(min(C.unit.n + slack, len(STREAM[0])))

            STREAM = [STREAM1]
            load_gain(0)
            for l in range(DEPTH):
                stage(len(IN1), -6)
                power()
                power()
                stage(0)
                power()
                stage(len(OUT1))
                power()
                load_gain(2 * l + 1)
                if l == 0:
                    stage(len(FF1))
                else:
                    rolled(pool, C, lambda *_: split(len(STREAM1) + MOE_UNITS, D - MOE_LOW), route_mask, extra)
                power()
                load_gain(2 * l + 2)
            C, SG[0], STREAM[0] = Counts(), S2, STREAM2
            load_params2(0)
            for l in range(DEPTH):
                power()
                load_gain(5 + 2 * l)
                stage(len(IN2), 4)
                power()
                power()
                stage(len(GATE2), 0)
                power()
                stage(len(BRANCH2) + len(OUT2))
                power()
                load_gain(6 + 2 * l)
                stage(len(FF2))
                if l + 1 < DEPTH:
                    load_params2(l + 1)
            power()

        @block.vector
        def _(dve):
            C = Counts()
            SG = [S]
            asked = Tally()
            V = nc.vector

            def step(ins):
                n = C.own.take()
                ins.then_inc(SG[0].vec, 1)
                dve.wait_ge(SG[0].vec, C.own.at(n) + 1)

            def aux_in():
                n = C.aux.take()
                dve.wait_ge(SG[0].aux_full, C.aux.at(n) + 1)
                return aux[n % 4]

            def evac(ins):
                ins.then_inc(SG[0].aux_evac, 1)

            def read_back():
                dve.wait_ge(SG[0].aux_evac, C.aux.at(C.aux.n))

            def turn_in(dst):
                p, n, m = dst.shape
                bank = aux_in()
                evac(V.tensor_copy(dst, bank[0:p, 0:n * m].rearrange("p (n m) -> p n m", n=n)))

            def parts_in(dst):
                p, n, m = dst[0].shape
                src = aux_in()[0:p, 0:n * m].rearrange("p (n m) -> p n m", n=n)
                step(V.tensor_copy(dst[0], src))
                evac(V.tensor_tensor(dst[1], src, dst[0], ALU.subtract))

            def turn_all_in():
                for b in range(TB):
                    for h in range(2):
                        parts_in([part[:, 4 * h:4 * h + 4, b * P:(b + 1) * P] for part in act_t])

            def split(limit):
                limit = min(limit, len(STREAM1) + MOE_UNITS)
                while C.split.n < limit:
                    n = C.split.take()
                    dve.wait_ge(SG[0].high_ready, C.split.at(n) + 1)
                    V.tensor_tensor(lows[n % UNITS][:, 0:D - MOE_LOW], ring[n % UNITS][:, 0:D - MOE_LOW],
                                    highs[n % HIGHS][:, 0:D - MOE_LOW], ALU.subtract).then_inc(SG[0].low_vec, 1)

            def rstd(groups, value, scale, eps):
                n = asked.take()
                V.tensor_scalar(rs_in[:, 0:groups], value, scale, eps, ALU.mult, ALU.add).then_inc(var_ready, 1)
                dve.wait_ge(rstd_ready, n + 1)

            def moments(src, eps):
                _, groups, width = src.shape
                parts = max(1, width // 512)
                for g in range(groups):
                    for i in range(parts):
                        ins = V.bn_stats(stats[:, g, i, :], src[:, g, i * 512:min(width, (i + 1) * 512)])
                step(ins)
                for g in range(groups):
                    ins = V.bn_aggr(mv[:, g, :], stats[:, g, 0:parts, :].rearrange("p i s -> p (i s)"))
                step(ins)
                rstd(groups, mv[:, 0:groups, 1], 1.0, eps)

            def spread(v, width):
                return v.unsqueeze(2).broadcast_to([P, v.shape[1], width])

            def over(v, n):
                return v.unsqueeze(1).broadcast_to([P, n, v.shape[1]])

            def standardise(dst, src, eps, signal=None):
                _, groups, width = src.shape
                moments(src, eps)
                step(V.tensor_tensor(dst, src, spread(mv[:, 0:groups, 0], width), ALU.subtract))
                ins = V.tensor_tensor(dst, dst, spread(rs_out[:, 0:groups], width), ALU.mult)
                if signal is None:
                    step(ins)
                else:
                    ins.then_inc(signal, 1)

            def gain_in(norm):
                dve.wait_ge(gain_loaded, 16 * sum(1 if g[2] is None else 2 for g in gains[0:norm + 1]))

            def add_products(factor):
                for b in range(TB):
                    C.tile.n += 2
                    dve.wait_ge(SG[0].tile_evac, C.tile.n)
                    step(V.scalar_tensor_tensor(x[:, b, :], x[:, b, :], factor, acc[:, b, :], ALU.mult, ALU.add))

            def layer_norm(norm):
                moments(x[:, :, :], EPS1)
                gain_in(norm)
                for b in range(TB):
                    step(V.tensor_scalar(x[:, b, :], x[:, b, :], mv[:, b, 0:1], rs_out[:, b:b + 1],
                                         ALU.subtract, ALU.mult))
                    step(V.tensor_tensor(x[:, b, :], x[:, b, :], gain[:, 0, :], ALU.mult))
                    V.tensor_tensor(x[:, b, :], x[:, b, :], gain[:, 1, :], ALU.add).then_inc(nat_ready, 1)

            def rms_norm(norm):
                for b in range(TB):
                    ins = V.tensor_tensor_reduce(out=nat[:, b, :], in0=x[:, b, :], in1=x[:, b, :], scale=1.0,
                                                 scalar=0.0, op0=ALU.mult, op1=ALU.add,
                                                 accum_out=mv[:, b, 1:2])
                step(ins)
                rstd(TB, mv[:, 0:TB, 1], 1.0 / D, EPS2)
                gain_in(norm)
                for b in range(TB):
                    V.scalar_tensor_tensor(nat[:, b, :], x[:, b, :], rs_out[:, b:b + 1], gain[:, 0, :],
                                           ALU.mult, ALU.mult).then_inc(nat_ready, 1)

            def score_rows(bank, s, bias, nk, at):
                for m in range(2):
                    ins = V.tensor_tensor_reduce(out=sc[:, s, m, 0:nk], in0=bank[:, at(m):at(m) + nk],
                                                 in1=bias[:, SEQ - nk:SEQ], scale=1.0, scalar=-3e38,
                                                 op0=ALU.add, op1=ALU.max,
                                                 accum_out=small[:, 2 * s + m:2 * s + m + 1])
                evac(ins)
                read_back()
                V.tensor_scalar(negm[:, s, :], small[:, 2 * s:2 * s + 2], -1.0, None, ALU.mult).then_inc(scores_ready, 1)

            def pipelined(n, scores, turned, values):
                scores(0)
                scores(1)
                for u in range(n):
                    turned(u)
                    if u + 2 < n:
                        scores(u + 2)
                    values(u)

            V.memset(rel1[BUCKETS:BUCKETS + 1, :], 1.0).then_inc(filled, 1)
            V.memset(rel2[BUCKETS:BUCKETS + 1, :], 1.0).then_inc(filled, 1)
            dve.wait_ge(small_loaded, 16)
            for l in range(DEPTH):
                turn_all_in()
                t0 = C.tile.n
                C.tile.n += 2 * len(TILES1)
                if l == 0:
                    for i, heads in enumerate((HEADS1, NSA_H)):
                        V.tensor_copy(biasrow[0:heads, i, :], aux_in()[0:heads, :]).then_inc(S.aux_evac, 1)
                    read_back()
                    V.memset(small[:, 64:65], 0.0).then_inc(rows_ready, 1)
                    bank = aux_in()
                    evac(V.tensor_copy(bias_c[:, :, :, :].rearrange("p b n h -> p (b n h)"), bank[:, 0:TB * N_CMP * NSA_H]))
                    dve.wait_ge(params_loaded, 16 * PARAMS1)
                    for n in range(DEPTH):
                        for i in range(2):
                            ins = V.tensor_tensor_reduce(out=small[:, 0:64], in0=lamv[:, 2 * i, n, :],
                                                         in1=lamv[:, 2 * i + 1, n, :], scale=1.0, scalar=0.0,
                                                         op0=ALU.mult, op1=ALU.add,
                                                         accum_out=lam[:, 4 + 2 * n + i:5 + 2 * n + i])
                            if n == DEPTH - 1 and i == 1:
                                ins.then_inc(lam_dots, 1)
                            else:
                                step(ins)
                dve.wait_ge(S.tile_evac, t0 + 2)
                values_ = z[:, 0, :, 256:512]
                for b in range(TB):
                    v = values_[:, b, :].rearrange("p (h d) -> p h d", h=4)
                    standardise(v, v, EPS1, vn_ready)
                bank = aux_in()
                evac(V.tensor_tensor(gm_wt[:, :, :], bank[:, :].rearrange("p (h t) -> p h t", h=4), over(triu, 4),
                                     ALU.mult))
                for dst in (q_t, k_t):
                    for b in range(TB):
                        for h in range(2):
                            turn_in(dst[:, 4 * h:4 * h + 4, b * P:(b + 1) * P])
                for b in range(TB):
                    bank = aux_in()
                    for h in range(4):
                        ins = V.scalar_tensor_tensor(nat[:, b, h * 64:(h + 1) * 64], bank[:, h * 64:(h + 1) * 64],
                                                     gm_bs[:, l, h:h + 1], z[:, 0, b, h * 64:(h + 1) * 64],
                                                     ALU.add, ALU.mult)
                    evac(ins)
                for g2 in range(2):
                    bank = aux_in()
                    evac(V.tensor_copy(poolT[:, 2 * g2:2 * g2 + 2, :],
                                       bank[0:64, :].rearrange("p (i t) -> p i t", i=2)))
                for b in range(TB):
                    bank = aux_in()
                    evac(V.tensor_tensor(nat[:, b, 768:1024], bank[:, 0:256], pool_s[:, l, :], ALU.mult))
                dve.wait_ge(bias_loaded, 32)
                if l == 0:
                    dve.wait_ge(lam_exp, 1)
                    for n in range(DEPTH):
                        step(V.tensor_tensor(lam[:, 2 * n:2 * n + 1], lam[:, 2 * n + 1:2 * n + 2], lam[:, 2 * n:2 * n + 1],
                                             ALU.subtract))
                        step(V.tensor_scalar(lam[:, 2 * n:2 * n + 1], lam[:, 2 * n:2 * n + 1], -lam_init(n), None, ALU.add))

                def scores(u):
                    score_rows(aux_in(), u % 2, bias1[:, u // TB, :], (u % TB + 1) * P, lambda m: m * SEQ)

                def turned(u):
                    s, nk = u % 2, (u % TB + 1) * P
                    dve.wait_ge(probs_ready, l * HEADS1 * TB + u + 1)
                    step(V.reciprocal(coef[:, s, 0:2], den[:, s, :]))
                    step(V.tensor_tensor(coef[:, s, 2:3], coef[:, s, 1:2], lam[:, 2 * l:2 * l + 1], ALU.mult))
                    step(V.tensor_scalar(sc[:, s, 0, 0:nk], sc[:, s, 0, 0:nk], coef[:, s, 0:1], None, ALU.mult))
                    V.scalar_tensor_tensor(sc[:, s, 0, 0:nk], sc[:, s, 1, 0:nk], coef[:, s, 2:3],
                                           sc[:, s, 0, 0:nk], ALU.mult, ALU.add).then_inc(attn_ready, 1)
                    turn_in(p_t[:, s, 0:nk].rearrange("p (k q) -> p k q", q=P))

                def values(u):
                    h, b = divmod(u, TB)
                    evac(V.tensor_copy(nat[:, b, 256 + h * P:256 + (h + 1) * P], aux_in()[:, 0:P]))

                pipelined(HEADS1 * TB, scores, turned, values)
                read_back()
                for b in range(TB):
                    o = nat[:, b, 256:768].rearrange("p (h d) -> p h d", h=HEADS1)
                    for h in range(HEADS1):
                        ins = V.tensor_tensor_reduce(out=sc[:, 0, 0, 0:P], in0=o[:, h, :], in1=o[:, h, :],
                                                     scale=1.0, scalar=0.0, op0=ALU.mult, op1=ALU.add,
                                                     accum_out=mv[:, b * HEADS1 + h, 1:2])
                        step(ins)
                rstd(TB * HEADS1, mv[:, 0:TB * HEADS1, 1], 1.0 / P, EPS1)
                for b in range(TB):
                    for h in range(HEADS1):
                        g = b * HEADS1 + h
                        o = nat[:, b, 256 + h * P:256 + (h + 1) * P]
                        ins = V.scalar_tensor_tensor(o, o, rs_out[:, g:g + 1], subln[:, l, :], ALU.mult, ALU.mult)
                    step(ins)
                    o = nat[:, b, 256:768]
                    V.tensor_scalar(o, o, 1.0 - lam_init(l), None, ALU.mult).then_inc(nat_ready, 1)
                turn_all_in()
                add_products(ALPHA)
                layer_norm(2 * l)
                turn_all_in()
                if l == 0:
                    def hidden_in(t, width):
                        for b in range(TB):
                            parts_in([part[:, 4 * t:4 * t + width // P, b * P:(b + 1) * P] for part in hid1_t])

                    for i, part in enumerate(FF_PARTS):
                        for t, (_, width) in enumerate(part):
                            C.tile.n += 4
                            dve.wait_ge(S.tile_evac, C.tile.n)
                            g = hs[:, t % 2, :, 0:width]
                            V.tensor_tensor(g, g, hu[:, t % 2, :, 0:width], ALU.mult).then_inc(S.gated, 1)
                            C.gated.n += 1
                            if t > 0:
                                hidden_in(t - 1, part[t - 1][1])
                        hidden_in(t, width)
                        add_products(1.0 if i else ALPHA)
                    layer_norm(1)
            for b in range(TB):
                evac(V.tensor_copy(logits[:, b, :], aux_in()[:, 0:N_EXP]))
            read_back()
            for b in range(TB):
                ins = V.max(top[:, b, :], logits[:, b, :])
            step(ins)
            for b in range(TB):
                ins = V.max_index(topi[:, b, :], top[:, b, :], logits[:, b, :])
            step(ins)
            step(V.tensor_copy(topf[:, :, :], topi[:, :, :]))
            V.tensor_tensor(small[:, 0:2], top[:, :, 1], top[:, :, 0], ALU.subtract).then_inc(route_dif, 1)
            dve.wait_ge(route_exp, 1)
            step(V.tensor_scalar(small[:, 10:12], small[:, 8:10], 1.0, None, ALU.add))
            step(V.reciprocal(small[:, 12:14], small[:, 10:12]))
            step(V.tensor_tensor(small[:, 14:16], small[:, 8:10], small[:, 12:14], ALU.mult))
            step(V.memset(gates[:, :, :], 0.0))
            step(V.memset(rank[:, :, :], -1000.0))
            for b in range(TB):
                for i in range(2):
                    V.tensor_scalar(pick[:, b, i, :], iota[:, 0:8], topf[:, b, i:i + 1],
                                    small[:, 12 + 2 * i + b:13 + 2 * i + b], ALU.is_equal, ALU.mult)
                    step(V.tensor_scalar(pick[:, b, 2, :] if i else mask[:, b, :], iota[:, 0:8],
                                         topf[:, b, i:i + 1], None, ALU.is_equal))
                step(V.tensor_tensor(gates[:, b, 0:8], pick[:, b, 0, :], pick[:, b, 1, :], ALU.add))
                ins = V.tensor_tensor(mask[:, b, :], mask[:, b, :], pick[:, b, 2, :], ALU.add)
                if b == TB - 1:
                    ins.then_inc(route_mask, 1)
                    dve.wait_ge(route_mask, 1)
                else:
                    step(ins)
            bank = aux_in()
            for b in range(TB):
                ins = V.scalar_tensor_tensor(rank[:, b, 0:8], bank[:, b * 8:b * 8 + 8], 1000.0, mask[:, b, :],
                                             ALU.add, ALU.mult)
            step(ins)
            over_cap, place, mine, junk, seen = (excess[:, k, :] for k in range(5))
            evac(V.tensor_scalar(over_cap, bank[:, 16:24], float(CAP), None, ALU.is_gt))
            read_back()
            step(V.tensor_scalar(rank[:, :, 0:8], rank[:, :, 0:8], -1000.0, None, ALU.add))

            def find_extra():
                step(V.memset(place, 0.0))
                for i in range(1, N_EXP):
                    step(V.tensor_tensor(place[:, i:i + 1], place[:, i - 1:i], over_cap[:, i - 1:i], ALU.add))
                for j in range(EXTRA):
                    step(V.scalar_tensor_tensor(mine, place, float(j), over_cap, ALU.is_equal, ALU.mult))
                    step(V.tensor_reduce(seen[:, 0:1], mine, AX.X, ALU.add))
                    for b in range(TB):
                        for src, dst in ((rank, rank), (gates, gates)):
                            step(V.tensor_tensor(junk, mine, src[:, b, 0:8], ALU.mult))
                            step(V.tensor_reduce(dst[:, b, N_EXP + j:N_EXP + j + 1], junk, AX.X, ALU.add))
                        at = rank[:, b, N_EXP + j:N_EXP + j + 1]
                        step(V.scalar_tensor_tensor(at, seen[:, 0:1], 1000.0, at, ALU.mult, ALU.add))
                        step(V.tensor_scalar(at, at, -1000.0 - CAP, None, ALU.add))
                    step(V.tensor_copy(extra[:, j:j + 1], seen[:, 0:1]))
                    step(V.tensor_tensor(junk, mine, iota[:, 0:8], ALU.mult))
                    step(V.tensor_reduce(seen[:, 1:2], junk, AX.X, ALU.add))
                    ins = V.tensor_copy(extra[:, EXTRA + j:EXTRA + j + 1], seen[:, 1:2])
                    if j == EXTRA - 1:
                        ins.then_inc(route_mask, 1)
                        dve.wait_ge(route_mask, 2)
                    else:
                        step(ins)

            step(V.memset(acc[:, :, :], 0.0))

            def choose(e):
                col = (lambda v, b: v[:, b, e:e + 1]) if isinstance(e, int) else (
                    lambda v, b: v[:, b, bass.ds(e, 1)])
                for b in range(TB):
                    V.tensor_scalar(sel[:, b, :], iota, col(rank, b), None, ALU.is_equal)
                    ins = V.tensor_scalar(sel_g[:, b, :], iota, col(rank, b), col(gates, b), ALU.is_equal, ALU.mult)
                ins.then_inc(SG[0].picked, 1)

            def gathered():
                for j in range(4):
                    parts_in([part[:, 2 * j:2 * j + 2, :] for part in xg_t])

            def gates_in():
                turn_in(sel_gt)

            def expert(e, _):
                start, lead = C.split.n, HIGHS - 1

                def hidden_in(t):
                    parts_in([part[:, 4 * t:4 * t + 4, :] for part in hide_t])

                for t in range(MOE_TILES):
                    split(start + (t + 1) * KC + lead)
                    n = C.tile.take(2)
                    dve.wait_ge(SG[0].tile_evac, C.tile.at(n) + 2)
                    V.tensor_tensor(hs_e[:, t % 2, :], hs_e[:, t % 2, :], hu_e[:, t % 2, :],
                                    ALU.mult).then_inc(SG[0].gated, 1)
                    C.gated.n += 1
                    if t > 0:
                        hidden_in(t - 1)
                C.tile.take(2)
                C.picked.take()
                choose(e + 1)
                second = start + MOE_TILES * KC
                split(second + GATHER_AT + lead)
                gathered()
                split(second + D_FFE // P - 4 + lead)
                hidden_in(MOE_TILES - 1)
                split(start + MOE_UNITS)
                for b in range(TB):
                    for h in range(2):
                        y = acc[:, b, h * 512:(h + 1) * 512]
                        evac(V.tensor_tensor(y, y, aux_in()[:, :], ALU.add))
                read_back()
                gates_in()

            choose(0)
            C.picked.n += 1
            find_extra()
            gathered()
            gates_in()
            C.split.n = len(STREAM1)
            rolled(dve, C, expert, route_mask, extra)
            V.memset(small[:, 21:22], 0.0).then_inc(params_used, 1)
            C, SG[0] = Counts(), S2
            for b in range(TB):
                step(V.scalar_tensor_tensor(x[:, b, :], x[:, b, :], ALPHA, acc[:, b, :], ALU.mult, ALU.add))
            layer_norm(3)

            for l in range(DEPTH):
                if l == 0:
                    dve.wait_ge(nat_ready, TB * (NORM_STAGE[3] + 1))
                rms_norm(4 + 2 * l)
                turn_all_in()
                C.tile.n += 16
                dve.wait_ge(S2.tile_evac, C.tile.n)
                dve.wait_ge(layer_loaded, 16 * PARAMS2 * (l + 1))
                turn_in(taps[:, :, :])
                step(V.memset(cbuf[:, :], 0.0))
                bank = aux_in()
                for k in range(2):
                    V.tensor_copy(c_t[0:64, 3 * k + 2, 0:CMP_BLOCK], bank[0:64, k * 32:(k + 1) * 32])
                    ins = V.tensor_copy(c_t[64:128, 3 * k + 2, 0:CMP_BLOCK - 1],
                                        bank[0:64, k * 32 + 1:(k + 1) * 32])
                evac(ins)
                for b in range(TB):
                    bank = aux_in()
                    src = bank[0:64, :].rearrange("p (k g t) -> p k g t", k=2, g=2)
                    lo = 1 if b == 0 else 0
                    for k in range(2):
                        V.tensor_copy(c_t[0:64, 3 * k:3 * k + 2, b * P:(b + 1) * P], src[:, k, :, :])
                        ins = V.tensor_copy(c_t[64:128, 3 * k:3 * k + 2, b * P - 1 + lo:(b + 1) * P - 1],
                                            src[:, k, :, lo:P])
                    evac(ins)
                    turn_in(k_t[:, 0:4, b * P:(b + 1) * P])
                    for h in range(2):
                        turn_in(q_t[:, 4 * h:4 * h + 4, b * P:(b + 1) * P])
                for k in range(2):
                    bank = aux_in()
                    evac(V.tensor_copy(hidp[:, k, :], bank[:, 0:45]))
                    read_back()
                    V.memset(small[:, 22:23], 0.0).then_inc(hidc_in, 1)
                bank = aux_in()
                evac(V.tensor_copy(kcmp[:, :, :], bank[0:64, 0:2 * N_CMP].rearrange("p (g n) -> p g n", g=2)))
                bank = aux_in()
                evac(V.tensor_copy(vcmp[:, :, :], bank[0:N_CMP, 0:128].rearrange("p (g d) -> p g d", g=2)))
                bank = aux_in()
                for b in range(TB):
                    n = NSA_H * N_CMP
                    ins = V.tensor_tensor(sc_c[:, b, :, :],
                                          bank[:, b * n:(b + 1) * n].rearrange("p (h n) -> p h n", h=NSA_H),
                                          bias_c[:, b, :, :].rearrange("p n h -> p h n"), ALU.add)
                evac(ins)
                read_back()
                s2 = sc_c[:, :, :, :].rearrange("p b h n -> p (b h) n")
                step(V.tensor_reduce(small[:, 0:16], s2, AX.X, ALU.max))
                step(V.tensor_scalar(small[:, 0:16], small[:, 0:16], -1e29, None, ALU.max))
                V.tensor_tensor(s2, s2, spread(small[:, 0:16], N_CMP), ALU.subtract).then_inc(cmp_scores, 1)
                dve.wait_ge(cmp_exp, l + 1)
                step(V.tensor_reduce(small[:, 0:16], s2, AX.X, ALU.add))
                step(V.tensor_scalar(small[:, 0:16], small[:, 0:16], 1e-30, None, ALU.max))
                step(V.reciprocal(small[:, 16:32], small[:, 0:16]))
                step(V.tensor_tensor(small[:, 0:16].rearrange("p (b h) -> p b h", b=TB),
                                     small[:, 16:32].rearrange("p (b h) -> p b h", b=TB),
                                     gates2[:, :, 0:24:3], ALU.mult))
                V.tensor_tensor(s2, s2, spread(small[:, 0:16], N_CMP), ALU.mult).then_inc(cmp_probs, 1)
                for b in range(TB):
                    for h2 in range(2):
                        turn_in(pc_t[:, 4 * h2:4 * h2 + 4, :])
                    evac(V.tensor_copy(o_cmp[:, b, :], aux_in()[:, :]))

                def scores(u):
                    nk = (u % TB + 1) * P
                    score_rows(aux_in(), u % 2, bias2[:, u // TB, :], nk, lambda m: m * nk)

                def turned(u):
                    h, b = divmod(u, TB)
                    s, nk = u % 2, (b + 1) * P
                    dve.wait_ge(probs_ready, (DEPTH * HEADS1 + l * NSA_H) * TB + u + 1)
                    step(V.reciprocal(coef[:, s, 0:2], den[:, s, :]))
                    step(V.tensor_tensor(coef[:, s, 2:4], coef[:, s, 0:2], gates2[:, b, 3 * h + 1:3 * h + 3], ALU.mult))
                    turn_in(p_t[:, s, 0:2 * nk].rearrange("p (k q) -> p k q", q=P))

                def values(u):
                    h, b = divmod(u, TB)
                    s = u % 2
                    bank = aux_in()
                    o = nat[:, b, h * 64:(h + 1) * 64]
                    step(V.scalar_tensor_tensor(o, bank[:, 0:64], coef[:, s, 2:3], o_cmp[:, b, h * 64:(h + 1) * 64],
                                                ALU.mult, ALU.add))
                    evac(V.scalar_tensor_tensor(o, bank[:, 64:128], coef[:, s, 3:4], o, ALU.mult, ALU.add))

                pipelined(NSA_H * TB, scores, turned, values)

                t1 = sc[:, 0, 0, :].rearrange("p (h d) -> p h d", h=8)
                t2 = sc[:, 1, 0, :].rearrange("p (h d) -> p h d", h=8)
                for b in range(TB):
                    qk = z[:, 3, b, :].rearrange("p (h d) -> p h d", h=8)
                    lo, hi = qk[:, :, 0:32], qk[:, :, 32:64]
                    cos, sin = over(rope_cos[:, b, :], 8), over(rope_sin[:, b, :], 8)
                    V.tensor_tensor(t1, hi, sin, ALU.mult)
                    V.tensor_tensor(t2, lo, sin, ALU.mult)
                    V.tensor_tensor(rot[:, b, :, 0:32], lo, cos, ALU.mult)
                    step(V.tensor_tensor(rot[:, b, :, 32:64], hi, cos, ALU.mult))
                    V.tensor_tensor(rot[:, b, :, 0:32], rot[:, b, :, 0:32], t1, ALU.subtract)
                    ins = V.tensor_tensor(rot[:, b, :, 32:64], rot[:, b, :, 32:64], t2, ALU.add)
                    if b == TB - 1:
                        ins.then_inc(rot_ready, 1)
                    else:
                        step(ins)
                for b in range(TB):
                    for h in range(2):
                        turn_in(q_t[:, 4 * h:4 * h + 4, b * P:(b + 1) * P])

                def ret_scores(h):
                    bank = aux_in()
                    evac(V.tensor_tensor(p_t[:, h % 2, 0:3 * P], bank[:, 0:3 * P], decay[:, h, :], ALU.mult))

                def ret_values(h):
                    bank = aux_in()
                    evac(V.tensor_copy(nat[:, :, 512 + h * P:512 + (h + 1) * P],
                                       bank[:, 0:2 * P].rearrange("p (b d) -> p b d", b=TB)))

                ret_scores(0)
                for h in range(RET_H):
                    if h + 1 < RET_H:
                        ret_scores(h + 1)
                    ret_values(h)
                for b in range(TB):
                    V.tensor_tensor(z[:, 6, b, :], z[:, 6, b, :], z[:, 7, b, :], ALU.mult).then_inc(conv_in, 1)
                step(V.memset(u_t[:, :, 0:PAD], 0.0))
                for b in range(TB):
                    turn_in(u_t[:, :, PAD + b * P:PAD + (b + 1) * P])
                for b in range(TB):
                    o = nat[:, b, 512:1024].rearrange("p (h d) -> p h d", h=RET_H)
                    standardise(o, o, EPS2)
                    o = nat[:, b, 512:1024]
                    step(V.tensor_tensor(o, o, ret_gn[:, :], ALU.mult))
                    V.tensor_tensor(o, o, z[:, 5, b, :], ALU.mult).then_inc(nat_ready, 1)
                for b in range(TB):
                    for r in range(2):
                        parts_in([part[:, :, b * P:(b + 1) * P] for part in br_t[r]])
                read_back()
                for j in range(CONV_W):
                    for c in range(4):
                        if j == 0:
                            C.own.n += 1
                            V.tensor_scalar(y_t[:, c, :], u_t[:, c, j:j + SEQ], taps[:, c, j:j + 1],
                                            taps[:, c, CONV_W:CONV_W + 1], ALU.mult, ALU.add).then_inc(S2.vec, 1)
                            continue
                        dve.wait_ge(S2.vec, C.own.n - 3)
                        ins = V.scalar_tensor_tensor(y_t[:, c, :], u_t[:, c, j:j + SEQ], taps[:, c, j:j + 1],
                                                     y_t[:, c, :], ALU.mult, ALU.add)
                        if j == CONV_W - 1 and c == 3:
                            ins.then_inc(conv_out, 1)
                        else:
                            C.own.n += 1
                            ins.then_inc(S2.vec, 1)
                for b in range(TB):
                    turn_in(nat[:, b, 0:512].rearrange("p (c d) -> p c d", c=4))
                read_back()
                standardise(nat[:, :, 0:512], nat[:, :, 0:512], EPS2)
                for b in range(TB):
                    o = nat[:, b, 0:512]
                    step(V.tensor_tensor(o, o, conv_ln[:, 0, :], ALU.mult))
                    V.tensor_tensor(o, o, conv_ln[:, 1, :], ALU.add).then_inc(conv_norm, 1)
                for b in range(TB):
                    parts_in([part[:, :, b * P:(b + 1) * P] for part in br_t[2]])
                C.tile.n += 12
                for r in range(3):
                    for b in range(TB):
                        C.tile.n += 2
                        dve.wait_ge(S2.tile_evac, C.tile.n)
                        if r == 0:
                            V.tensor_tensor(nat[:, b, :], sig[0][:, b, :], acc[:, b, :], ALU.mult).then_inc(merged, 1)
                            continue
                        g = sig[r][:, b, :]
                        ins = V.tensor_tensor(g, g, acc[:, b, :], ALU.mult)
                        if r == 1:
                            ins.then_inc(merged, 1)
                            dve.wait_ge(merged, (2 * l + 1) * TB + b + 1)
                            step(V.tensor_tensor(nat[:, b, :], nat[:, b, :], g, ALU.add))
                        else:
                            step(ins)
                            V.tensor_tensor(nat[:, b, :], nat[:, b, :], g, ALU.add).then_inc(nat_ready, 1)
                turn_all_in()
                add_products(1.0)
                rms_norm(5 + 2 * l)
                turn_all_in()

                def hidden_in(t):
                    for b in range(TB):
                        parts_in([part[:, 4 * t:4 * t + 4, b * P:(b + 1) * P] for part in hid2_t])

                for i, part in enumerate(FF2_PARTS):
                    for t in range(len(part)):
                        C.tile.n += 2
                        dve.wait_ge(S2.tile_evac, C.tile.n)
                        g = hs[:, t % 2, :, :]
                        V.tensor_tensor(g, g, g, ALU.mult).then_inc(gated2, 1)
                        if t > 0:
                            hidden_in(t - 1)
                    hidden_in(t)
                    if i == len(FF2_PARTS) - 1:
                        read_back()
                        V.memset(small[:, 21:22], 0.0).then_inc(params_used, 1)
                    add_products(1.0)
            rms_norm(8)


def buckets(dist):
    n = np.maximum(dist, 0)
    exact = BUCKETS // 2
    far = np.maximum(n, 1).astype(np.float32)
    large = exact + (np.log(far / np.float32(exact)) / np.float32(math.log(MAX_DIST / exact))
                     * np.float32(BUCKETS - exact)).astype(np.int32)
    return np.where(n < exact, n, np.minimum(large, BUCKETS - 1))


def one_hot_buckets(dist):
    rows = (np.arange(BUCKETS).reshape(-1, *[1] * dist.ndim) == buckets(dist)) & (dist >= 0)
    return np.concatenate([rows.astype(np.float32), np.where(dist < 0, NEG, 0.0).astype(np.float32)[None]])


def tables():
    i = np.arange(P)
    half = RET_DK // 2
    inv = 10000.0 ** (-np.arange(half, dtype=np.float32) / np.float32(half))
    ang = (np.arange(SEQ, dtype=np.float32)[:, None] * inv[None, :].astype(np.float32)).astype(np.float32)
    trig = [f(ang.astype(np.float64)).reshape(TB, P, half).transpose(1, 0, 2).reshape(P, TB * half)
            for f in (np.cos, np.sin)]
    small = np.concatenate([np.eye(P), i[:, None] <= i[None, :], i[:, None] < i[None, :],
                            np.broadcast_to(i, (P, P)), *trig], axis=1)
    rows = one_hot_buckets(SEQ - 1 - np.arange(512))
    block_end = CMP_STRIDE * np.arange(N_CMP) + CMP_BLOCK - 1
    dist_c = np.arange(SEQ).reshape(TB, 1, P) - block_end.reshape(1, N_CMP, 1)
    onehot = np.concatenate([rows, one_hot_buckets(dist_c).reshape(BUCKETS + 1, -1)], axis=1)
    t = np.arange(SEQ)
    pool = []
    for w in WINDOWS:
        inside = (t[:, None] <= t[None, :]) & (t[:, None] > t[None, :] - w)
        pool.append(inside / np.minimum(t + 1, w)[None, :] - np.eye(SEQ))
    pool = np.stack(pool).reshape(4, TB, P, SEQ).transpose(2, 1, 0, 3).reshape(P, -1)
    log_g = np.log1p(-np.exp2(-5.0 - np.arange(RET_H)))
    diff = t[None, :] - i[:, None]
    decay = np.where(diff >= 0, np.exp(log_g[:, None, None] * np.maximum(diff, 0)), 0.0) * RET_DK ** -0.5
    decay = np.concatenate([decay, decay[:, :, 0:P]], axis=2).transpose(1, 0, 2).reshape(P, -1)
    named = {"c_small": small, "c_onehot": onehot, "c_pool": pool, "c_decay": decay}
    return {n: np.ascontiguousarray(v, dtype=np.float32) for n, v in named.items()}


def kernel(**inputs):
    import concourse.bacc as bacc
    from concourse.bass_utils import run_bass_kernel_spmd

    nc = bacc.Bacc("TRN2", target_bir_lowering=False, num_devices=1)
    arrays, aps = {}, {}
    for name, a in {**inputs, **tables()}.items():
        a = np.ascontiguousarray(a)
        arrays[f"in_{name}"] = a
        aps[name] = nc.dram_tensor(f"in_{name}", a.shape, mybir.dt.from_np(a.dtype), kind="ExternalInput").ap()
    out = nc.dram_tensor("out_x", (1, SEQ, D), F32, kind="ExternalOutput").ap()
    build(nc, aps, out)
    r = run_bass_kernel_spmd(nc, [arrays], core_ids=[0])
    return r.results[0]["out_x"]
```

```python
import math

import numpy as np

import concourse.bass as bass
from concourse import mybir
from contextlib import ExitStack

F32 = mybir.dt.float32
F32R = mybir.dt.float32r
I32 = mybir.dt.int32
U32 = mybir.dt.uint32
ALU = mybir.AluOpType
ACT = mybir.ActivationFunctionType
AX = mybir.AxisListType

P = 128
SEQ, D = 256, 1024
TB = SEQ // P
KC = D // P
DEPTH = 2
HEADS1, DH1 = 4, 64
D_FF, N_EXP, D_FFE = 2816, 8, 3584
NSA_H, NSA_G, DH2 = 8, 2, 64
RET_H, RET_DK, RET_DV = 4, 64, 128
CONV_CH, CONV_W = 512, 31
CMP_BLOCK, CMP_STRIDE = 32, 16
N_CMP = SEQ // CMP_STRIDE - CMP_BLOCK // CMP_STRIDE + 1
D_FF2 = 4096
BUCKETS, MAX_DIST = 32, 128
WINDOWS = (2, 4, 8, 16)
ALPHA = (2 * DEPTH) ** 0.25
EPS1, EPS2 = 1e-5, 1e-6
QSCALE = DH1 ** -0.5
NEG = -1e30
UNITS = 7
HIGHS = 4
EXPERT_UNITS, EXPERT_HIGHS = 14, 6
MOE_LOW = 576
REACH = SEQ + P
CAP = P
EXTRA = 2 * SEQ // (CAP + 1)
ROUNDS = N_EXP + EXTRA
assert SEQ <= 2 * CAP

TILES1 = [(0, 512), (512, 512), (1024, 512), (1536, 512), (2048, 256)]
TILES2 = [(0, 512), (512, 512), (1024, 280), (1304, 512), (1816, 512), (2328, 512), (2840, 512),
          (3352, 512)] + [(3864 + 512 * i, 512) for i in range(6)]
FF_PARTS = [[(c, min(512, D_FF - c)) for c in range(a, min(a + 1536, D_FF), 512)] for a in (0, 1536)]
FF2_PARTS = [[(c, 512) for c in range(a, a + 2048, 512)] for a in (0, 2048)]
MOE_TILES = D_FFE // 512


def lam_init(layer):
    return 0.8 - 0.6 * math.exp(-0.3 * layer)


def narrow_units(tiles):
    return [2 * width for _, width in tiles for _ in range(KC // 2)]


def wide_units(rows):
    return [D] * (rows // P)


def part_units(parts, matrices):
    return sum([narrow_units([t for t in part for _ in range(matrices)])
                + wide_units(sum(width for _, width in part)) for part in parts], [])


ORDER1, ORDER2 = [1, 2, 3, 0, 4], [0, 1, 2, 6, 7, 3, 4, 5] + list(range(8, 14))
EARLY = 3
NORM_AT, MIX_AT, POOL_AT = (0, 1), (2, 3), (5, 6)
TURN1, STEPS1 = [1, 1, 1, 1], [1, 1, 1, 1, 0, 0, 0, 0]
TURN2, STEPS2 = [1, 1, 1, 2, 3, 1, 1, 2, 1, 1], [1] * 16
TAPS_TURN, TAPS_STEPS = [2, 2, 2], [1, 1] * 8
TAPS_VEC = sum(TAPS_TURN) + sum(TAPS_STEPS)
TAPS_POOL = CONV_W - TAPS_VEC
AFTER2 = [4, 2, 0, 0, 0, 0]
IN1, OUT1, FF1 = narrow_units([TILES1[t] for t in ORDER1]), wide_units(D), part_units(FF_PARTS, 2)
IN2 = narrow_units([TILES2[t] for t in ORDER2])
BEFORE_RET = EARLY * KC // 2 + sum(TURN2) + sum(STEPS2) + sum(AFTER2)
BRANCH2, OUT2, FF2 = 3 * wide_units(512), wide_units(D), part_units(FF2_PARTS, 1)
STREAM1 = IN1 + OUT1 + FF1 + IN1 + OUT1
STREAM2 = DEPTH * (IN2 + BRANCH2 + OUT2 + FF2)


class Tally:

    def __init__(self):
        self.n, self.i, self.per = 0, None, 0

    def at(self, n):
        return n if self.i is None else n + self.i * self.per

    def take(self, k=1):
        self.n += k
        return self.n - k


class Signals:

    def __init__(self, sem, suffix=""):
        self.unit_loaded = [sem(f"unit_loaded{i}{suffix}") for i in range(UNITS)]
        self.high_ready = sem("high_ready" + suffix)
        self.low_pool = sem("low_pool" + suffix)
        self.low_vec = sem("low_vec" + suffix)
        self.unit_done = sem("unit_done" + suffix)
        self.tile_full = sem("tile_full" + suffix)
        self.tile_evac = sem("tile_evac" + suffix)
        self.aux_full = sem("aux_full" + suffix)
        self.aux_evac = sem("aux_evac" + suffix)
        self.vec = sem("vec" + suffix)
        self.gated = sem("gated" + suffix)
        self.picked = sem("picked" + suffix)


class Counts:

    def __init__(self):
        self.unit, self.split, self.tile, self.full = Tally(), Tally(), Tally(), Tally()
        self.aux, self.gated, self.picked, self.low, self.own = (Tally() for _ in range(5))

    def all(self):
        return [self.unit, self.split, self.tile, self.full, self.aux, self.gated, self.picked, self.low,
                self.own]


PARAMS1, PARAMS2, TABLES2, FILLS = 1 + 9 * DEPTH, 8, 4, 5
NORM_STAGE = [1, 2, 4, 5, 6, 9, 10, 13, 14]
GAIN_ROW, GAIN_AFTER = [0, 0, 0, 0, 2, 0, 1, 2, 0], [None, 0, 1, 2, None, 3, 3, 4, 5]

GATHER_AT = 4
MOE_UNITS = (2 * MOE_TILES * KC) // 2 + D_FFE // P
assert MOE_UNITS % EXPERT_UNITS == 0 and MOE_UNITS % EXPERT_HIGHS == 0
MOE_PER = (MOE_UNITS, MOE_UNITS, MOE_TILES * 2 + 2, 1, 16, MOE_TILES, 1, MOE_UNITS, MOE_TILES + 4)


def rolled(eng, C, body, routed, extra, lead=0, once=None):
    begun = [t.n for t in C.all()]

    def turn(e, expert, last):
        rolls = not isinstance(e, int)
        for t, n, per in zip(C.all(), begun, MOE_PER):
            t.n, t.i, t.per = (n, e, per) if rolls else (n + e * per, None, per)
        before = [t.n for t in C.all()]
        body(e, expert, last)
        for t, n, per in zip(C.all(), before, MOE_PER):
            assert t.n - n in (0, per, per - lead), (t.n - n, per)

    with eng.Fori(0, N_EXP - 1) as e:
        turn(e, e, False)
    if once:
        work, steps = once
        at = C.all().index(C.own)
        C.own.n, C.own.i = begun[at] + (N_EXP - 1) * MOE_PER[at], None
        before = C.own.n
        work()
        assert C.own.n - before == steps
        begun[at] += steps
    turn(N_EXP - 1, N_EXP - 1, True)
    eng.wait_ge(routed, 2)
    begun[C.all().index(C.split)] -= lead
    with eng.Fori(N_EXP, ROUNDS) as e:
        active = eng.value_load(extra[0:1, bass.ds(e - N_EXP, 1)], min_val=0, max_val=1)
        with eng.If(active):
            turn(e, eng.value_load(extra[0:1, bass.ds(e - N_EXP + EXTRA, 1)], min_val=0, max_val=N_EXP - 1), True)


def wait(eng, sem, value):
    if not isinstance(value, int) or value > 0:
        eng.wait_ge(sem, value)


def build(nc, A, out):
    ctx = ExitStack()
    with ctx:
        def sb(name, shape, dt=F32, where=ctx):
            return where.enter_context(nc.sbuf_tensor(name, shape, dt))

        def shared(name, shape, where=ctx):
            with ExitStack() as first:
                plain = sb(name, shape, F32, first)
            return plain, sb(name + "_parts", shape, F32R, where)

        def sem(name):
            return ctx.enter_context(nc.semaphore(name))

        ring, lows = zip(*(shared(f"unit{i}", [P, 1024]) for i in range(UNITS)))
        highs = [sb(f"high{i}", [P, 1024], F32R) for i in range(HIGHS)]
        x = sb("x_sb", [P, TB, D])
        nat, nat_parts = shared("nat", [P, TB, D])
        acts = sb("acts", [P, 2, KC, SEQ], F32R)
        act_t = [acts[:, i, :, :] for i in range(2)]
        acc = sb("acc", [P, TB, D])
        zbuf, zparts = shared("zbuf", [P, 8192])
        z = zbuf[:, :].rearrange("p (t b n) -> p t b n", t=8, b=TB)

        def hidden_parts(chunks):
            return [zparts[:, i * chunks * SEQ:(i + 1) * chunks * SEQ].rearrange("p (c t) -> p c t", t=SEQ)
                    for i in range(2)]

        hid1_t, hid2_t = hidden_parts(12), hidden_parts(16)
        gbuf, gparts = shared("gbuf", [P, 4096])
        hs = gbuf[:, 0:2048].rearrange("p (i b n) -> p i b n", i=2, b=TB)
        hu = gbuf[:, 2048:4096].rearrange("p (i b n) -> p i b n", i=2, b=TB)
        br_high = gparts[:, 0:3072].rearrange("p (r c t) -> p r c t", r=3, c=4)
        br_low = [zparts[:, t * 1024:(t + 1) * 1024].rearrange("p (c t) -> p c t", t=SEQ)
                  for t in (4, 5, 7)]
        br_t = [[br_high[:, r, :, :], br_low[r]] for r in range(3)]
        cmp_w1 = gbuf[:, :].rearrange("p (k l f) -> p k l f", k=2, l=CMP_BLOCK // 2)
        q_buf, q_parts = shared("q_buf", [P, 8 * SEQ])
        k_buf, k_parts = shared("k_buf", [P, 8 * SEQ])
        q_t, k_t = (v[0:64, :].rearrange("p (h t) -> p h t", h=8) for v in (q_buf, k_buf))
        sc = sb("sc", [P, 2, 2, SEQ])
        p_t, p_parts = shared("p_t", [P, 2, 512])
        gain = sb("gain", [P, 3, D])
        bias2 = sb("bias2", [P, NSA_H, SEQ])
        bias_c = sb("bias_c", [P, TB, N_CMP, NSA_H])
        consts = sb("consts_sb", [P, 640])
        ident, triu, before, iota = (consts[:, i * P:(i + 1) * P] for i in range(4))
        rope_cos = consts[:, 512:576].rearrange("p (b d) -> p b d", b=TB)
        rope_sin = consts[:, 576:640].rearrange("p (b d) -> p b d", b=TB)
        ones = sb("ones", [P, P])
        half = sb("half", [P, 8])
        rs_in = sb("rs_in", [P, 8])
        rs_out = sb("rs_out", [P, 8])
        stats = sb("stats", [P, 8, 2, 6])
        mv = sb("mv", [P, 8, 2])
        negm = sb("negm", [P, 2, 2])
        den = sb("den", [P, 2, 2])
        coef = sb("coef", [P, 2, 4])
        small = sb("small", [P, 65])
        biasrow = acc[0:8, 0, :].rearrange("p (i n) -> p i n", i=2)
        rel1 = sb("rel1", [BUCKETS + 1, HEADS1])
        rel2 = sb("rel2", [BUCKETS + 1, NSA_H])
        extra = sb("extra", [P, 2 * EXTRA], I32)

        one = ExitStack()
        with one:
            gm_ws = sb("gm_ws", [P, DEPTH, 4, P], where=one)
            gm_bs = sb("gm_bs", [P, DEPTH, 4], where=one)
            lamv = sb("lamv", [P, 4, DEPTH, 64], where=one)
            subln = sb("subln", [P, DEPTH, P], where=one)
            pool_w = sb("pool_w_sb", [64, DEPTH, 4, 64], where=one)
            pool_s = sb("pool_s", [P, DEPTH, 256], where=one)
            bias1, bias1_parts = shared("bias1", [P, HEADS1, SEQ], one)
            gm_wt = sb("gm_wt", [P, 4, P], where=one)
            router = sb("router", [P, KC, N_EXP], where=one)
            router_parts = sb("router_parts", [P, KC, 2, N_EXP], F32R, where=one)
            lam = sb("lam", [P, 8], where=one)
            logits = sb("logits", [P, TB, 8], where=one)
            top = sb("top", [P, TB, 8], where=one)
            topi = sb("topi", [P, TB, 8], U32, where=one)
            topf = sb("topf", [P, TB, 8], where=one)
            pick = sb("pick", [P, TB, 2, 8], where=one)
            gates = sb("gates", [P, TB, ROUNDS + 1], where=one)
            rank = sb("rank", [P, TB, ROUNDS + 1], where=one)
            mask = sb("mask", [P, TB, N_EXP], where=one)
            excess = sb("excess", [P, 2, N_EXP], where=one)
            extra_is = sb("extra_is", [P, EXTRA, N_EXP], where=one)
            extra_of = sb("extra_of", [P, 5, EXTRA, N_EXP], where=one)
            seen = sb("seen", [P, 3, EXTRA], where=one)
        squares = gbuf[:, 1024:2048].rearrange("p (u d) -> p u d", u=HEADS1 * TB)
        poolT = gbuf[0:64, 0:1024].rearrange("p (g t) -> p g t", g=4)
        pool_a = z[:, 6:8, :, :].rearrange("p t b (g n) -> p (t b g) n", g=2)
        onehot = acc[0:BUCKETS + 1, 1, 0:512]
        onehot_c = gbuf[0:BUCKETS + 1, 0:TB * N_CMP * P].rearrange(
            "p (b n q) -> p b n q", b=TB, n=N_CMP)
        xg_t = [act_t[i][:, 0:4, :].rearrange("p c (h n) -> p (c h) n", h=2) for i in range(2)]
        sel, sel_g = (sc[:, i, :, 0:P] for i in range(2))
        sel_gt = sc[:, 0, :, P:2 * P]
        ye = gbuf[:, 1024:2048]
        hs_e = gbuf[:, 0:1024].rearrange("p (i n) -> p i n", i=2)
        hu_e = gbuf[:, 2048:3072].rearrange("p (i n) -> p i n", i=2)
        hide_t = [zparts[:, i * 4096:i * 4096 + D_FFE].rearrange("p (c n) -> p c n", n=CAP) for i in range(2)]

        def pieces(v):
            return [v[:, 0:1024], v[:, 1024:2048]]

        expert_ring = pieces(q_buf) + pieces(k_buf) + [nat[:, b, :] for b in range(TB)] + [
            p_t[:, :, :].rearrange("p i n -> p (i n)")]
        expert_lows = pieces(q_parts) + pieces(k_parts) + [nat_parts[:, b, :] for b in range(TB)] + [
            p_parts[:, :, :].rearrange("p i n -> p (i n)")]
        expert_highs = [gparts[:, 3072:4096], bias1_parts[:, :, :].rearrange("p h t -> p (h t)")]
        for n in range(len(STREAM1), len(STREAM1) + UNITS):
            expert_ring.append(ring[n % UNITS][:, :])
            expert_lows.append(lows[n % UNITS][:, :])
        for n in range(len(STREAM1), len(STREAM1) + HIGHS):
            expert_highs.append(highs[n % HIGHS][:, :])
        assert len(expert_ring) == EXPERT_UNITS and len(expert_highs) == EXPERT_HIGHS

        two = ExitStack()
        with two:
            decay = sb("decay", [P, RET_H, 384], where=two)
            ret_gn = sb("ret_gn", [P, 512], where=two)
            conv_nat = sb("conv_nat", [CONV_W + 1, CONV_CH], where=two)
            conv_ln = sb("conv_ln", [P, 2, CONV_CH], where=two)
            cmp_w2 = sb("cmp_w2", [P, 2, 64], where=two)
            pe_nat = sb("pe_nat", [CMP_BLOCK, 2, 64], where=two)
            taps = sb("taps", [P, 4, CONV_W + 1], where=two)
            cbuf = sb("cbuf", [P, 6 * SEQ], where=two)
            hidp = sb("hidp", [P, 2, 45], where=two)
            hidc = sb("hidc", [P, 2, 2 * N_CMP], where=two)
            kcmp = sb("kcmp", [64, 2, N_CMP], where=two)
            vcmp = sb("vcmp", [N_CMP, 2, 64], where=two)
            sc_c = sb("sc_c", [P, TB, NSA_H, N_CMP], where=two)
            gates2 = sb("gates2", [P, TB, 24], where=two)
        pc_t = p_t[0:N_CMP, :, :].rearrange("p i (h q) -> p (i h) q", q=P)
        c_t = cbuf[:, :].rearrange("p (s t) -> p s t", s=6)
        PAD = CONV_W - 1
        u_t = cbuf[:, 0:4 * (PAD + SEQ)].rearrange("p (c t) -> p c t", c=4)
        y_t = z[:, 6, :, :].rearrange("p b (c t) -> p (b c) t", t=SEQ)
        y_pool, tap_pool = z[:, 7, :, :], gbuf[:, 0:1024]
        o_conv = z[:, 3, :, :]
        o_cmp = acc[:, 0, :].rearrange("p (b n) -> p b n", b=TB)
        rot = acc[:, 1, :].rearrange("p (b h d) -> p b h d", b=TB, h=8)
        tile_of = lambda v: v.rearrange("p (b n) -> p b n", b=TB)
        sig = [z[:, 0, :, :], tile_of(gbuf[:, 3072:4096]), z[:, 1, :, :], z[:, 2, :, :],
               tile_of(q_buf[:, 0:1024]), tile_of(q_buf[:, 1024:2048])]

        tiles = [ctx.enter_context(nc.psum_tensor(f"tile{i}", [P, 512], F32)) for i in range(4)]
        aux = [ctx.enter_context(nc.psum_tensor(f"aux{i}", [P, 512], F32)) for i in range(4)]
        rows = nc.dram_tensor("bias_rows", (HEADS1 + NSA_H, P, REACH), F32)

        S = Signals(sem)
        S2 = Signals(sem, "_2")
        expert_loaded = [sem(f"expert_loaded{i}") for i in range(EXPERT_UNITS)]
        x_loaded = sem("x_loaded")
        small_loaded = sem("small_loaded")
        consts_loaded = sem("consts_loaded")
        pool_loaded = sem("pool_loaded")
        filled = sem("filled")
        params_loaded = sem("params_loaded")
        tables_loaded = sem("tables_loaded")
        layer_loaded = sem("layer_loaded")
        cmp_loaded = sem("cmp_loaded")
        params_used = sem("params_used")
        gain_loaded = [sem(f"gain_loaded{i}") for i in range(3)]
        rows_ready = sem("rows_ready")
        rows_stored = sem("rows_stored")
        bias_loaded = sem("bias_loaded")
        nat_ready = sem("nat_ready")
        var_ready = sem("var_ready")
        rstd_ready = sem("rstd_ready")
        scores_ready = sem("scores_ready")
        probs_ready = sem("probs_ready")
        attn_ready = sem("attn_ready")
        squared = sem("squared")
        vn_ready = sem("vn_ready")
        lam_dots = sem("lam_dots")
        lam_exp = sem("lam_exp")
        route_dif = sem("route_dif")
        route_exp = sem("route_exp")
        route_mask = sem("route_mask")
        merged = sem("merged")
        hidc_in = sem("hidc_in")
        hidc_ready = sem("hidc_ready")
        cmp_scores = sem("cmp_scores")
        cmp_exp = sem("cmp_exp")
        cmp_probs = sem("cmp_probs")
        rot_ready = sem("rot_ready")
        conv_in = sem("conv_in")
        conv_ready = sem("conv_ready")
        pool_taps = sem("pool_taps")
        conv_out = sem("conv_out")
        conv_norm = sem("conv_norm")
        conv_act = sem("conv_act")
        out_stored = sem("out_stored")
        gated2 = sem("gated2")

        def expert_unit(sig_, n):
            return n - len(STREAM1) if sig_ is S else -1

        def slot(sig_, n):
            m = expert_unit(sig_, n)
            if m >= 0:
                k = m % EXPERT_UNITS
                return expert_ring[k], expert_lows[k], expert_loaded[k], m // EXPERT_UNITS + 1
            k = n % UNITS
            return ring[k][:, :], lows[k][:, :], sig_.unit_loaded[k], n // UNITS + 1

        def high_slot(sig_, n):
            m = expert_unit(sig_, n)
            return expert_highs[m % EXPERT_HIGHS] if m >= 0 else highs[n % HIGHS][:, :]

        gains = ([("ln1_g", 0, "ln1_b"), ("ln2_g", 0, "ln2_b"), ("ln1_g", 1, "ln1_b"), ("ln2_g", 1, "ln2_b")]
                 + [(n, l, None) for l in range(DEPTH) for n in ("norm_mix_2", "norm_mlp_2")]
                 + [("norm_final_2", None, None)])
        def row(src, width):
            return src.rearrange("(o n) -> o n", o=1).to_broadcast([P, width])

        block = ctx.enter_context(nc.Block())

        @block.sync
        def _(sp):
            C = Counts()

            def unit(sig_, dst, src):
                n = C.unit.take()
                behind = EXPERT_UNITS if expert_unit(sig_, n) >= 0 else UNITS
                wait(sp, sig_.unit_done, C.unit.at(n - behind + 1))
                memory, _, loaded, _ = slot(sig_, n)
                sp.dma_start(dst(memory), src).then_inc(loaded, 16)

            def narrow(sig_, w, c0, width):
                for r0 in range(0, D, 256):
                    unit(sig_, lambda r: r[:, 0:2 * width].rearrange("p (c n) -> p c n", c=2),
                         w[r0:r0 + 256, c0:c0 + width].rearrange("(c p) n -> p c n", p=P))

            def wide(sig_, w, first, rows_):
                for r0 in range(first, first + rows_, P):
                    unit(sig_, lambda r: r[:, :], w[r0:r0 + P, :])

            def hidden(sig_, parts, w1s, w2):
                for part in parts:
                    for c0, width in part:
                        for w1 in w1s:
                            narrow(sig_, w1, c0, width)
                    wide(sig_, w2, part[0][0], sum(width for _, width in part))

            def expert(sig_, e):
                w1, w3, w2 = (A[n][0, bass.ds(e, 1)].rearrange("o k n -> (o k) n")
                              for n in ("moe_w1", "moe_w3", "moe_w2"))
                for t in range(MOE_TILES):
                    narrow(sig_, w1, t * 512, 512)
                    narrow(sig_, w3, t * 512, 512)
                wide(sig_, w2, 0, D_FFE)

            def load_on(dst, src, sig_=params_loaded, scattered=False):
                sp.dma_start(dst, src, allow_slow_non_contiguous=scattered).then_inc(sig_, 16)

            def load_tables():
                load_on(rel1[0:BUCKETS, :], A["rel_bias"], consts_loaded)
                load_on(rel2[0:BUCKETS, :], A["rel_table_2"], consts_loaded)
                load_on(onehot, A["c_onehot"][:, 0:512], consts_loaded)
                load_on(gbuf[0:BUCKETS + 1, 0:TB * N_CMP * P], A["c_onehot"][:, 512:512 + TB * N_CMP * P], consts_loaded)

            def load_params1():
                for l in range(DEPTH):
                    load_on(gm_ws[:, l, :, :], A["gmlp_ws"][l].rearrange("h t s -> t h s"))
                    load_on(gm_bs[:, l, :], A["gmlp_bs"][l].rearrange("h t -> t h"), scattered=True)
                    load_on(subln[:, l, :], row(A["diff_subln_g"][l], P))
                    load_on(pool_w[:, l, :, :], A["pool_w"][l].rearrange("g c d -> c g d"))
                    load_on(pool_s[:, l, :], row(A["pool_scale"][l], 256))
                    for i, name in enumerate(("lam_q1", "lam_k1", "lam_q2", "lam_k2")):
                        load_on(lamv[:, i, l, :], row(A[name][l], 64))
                load_on(router[:, :, :], A["router_w"][0].rearrange("(c p) e -> p c e", p=P))

            def load_params2(l):
                def load(dst, src):
                    sp.dma_start(dst, src).then_inc(layer_loaded, 16)

                sp.wait_ge(params_used, l + 1)
                load(conv_nat[0:CONV_W, :], A["conv_w_2"][l])
                load(conv_nat[CONV_W:CONV_W + 1, :], A["conv_b_2"][l:l + 1, :])
                for k, kind in enumerate("kv"):
                    load(cmp_w1[:, k, :, :], A[f"cmp_w1_{kind}_2"][l].rearrange("(i a) d f -> (a d) i f", a=2))
                    load(cmp_w2[:, k, :], A[f"cmp_w2_{kind}_2"][l])
                    load(pe_nat[:, k, :], A[f"cmp_pe_{kind}_2"][l])

            def load_tables2(l):
                def load(dst, src):
                    sp.dma_start(dst, src).then_inc(tables_loaded, 16)

                load(decay[:, :, :], A["c_decay"].rearrange("p (h t) -> p h t", h=RET_H))
                load(ret_gn[:, :], row(A["ret_gn_2"][l], 512))
                load(conv_ln[:, 0, :], row(A["conv_ln_g_2"][l], CONV_CH))
                load(conv_ln[:, 1, :], row(A["conv_ln_b_2"][l], CONV_CH))

            sp.dma_start(x[:, :, :], A["x"][0].rearrange("(b p) d -> p b d", p=P)).then_inc(x_loaded, 16)
            sp.dma_start(consts[:, :], A["c_small"]).then_inc(small_loaded, 16)
            for l in range(DEPTH):
                for i, t in enumerate(ORDER1):
                    c0, width = TILES1[t]
                    if l == 0 and 0 < i < 3:
                        (load_tables, load_params1)[i - 1]()
                    narrow(S, A["w_in"][l], c0, width)
                wide(S, A["w_out"][l], 0, D)
                if l == 0:
                    hidden(S, FF_PARTS, (A["ffn_w1"][0], A["ffn_w3"][0]), A["ffn_w2"][0])
                else:
                    sp.wait_ge(S.unit_done, len(STREAM1) - len(OUT1) + 1)
                    rolled(sp, C, lambda _, e, last: expert(S, e), route_mask, extra)
            sp.wait_ge(params_used, 1)
            C = Counts()
            for l in range(DEPTH):
                for i, t in enumerate(ORDER2):
                    if i == len(ORDER2) - 2:
                        wide(S2, A["w_branch_2"][l, 0], 0, 512)
                    if i == 1:
                        load_params2(l)
                    if i == len(ORDER2) - 4:
                        load_tables2(l)
                    narrow(S2, A["w_in_2"][l], *TILES2[t])
                for r in range(1, 3):
                    wide(S2, A["w_branch_2"][l, r], 0, 512)
                wide(S2, A["w_out_2"][l], 0, D)
                hidden(S2, FF2_PARTS, (A["w_ff1_2"][l],), A["w_ff2_2"][l])
            sp.wait_ge(nat_ready, TB * (NORM_STAGE[-1] + 1))
            sp.dma_start(out[0].rearrange("(b p) d -> p b d", p=P), nat[:, :, :]).then_inc(out_stored, 16)
            sp.wait_ge(out_stored, 16)

        @block.tensor
        def _(pe):
            C = Counts()
            SG = [S]

            def unit(shared):
                n = C.unit.take()
                pe.wait_ge(SG[0].low_pool, C.unit.at(n) + 1)
                if shared:
                    pe.wait_ge(SG[0].low_vec, C.low.at(C.low.take()) + 1)
                return high_slot(SG[0], n), slot(SG[0], n)[1]

            def products(bank, lhs, high, low, start, stop):
                nc.tensor.matmul(bank, lhs[0], high, start=start, stop=False)
                nc.tensor.matmul(bank, lhs[0], low, start=False, stop=False)
                return nc.tensor.matmul(bank, lhs[1], high, start=False, stop=stop)

            def tile_bank():
                n = C.tile.take()
                wait(pe, SG[0].tile_evac, C.tile.at(n - 3))
                return tiles[n % 4]

            def aux_bank():
                n = C.aux.take()
                wait(pe, SG[0].aux_evac, C.aux.at(n - 3))
                return aux[n % 4]

            def aux_done():
                wait(pe, SG[0].aux_evac, C.aux.at(C.aux.n))

            def narrow(*args, **options):
                for _ in by_unit(*args, **options):
                    pass

            def by_unit(width, lhs, blocks=TB, shared=False, when=None):
                banks = {}
                for k in range(KC // 2):
                    high, low = (v[:, 0:2 * width].rearrange("p (c n) -> p c n", c=2) for v in unit(shared))
                    for b in range(blocks):
                        if k == 0:
                            banks[b] = tile_bank()
                        if when and k % 2 == 0:
                            when(b, k // 2)
                        for c in range(2):
                            mm = products(banks[b][:, 0:width], lhs(2 * k + c, b), high[:, c, :], low[:, c, :],
                                          k == 0 and c == 0, k == KC // 2 - 1 and c == 1)
                        if k == KC // 2 - 1 and b < blocks - 1:
                            mm.then_inc(SG[0].tile_full, 1)
                    mm.then_inc(SG[0].unit_done, 1)
                    yield

            def by_units(widths):
                for width in widths:
                    yield from by_unit(width, lhs_act)

            def go_on(later, units):
                for _ in range(units):
                    next(later)

            def wide(units, lhs, blocks=TB, shared=False, between={}, when=None):
                banks = []
                for k in range(units):
                    if k in between:
                        between[k]()
                    high, low = unit(shared)
                    for b in range(blocks):
                        if when and k % 4 == 0:
                            when(b, k // 4)
                        for h in range(2):
                            at = slice(h * 512, (h + 1) * 512)
                            if k == 0:
                                banks.append(tile_bank())
                            mm = products(banks[2 * b + h][:, :], lhs(k, b), high[:, at], low[:, at],
                                          k == 0, k == units - 1)
                            if k == units - 1 and (b, h) != (blocks - 1, 1):
                                mm.then_inc(SG[0].tile_full, 1)
                    mm.then_inc(SG[0].unit_done, 1)

            def turn(sources):
                bank = aux_bank()
                for i, src in enumerate(sources):
                    k, m = src.shape
                    mm = nc.tensor.transpose(bank[0:m, i * k:(i + 1) * k], src, ident[0:k, 0:k])
                mm.then_inc(SG[0].aux_full, 1)

            def turn_all(src, stage=None):
                for b in range(TB):
                    if stage is not None:
                        pe.wait_ge(nat_ready, 2 * stage + b + 1)
                    for h in range(2):
                        turn([src[:, b, (4 * h + i) * P:(4 * h + i + 1) * P] for i in range(4)])

            def block_of(v):
                return lambda c, b: [part[:, c, b * P:(b + 1) * P] for part in v]

            lhs_act = block_of(act_t)

            def arriving():
                n = C.aux.n - 2 * TB
                return lambda b, h: pe.wait_ge(SG[0].aux_evac, n + 2 * b + h + 1)

            def hidden_layer(parts, matrices, turn_hidden, hid_t):
                when = arriving()
                for part in parts:
                    for t, (_, width) in enumerate(part):
                        for _ in range(matrices):
                            narrow(width, lhs_act, when=when)
                            when = None
                        if t > 0:
                            turn_hidden(t - 1, part[t - 1][1])
                    turned = C.aux.n

                    def in_by(n):
                        return lambda: pe.wait_ge(SG[0].aux_evac, n)

                    wide(sum(width for _, width in part) // P, block_of(hid_t), between={
                        0: in_by(turned - TB), 2: lambda: turn_hidden(t, width), 4 * (t - 1): in_by(turned),
                        4 * t: aux_done})

            def pipelined(n, scores, turned, values, between):
                scores(0)
                scores(1)
                for u in range(n):
                    turned(u)
                    if u + 2 < n:
                        scores(u + 2)
                    between(u)
                    values(u)

            def tables_of_bias():
                pe.wait_ge(consts_loaded, 64)
                pe.wait_ge(filled, FILLS)
                for rel, heads in ((rel1, HEADS1), (rel2, NSA_H)):
                    nc.tensor.matmul(aux_bank()[0:heads, :], rel[:, :], onehot, start=True,
                                     stop=True).then_inc(S.aux_full, 1)
                bank = aux_bank()
                for b in range(TB):
                    for n in range(N_CMP):
                        at = (b * N_CMP + n) * NSA_H
                        mm = nc.tensor.matmul(bank[:, at:at + NSA_H], onehot_c[:, b, n, :], rel2[:, :],
                                              start=True, stop=True)
                mm.then_inc(S.aux_full, 1)

            pe.wait_ge(x_loaded, 16)
            pe.wait_ge(small_loaded, 16)
            for l in range(DEPTH):
                turn_all(x, None if l == 0 else 2)
                t0 = C.tile.n
                for t in range(EARLY):
                    narrow(TILES1[ORDER1[t]][1], lhs_act, when=arriving() if t == 0 else None)
                if l == 0:
                    tables_of_bias()
                later = by_units([TILES1[t][1] for t in ORDER1[EARLY:]])
                wait(pe, S.tile_evac, t0 + 4)
                for t in (1, 2):
                    for b in range(TB):
                        for h in range(2):
                            turn([z[:, t, b, (4 * h + i) * 64:(4 * h + i + 1) * 64] for i in range(4)])
                        go_on(later, TURN1[TB * (t - 1) + b])
                pe.wait_ge(params_loaded, 16 * PARAMS1)
                turn([gm_ws[:, l, h, :] for h in range(4)])
                aux_done()
                wait(pe, S.tile_evac, t0 + 6)

                def mix(b):
                    pe.wait_ge(vn_ready, 2 * l + b + 1)
                    bank = aux_bank()
                    for h in range(4):
                        mm = nc.tensor.matmul(bank[:, h * 64:(h + 1) * 64], gm_wt[:, h, :],
                                              z[:, 0, b, 256 + h * 64:256 + (h + 1) * 64],
                                              start=True, stop=True)
                    mm.then_inc(S.aux_full, 1)

                def pool_means(g2):
                    wait(pe, S.tile_evac, t0 + 10)
                    pe.wait_ge(pool_loaded, 16)
                    bank = aux_bank()
                    for i in range(2):
                        g = 2 * g2 + i
                        for s in range(TB):
                            mm = nc.tensor.matmul(bank[0:64, i * SEQ:(i + 1) * SEQ],
                                                  z[:, 4, s, g * 64:(g + 1) * 64], pool_a[:, s * 4 + g, :],
                                                  start=(s == 0), stop=(s == 1))
                    mm.then_inc(S.aux_full, 1)

                def between(u):
                    go_on(later, STEPS1[u])
                    if u in MIX_AT:
                        mix(MIX_AT.index(u))
                    if u in POOL_AT:
                        pool_means(POOL_AT.index(u))

                turned_at = {}

                def scores(u):
                    h, b = divmod(u, TB)
                    nk = (b + 1) * P
                    bank = aux_bank()
                    for m in range(2):
                        mm = nc.tensor.matmul(bank[:, m * SEQ:m * SEQ + nk],
                                              q_t[:, 2 * h + m, b * P:(b + 1) * P],
                                              k_t[:, 2 * h + m, 0:nk], start=True, stop=True)
                    mm.then_inc(S.aux_full, 1)

                def turned(u):
                    pe.wait_ge(attn_ready, l * HEADS1 * TB + u + 1)
                    turn([sc[:, u % 2, 0, k * P:(k + 1) * P] for k in range(u % TB + 1)])
                    turned_at[u] = C.aux.n

                def values(u):
                    h, b = divmod(u, TB)
                    pe.wait_ge(S.aux_evac, turned_at[u])
                    bank = aux_bank()
                    for k in range(b + 1):
                        mm = nc.tensor.matmul(bank[:, 0:P], p_t[:, u % 2, k * P:(k + 1) * P],
                                              z[:, 3, k, h * P:(h + 1) * P], start=(k == 0), stop=(k == b))
                    mm.then_inc(S.aux_full, 1)

                pipelined(HEADS1 * TB, scores, turned, values, between)
                for b in range(TB):
                    bank = aux_bank()
                    for g in range(4):
                        mm = nc.tensor.matmul(bank[:, g * 64:(g + 1) * 64], poolT[:, g, b * P:(b + 1) * P],
                                              pool_w[:, l, g, :], start=True, stop=True)
                    mm.then_inc(S.aux_full, 1)
                turn_all(nat, 3 * l)
                wide(KC, lhs_act, when=arriving())
                turn_all(x, 3 * l + 1)
                if l == 0:
                    def turn_hidden(t, width):
                        pe.wait_ge(S.gated, C.gated.take() + 1)
                        for b in range(TB):
                            turn([hs[:, t % 2, b, i * P:(i + 1) * P] for i in range(width // P)])

                    hidden_layer(FF_PARTS, 2, turn_hidden, hid1_t)
                else:
                    when = arriving()
                    for b in range(TB):
                        bank = aux_bank()
                        for c in range(KC):
                            if c % 4 == 0:
                                when(b, c // 4)
                            for i, part in enumerate(lhs_act(c, b)):
                                mm = nc.tensor.matmul(bank[:, 0:2 * N_EXP], part,
                                                      router_parts[:, c, :, :].rearrange("p i e -> p (i e)"),
                                                      start=(c == 0 and i == 0), stop=(c == KC - 1 and i == 1))
                        mm.then_inc(S.aux_full, 1)
                    pe.wait_ge(route_mask, 1)
                    bank = aux_bank()
                    for to, parts in enumerate([[(before, 0)], [(ones, 0), (before, 1)], [(ones, 0), (ones, 1)]]):
                        for i, (m, b) in enumerate(parts):
                            mm = nc.tensor.matmul(bank[:, to * 8:to * 8 + 8], m[:, :], mask[:, b, :],
                                                  start=(i == 0), stop=(i == len(parts) - 1))
                    mm.then_inc(S.aux_full, 1)

                    def gather():
                        n = C.picked.take()
                        pe.wait_ge(SG[0].picked, C.picked.at(n) + 1)
                        for j in range(4):
                            bank = aux_bank()
                            for i in range(2):
                                for b in range(TB):
                                    mm = nc.tensor.matmul(bank[:, i * P:(i + 1) * P],
                                                          x[:, b, (2 * j + i) * P:(2 * j + i + 1) * P],
                                                          sel[:, b, :], start=(b == 0), stop=(b == TB - 1))
                            mm.then_inc(SG[0].aux_full, 1)

                    def turn_gates():
                        turn([sel_g[:, b, :] for b in range(TB)])

                    def expert(*_):
                        def turn_hidden(t):
                            n = C.gated.take()
                            pe.wait_ge(SG[0].gated, C.gated.at(n) + 1)
                            turn([hs_e[:, t % 2, i * P:(i + 1) * P] for i in range(4)])

                        wait(pe, SG[0].aux_evac, C.aux.at(C.aux.n))
                        for t in range(MOE_TILES):
                            for _ in range(2):
                                narrow(512, lambda c, b: [part[:, c, :] for part in xg_t], 1, True)
                            if t > 0:
                                turn_hidden(t - 1)
                        turned = C.aux.n

                        def in_by(n):
                            return lambda: pe.wait_ge(SG[0].aux_evac, C.aux.at(n))

                        def last():
                            turn_hidden(MOE_TILES - 1)
                            aux_done()

                        wide(D_FFE // P, lambda c, b: [part[:, c, :] for part in hide_t], 1, True,
                             {0: in_by(turned - 1), GATHER_AT: gather, D_FFE // P - 8: in_by(turned),
                              D_FFE // P - 4: last})
                        out_tile = C.tile.n
                        wait(pe, SG[0].tile_evac, C.tile.at(out_tile))
                        for b in range(TB):
                            for h in range(2):
                                nc.tensor.matmul(aux_bank()[:, :], sel_gt[:, b, :], ye[:, h * 512:(h + 1) * 512],
                                                 start=True, stop=True).then_inc(SG[0].aux_full, 1)
                        turn_gates()

                    gather()
                    turn_gates()
                    rolled(pe, C, expert, route_mask, extra)

            C, SG[0] = Counts(), S2
            for l in range(DEPTH):
                turn_all(nat, 6 + 4 * l)
                t0 = C.tile.n
                for t in range(EARLY):
                    narrow(TILES2[ORDER2[t]][1], lhs_act, when=arriving() if t == 0 else None)
                later = by_units([TILES2[t][1] for t in ORDER2[EARLY:]])
                fills = iter(TURN2)
                pe.wait_ge(S2.tile_evac, t0 + 2 * EARLY)
                pe.wait_ge(layer_loaded, 16 * PARAMS2 * (l + 1))
                turn([conv_nat[:, c * P:(c + 1) * P] for c in range(4)])
                turn([pe_nat[:, k, :] for k in range(2)])
                for b in range(TB):
                    turn([z[:, 1, b, i * 64:(i + 1) * 64] for i in range(4)])
                    go_on(later, next(fills))
                    turn([z[:, 1, b, 256 + i * 64:256 + (i + 1) * 64] for i in range(2)]
                         + [z[:, 2, b, i * 64:(i + 1) * 64] for i in range(2)])
                    for h in range(2):
                        turn([z[:, 0, b, (4 * h + i) * 64:(4 * h + i + 1) * 64] for i in range(4)])
                    go_on(later, next(fills))
                aux_done()
                for k in range(2):
                    bank = aux_bank()
                    for i in range(CMP_BLOCK // 2):
                        last_col = 2 * i + CMP_STRIDE * (N_CMP - 1) + 1
                        mm = nc.tensor.matmul(bank[:, 0:3 * N_CMP], cmp_w1[:, k, i, :],
                                              c_t[:, 3 * k:3 * k + 3, 2 * i:last_col:CMP_STRIDE],
                                              start=(i == 0), stop=(i == CMP_BLOCK // 2 - 1))
                    mm.then_inc(S2.aux_full, 1)
                go_on(later, next(fills))
                pe.wait_ge(hidc_ready, 2 * l + 2)
                nc.tensor.matmul(aux_bank()[0:64, 0:2 * N_CMP], cmp_w2[:, 0, :], hidc[:, 0, :], start=True,
                                 stop=True).then_inc(S2.aux_full, 1)
                bank = aux_bank()
                for g in range(NSA_G):
                    mm = nc.tensor.matmul(bank[0:N_CMP, g * 64:(g + 1) * 64],
                                          hidc[:, 1, g * N_CMP:(g + 1) * N_CMP], cmp_w2[:, 1, :],
                                          start=True, stop=True)
                mm.then_inc(S2.aux_full, 1)
                go_on(later, next(fills))
                aux_done()
                bank = aux_bank()
                for b in range(TB):
                    for h in range(NSA_H):
                        at = (b * NSA_H + h) * N_CMP
                        mm = nc.tensor.matmul(bank[:, at:at + N_CMP], q_t[:, h, b * P:(b + 1) * P],
                                              kcmp[:, h // 4, :], start=True, stop=True)
                mm.then_inc(S2.aux_full, 1)
                go_on(later, next(fills))
                for b in range(TB):
                    pe.wait_ge(conv_in, 2 * l + b + 1)
                    turn([z[:, 6, b, c * P:(c + 1) * P] for c in range(4)])
                go_on(later, next(fills))
                pe.wait_ge(cmp_probs, l + 1)
                for b in range(TB):
                    for h2 in range(2):
                        turn([sc_c[:, b, 4 * h2 + i, :] for i in range(4)])
                    go_on(later, next(fills))
                    aux_done()
                    bank = aux_bank()
                    for h in range(NSA_H):
                        mm = nc.tensor.matmul(bank[:, h * 64:(h + 1) * 64], pc_t[:, h, :], vcmp[:, h // 4, :],
                                              start=True, stop=True)
                    mm.then_inc(S2.aux_full, 1)


                turned_at = {}

                def scores(u):
                    h, b = divmod(u, TB)
                    nk = (b + 1) * P
                    g = h // 4
                    nc.tensor.matmul(aux_bank()[:, 0:2 * nk].rearrange("p (r k) -> p r k", r=2),
                                     q_t[:, h, b * P:(b + 1) * P], k_t[:, g:g + 3:2, 0:nk],
                                     start=True, stop=True).then_inc(S2.aux_full, 1)

                def turned(u):
                    pe.wait_ge(probs_ready, (DEPTH * HEADS1 + l * NSA_H) * TB + u + 1)
                    turn([sc[:, u % 2, r, k * P:(k + 1) * P] for r in range(2) for k in range(u % TB + 1)])
                    turned_at[u] = C.aux.n

                def values(u):
                    h, b = divmod(u, TB)
                    g = h // 4
                    pe.wait_ge(S2.aux_evac, turned_at[u])
                    bank = aux_bank()
                    for r in range(2):
                        for k in range(b + 1):
                            v = (z[:, 1, k, 384 + g * 64:384 + (g + 1) * 64] if r == 0 else
                                 z[:, 2, k, 128 + g * 64:128 + (g + 1) * 64])
                            at = (r * (b + 1) + k) * P
                            mm = nc.tensor.matmul(bank[:, r * 64:(r + 1) * 64], p_t[:, u % 2, at:at + P], v,
                                                  start=(k == 0), stop=(k == b))
                    mm.then_inc(S2.aux_full, 1)

                pipelined(NSA_H * TB, scores, turned, values, lambda u: go_on(later, STEPS2[u]))
                fills = iter(AFTER2)

                go_on(later, next(fills))
                pe.wait_ge(rot_ready, l + 1)
                for b in range(TB):
                    for h in range(2):
                        turn([rot[:, b, 4 * h + i, :] for i in range(4)])
                for b in range(TB):
                    pe.wait_ge(conv_out, l + 1)
                    turn([y_t[:, c, b * P:(b + 1) * P] for c in range(4)])
                go_on(later, next(fills))
                aux_done()
                pe.wait_ge(S2.tile_evac, t0 + 2 * (ORDER2.index(4) + 1))
                decayed = {}

                def ret_scores(h):
                    bank = aux_bank()
                    nc.tensor.matmul(bank[:, 0:SEQ], q_t[:, 4 + h, 0:P], q_t[:, h, 0:SEQ], start=True, stop=True)
                    nc.tensor.matmul(bank[:, SEQ:SEQ + P], q_t[:, 4 + h, P:SEQ], q_t[:, h, P:SEQ],
                                     start=True, stop=True).then_inc(S2.aux_full, 1)
                    decayed[h] = C.aux.n

                def ret_values(h):
                    pe.wait_ge(S2.aux_evac, decayed[h])
                    bank = aux_bank()
                    for b, at, k in ((0, 0, 0), (1, P, 0), (1, 2 * P, 1)):
                        mm = nc.tensor.matmul(bank[:, b * P:(b + 1) * P], p_t[:, h % 2, at:at + P],
                                              z[:, 4, k, h * P:(h + 1) * P], start=(k == 0), stop=(k == b))
                    mm.then_inc(S2.aux_full, 1)

                ret_scores(0)
                for h in range(RET_H):
                    if h + 1 < RET_H:
                        ret_scores(h + 1)
                    go_on(later, next(fills))
                    ret_values(h)
                for b in range(TB):
                    turn([nat[:, b, c * P:(c + 1) * P] for c in range(4)])
                aux_done()
                wide(4, block_of(br_t[0]))
                for b in range(TB):
                    pe.wait_ge(nat_ready, 2 * (6 + 4 * l + 1) + b + 1)
                    turn([nat[:, b, 512 + c * P:512 + (c + 1) * P] for c in range(4)])
                for _ in later:
                    pass
                aux_done()
                wide(4, block_of(br_t[1]))
                for b in range(TB):
                    pe.wait_ge(conv_act, 2 * l + b + 1)
                    turn([o_conv[:, b, c * P:(c + 1) * P] for c in range(4)])
                aux_done()
                wide(4, block_of(br_t[2]))
                turn_all(nat, 6 + 4 * l + 2)
                wide(KC, lhs_act, when=arriving())
                turn_all(nat, 6 + 4 * l + 3)

                def turn_hidden2(t, width):
                    pe.wait_ge(gated2, C.gated.take() + 1)
                    for b in range(TB):
                        turn([hs[:, t % 2, b, i * P:(i + 1) * P] for i in range(width // P)])

                hidden_layer(FF2_PARTS, 1, turn_hidden2, hid2_t)

        @block.scalar
        def _(act):
            C = Counts()
            SG = [S]

            def load(dst, src, sig_):
                act.dma_start(dst, src).then_inc(sig_, 16)

            def ahead(limit):
                while C.split.n < limit:
                    n = C.split.take()
                    cols = STREAM[0][n] if n < len(STREAM[0]) else D
                    weights, _, loaded, loads = slot(SG[0], n)
                    value = 16 * loads
                    if C.split.i is not None:
                        value = value + C.split.i * (16 * C.split.per // EXPERT_UNITS)
                    act.wait_ge(loaded, value)
                    behind = EXPERT_HIGHS if expert_unit(SG[0], n) >= 0 else HIGHS
                    wait(act, SG[0].unit_done, C.split.at(n - behind + 1))
                    nc.scalar.activation(high_slot(SG[0], n)[:, 0:cols], weights[:, 0:cols],
                                         ACT.Copy).then_inc(SG[0].high_ready, 1)

            def idle():
                ahead(min(C.unit.n + HIGHS, END[0]))

            def used(units):
                C.unit.take(units)
                lead = (EXPERT_HIGHS if expert_unit(SG[0], C.unit.n - 1) >= 0 else HIGHS) - 1
                ahead(min(C.unit.n + lead, END[0]))

            def evac(dst, closes, func=ACT.Copy, width=512, scale=1.0, also=None, units=None):
                n = C.tile.take()
                if closes:
                    act.wait_ge(SG[0].unit_done, C.unit.at(C.unit.n if units is None else units))
                else:
                    act.wait_ge(SG[0].tile_full, C.full.at(C.full.take()) + 1)
                if also:
                    also(tiles[n % 4])
                nc.scalar.activation(dst, tiles[n % 4][:, 0:width], func, scale=scale).then_inc(SG[0].tile_evac, 1)

            def evac_tile(dst, func=ACT.Copy, width=512, scale=1.0, also=None):
                used(KC // 2)
                for b in range(TB):
                    evac(dst(b), b == TB - 1, func, width, scale, also and also(b))

            class Later:

                def __init__(self, tiles_):
                    self.tiles, self.begun, self.done = tiles_, C.unit.n, 0

                def go_on(self, units):
                    for _ in range(units):
                        used(1)
                        if (C.unit.n - self.begun) % (KC // 2) == 0:
                            dst, func, width = self.tiles[self.done]
                            self.done += 1
                            for b in range(TB):
                                evac(dst(b), b == TB - 1, func, width)

            def evac_wide(units, before_block=None):
                used(units)
                for b in range(TB):
                    if before_block:
                        before_block(b)
                    for h in range(2):
                        evac(acc[:, b, h * 512:(h + 1) * 512], (b, h) == (TB - 1, 1))

            def exps(count, base, width, later, steps):
                for u in range(count):
                    nk = width(u)
                    act.wait_ge(scores_ready, base + u + 1)
                    for m in range(2):
                        e = nc.scalar.activation(sc[:, u % 2, m, 0:nk], sc[:, u % 2, m, 0:nk], ACT.Exp,
                                                 bias=negm[:, u % 2, m:m + 1],
                                                 accum_out=den[:, u % 2, m:m + 1])
                    e.then_inc(probs_ready, 1)
                    if u > 0:
                        later.go_on(steps[u - 1])
                later.go_on(steps[count - 1])

            STREAM, END = [STREAM1], [len(STREAM1)]
            bias_by_stack = ((bias1, 0, HEADS1), (bias2, HEADS1, NSA_H))
            for l in range(DEPTH):
                def tile1(t):
                    width = TILES1[t][1]
                    return lambda b: z[:, t, b, 0:width], ACT.Gelu if t == 0 else ACT.Copy, width

                for t in range(EARLY):
                    dst, func, width = tile1(ORDER1[t])
                    evac_tile(dst, func, width, QSCALE if ORDER1[t] == 1 else 1.0)
                if l == 0:
                    load(zbuf[:, 6 * 1024:8 * 1024], A["c_pool"], pool_loaded)
                    act.wait_ge(rows_ready, 1)
                    for i, (_, first, heads) in enumerate(bias_by_stack):
                        load(rows.ap()[first:first + heads],
                             biasrow[0:heads, i, 0:REACH].unsqueeze(1).broadcast_to([heads, P, REACH]), rows_stored)
                later = Later([tile1(t) for t in ORDER1[EARLY:]])
                later.go_on(sum(TURN1) - 1)
                if l == 0:
                    act.wait_ge(rows_stored, 32)
                    for dst, first, heads in bias_by_stack:
                        load(dst[:, :, :], bass.AP(rows, first * P * REACH + P - 1,
                                                   [[REACH - 1, P], [P * REACH, heads], [1, SEQ]]), bias_loaded)
                later.go_on(1)
                if l == 0:
                    act.wait_ge(lam_dots, 1)
                    nc.scalar.activation(lam[:, 0:4], lam[:, 4:8], ACT.Exp).then_inc(lam_exp, 1)
                exps(HEADS1 * TB, l * HEADS1 * TB, lambda u: (u % TB + 1) * P, later, STEPS1)
                idle()
                evac_wide(KC)
                if l == 0:
                    for part in FF_PARTS:
                        for t, (_, width) in enumerate(part):
                            evac_tile(lambda b: hs[:, t % 2, b, 0:width], ACT.Silu, width)
                            evac_tile(lambda b: hu[:, t % 2, b, 0:width], ACT.Copy, width)
                        evac_wide(sum(width for _, width in part) // P)
                else:
                    act.wait_ge(route_dif, 1)
                    nc.scalar.activation(small[:, 8:10], small[:, 0:2], ACT.Exp).then_inc(route_exp, 1)
                    END[0] += EXPERT_HIGHS - 1
                    ahead(END[0])

                    def expert(_, __, last):
                        END[0] = C.unit.n + MOE_UNITS + (0 if last else EXPERT_HIGHS - 1)
                        for t in range(MOE_TILES):
                            used(KC // 2)
                            evac(hs_e[:, t % 2, :], True, ACT.Silu)
                            used(KC // 2)
                            evac(hu_e[:, t % 2, :], True)
                        used(D_FFE // P)
                        for h in range(2):
                            evac(ye[:, h * 512:(h + 1) * 512], h == 1)

                    rolled(act, C, expert, route_mask, extra, EXPERT_HIGHS - 1)
            C, SG[0] = Counts(), S2
            STREAM[0], END[0] = STREAM2, len(STREAM2)
            for l in range(DEPTH):
                for t in range(EARLY):
                    if t == 2:
                        evac_tile(lambda b: z[:, t, b, 0:256], ACT.Copy, 256,
                                  also=lambda b: lambda bank: nc.scalar.activation(
                                      gates2[:, b, :], bank[:, 256:280], ACT.Sigmoid))
                    else:
                        evac_tile(lambda b: z[:, t, b, :], scale=QSCALE if t == 0 else 1.0)

                def tile2(t):
                    if t >= 8:
                        return lambda b: sig[t - 8][:, b, :], ACT.Sigmoid, 512
                    return lambda b: z[:, t, b, :], {5: ACT.Silu, 7: ACT.Sigmoid}.get(t, ACT.Copy), 512

                later = Later([tile2(t) for t in ORDER2[EARLY:]])
                later.go_on(sum(TURN2[0:4]))
                for k in range(2):
                    act.wait_ge(hidc_in, 2 * l + k + 1)
                    nc.scalar.activation(hidc[:, k, :], hidp[:, k, 0:2 * N_CMP], ACT.Gelu_apprx_tanh,
                                         bias=hidp[:, k, 2 * N_CMP:2 * N_CMP + 1]).then_inc(hidc_ready, 1)
                later.go_on(TURN2[4] + TURN2[5])
                act.wait_ge(cmp_scores, l + 1)
                nc.scalar.activation(sc_c[:, :, :, :], sc_c[:, :, :, :], ACT.Exp).then_inc(cmp_exp, 1)
                later.go_on(sum(TURN2[6:10]))
                exps(NSA_H * TB, (DEPTH * HEADS1 + l * NSA_H) * TB, lambda u: (u % TB + 1) * P, later, STEPS2)
                later.go_on(sum(AFTER2))
                evac_wide(4)
                later.go_on(2 * KC // 2)
                idle()
                for b in range(TB):
                    act.wait_ge(conv_norm, 2 * l + b + 1)
                    nc.scalar.activation(o_conv[:, b, :], o_conv[:, b, :], ACT.Silu).then_inc(conv_act, 1)
                for r in range(1, 3):
                    evac_wide(4, lambda b: wait(act, merged, (2 * l + r - 1) * TB + b + 1))
                evac_wide(KC, lambda b: act.wait_ge(nat_ready, 2 * (6 + 4 * l + 2) + b + 1))
                for part in FF2_PARTS:
                    for t in range(len(part)):
                        evac_tile(lambda b: hs[:, t % 2, b, :], ACT.Relu)
                    evac_wide(sum(width for _, width in part) // P)

        @block.gpsimd
        def _(pool):
            C = Counts()
            SG = [S]
            pows = Tally()

            nc.gpsimd.memset(ones[:, :], 1.0).then_inc(filled, 1)
            nc.gpsimd.memset(half[:, :], -0.5).then_inc(filled, 1)
            nc.gpsimd.memset(rs_in[:, :], 1.0).then_inc(filled, 1)

            def split(limit, first=0):
                while C.split.n < limit:
                    n = C.split.take()
                    cols = STREAM[0][n] if n < len(STREAM[0]) else D
                    pool.wait_ge(SG[0].high_ready, C.split.at(n) + 1)
                    weights, low, _, _ = slot(SG[0], n)
                    nc.gpsimd.tensor_tensor(low[:, first:cols], weights[:, first:cols],
                                            high_slot(SG[0], n)[:, first:cols], ALU.subtract).then_inc(SG[0].low_pool, 1)

            def load_gain(norm):
                g, l, b = gains[norm]
                last_use = GAIN_AFTER[norm]
                if last_use is not None:
                    pool.wait_ge(nat_ready, 2 * NORM_STAGE[last_use] + TB)
                pool.dma_start(gain[:, GAIN_ROW[norm], :], row(A[g] if l is None else A[g][l], D)).then_inc(gain_loaded[GAIN_ROW[norm]], 16)
                if b is not None:
                    pool.dma_start(gain[:, 1, :], row(A[b][l], D)).then_inc(gain_loaded[GAIN_ROW[norm]], 16)

            def power(groups):
                n = pows.take()
                pool.wait_ge(var_ready, n + 1)
                if n == 0:
                    pool.wait_ge(filled, FILLS)
                nc.gpsimd.tensor_tensor(rs_out[:, 0:groups], rs_in[:, 0:groups], half[:, 0:groups], ALU.pow).then_inc(rstd_ready, 1)

            def tap(l, i):
                done = l * (2 * TAPS_POOL - 1)
                y, one = (v.rearrange("p (c t) -> p c t", t=SEQ)
                          for v in (y_pool.rearrange("p b n -> p (b n)"), tap_pool))
                j = TAPS_VEC + i
                if i > 1:
                    pool.wait_ge(pool_taps, done + 2 * i - 1)
                nc.gpsimd.tensor_tensor(one if i > 0 else y, u_t[:, :, j:j + SEQ],
                                        taps[:, :, j:j + 1].broadcast_to([P, 4, SEQ]), ALU.mult).then_inc(pool_taps, 1)
                if i > 0:
                    pool.wait_ge(pool_taps, done + 2 * i)
                    nc.gpsimd.tensor_tensor(y, y, one, ALU.add).then_inc(pool_taps, 1)

            def stage(units, slack=HIGHS):
                C.unit.take(units)
                split(min(C.unit.n + slack, len(STREAM[0])))

            STREAM = [STREAM1]
            load_gain(0)
            for l in range(DEPTH):
                stage(len(IN1), -sum(STEPS1) + len(NORM_AT))
                power(4)
                power(4)
                stage(0)
                power(TB * HEADS1)
                stage(len(OUT1))
                power(TB)
                load_gain(2 * l + 1)
                if l == 0:
                    stage(len(FF1))
                else:
                    load_gain(4)
                    rolled(pool, C, lambda *_: split(C.split.n + MOE_UNITS, D - MOE_LOW), route_mask, extra)
                power(TB)
                load_gain(2 * l + 2 if l == 0 else 5)
            C, SG[0], STREAM[0] = Counts(), S2, STREAM2
            for l in range(DEPTH):
                power(TB)
                if l > 0:
                    load_gain(7)
                first = C.unit.n + EARLY * KC // 2 + sum(TURN2) + 2
                split(first)
                pool.wait_ge(conv_ready, l + 1)
                for i in range(TAPS_POOL):
                    tap(l, i)
                    split(first + (i + 1) * sum(STEPS2) // TAPS_POOL)
                before_ret, before_conv = BEFORE_RET + 2, BEFORE_RET + 12
                stage(before_ret, 0)
                power(TB * RET_H)
                stage(before_conv - before_ret, 0)
                power(TB)
                stage(len(IN2) + len(BRANCH2) + len(OUT2) - before_conv)
                power(TB)
                load_gain(6 + 2 * l)
                stage(len(FF2))
            power(TB)

        @block.vector
        def _(dve):
            C = Counts()
            SG = [S]
            asked = Tally()
            V = nc.vector

            def step(ins):
                n = C.own.take()
                ins.then_inc(SG[0].vec, 1)
                dve.wait_ge(SG[0].vec, C.own.at(n) + 1)

            def aux_in():
                n = C.aux.take()
                dve.wait_ge(SG[0].aux_full, C.aux.at(n) + 1)
                return aux[n % 4]

            def evac(ins):
                ins.then_inc(SG[0].aux_evac, 1)

            def read_back():
                dve.wait_ge(SG[0].aux_evac, C.aux.at(C.aux.n))

            def turn_in(dst):
                p, n, m = dst.shape
                bank = aux_in()
                evac(V.tensor_copy(dst, bank[0:p, 0:n * m].rearrange("p (n m) -> p n m", n=n)))

            def parts_in(dst):
                p, n, m = dst[0].shape
                src = aux_in()[0:p, 0:n * m].rearrange("p (n m) -> p n m", n=n)
                step(V.tensor_copy(dst[0], src))
                evac(V.tensor_tensor(dst[1], src, dst[0], ALU.subtract))

            def turn_all_in():
                for b in range(TB):
                    for h in range(2):
                        parts_in([part[:, 4 * h:4 * h + 4, b * P:(b + 1) * P] for part in act_t])

            def split(limit):
                while C.split.n < limit:
                    n = C.split.take()
                    dve.wait_ge(SG[0].high_ready, C.split.at(n) + 1)
                    weights, low, _, _ = slot(SG[0], n)
                    V.tensor_tensor(low[:, 0:D - MOE_LOW], weights[:, 0:D - MOE_LOW],
                                    high_slot(SG[0], n)[:, 0:D - MOE_LOW], ALU.subtract).then_inc(SG[0].low_vec, 1)

            def rstd(groups, value, scale, eps):
                n = asked.take()
                V.tensor_scalar(rs_in[:, 0:groups], value, scale, eps, ALU.mult, ALU.add).then_inc(var_ready, 1)
                dve.wait_ge(rstd_ready, n + 1)

            def moments(src, eps):
                _, groups, width = src.shape
                parts = max(1, width // 512)
                for g in range(groups):
                    for i in range(parts):
                        ins = V.bn_stats(stats[:, g, i, :], src[:, g, i * 512:min(width, (i + 1) * 512)])
                step(ins)
                for g in range(groups):
                    ins = V.bn_aggr(mv[:, g, :], stats[:, g, 0:parts, :].rearrange("p i s -> p (i s)"))
                step(ins)
                rstd(groups, mv[:, 0:groups, 1], 1.0, eps)

            def spread(v, width):
                return v.unsqueeze(2).broadcast_to([P, v.shape[1], width])

            def over(v, n):
                return v.unsqueeze(1).broadcast_to([P, n, v.shape[1]])

            def standardise(dst, src, eps, signal=None):
                _, groups, width = src.shape
                moments(src, eps)
                step(V.tensor_tensor(dst, src, spread(mv[:, 0:groups, 0], width), ALU.subtract))
                ins = V.tensor_tensor(dst, dst, spread(rs_out[:, 0:groups], width), ALU.mult)
                if signal is None:
                    step(ins)
                else:
                    ins.then_inc(signal, 1)

            def gain_in(norm):
                loads = sum(1 if gains[n][2] is None else 2 for n in range(norm + 1) if GAIN_ROW[n] == GAIN_ROW[norm])
                dve.wait_ge(gain_loaded[GAIN_ROW[norm]], 16 * loads)

            def add_products(factor):
                for b in range(TB):
                    C.tile.n += 2
                    dve.wait_ge(SG[0].tile_evac, C.tile.n)
                    step(V.scalar_tensor_tensor(x[:, b, :], x[:, b, :], factor, acc[:, b, :], ALU.mult, ALU.add))

            def layer_norm(norm, src=x):
                moments(src[:, :, :], EPS1)
                gain_in(norm)
                for b in range(TB):
                    step(V.scalar_tensor_tensor(x[:, b, :], src[:, b, :], mv[:, b, 0:1], gain[:, 0, :],
                                                ALU.subtract, ALU.mult))
                    V.scalar_tensor_tensor(x[:, b, :], x[:, b, :], rs_out[:, b:b + 1], gain[:, 1, :],
                                           ALU.mult, ALU.add).then_inc(nat_ready, 1)

            def rms_norm(norm):
                for b in range(TB):
                    ins = V.tensor_tensor_reduce(out=nat[:, b, :], in0=x[:, b, :], in1=x[:, b, :], scale=1.0,
                                                 scalar=0.0, op0=ALU.mult, op1=ALU.add,
                                                 accum_out=mv[:, b, 1:2])
                step(ins)
                rstd(TB, mv[:, 0:TB, 1], 1.0 / D, EPS2)
                gain_in(norm)
                for b in range(TB):
                    V.scalar_tensor_tensor(nat[:, b, :], x[:, b, :], rs_out[:, b:b + 1], gain[:, GAIN_ROW[norm], :],
                                           ALU.mult, ALU.mult).then_inc(nat_ready, 1)

            def score_rows(bank, s, bias, nk, at):
                for m in range(2):
                    ins = V.tensor_tensor_reduce(out=sc[:, s, m, 0:nk], in0=bank[:, at(m):at(m) + nk],
                                                 in1=bias[:, SEQ - nk:SEQ], scale=1.0, scalar=-3e38,
                                                 op0=ALU.add, op1=ALU.max,
                                                 accum_out=small[:, 2 * s + m:2 * s + m + 1])
                evac(ins)
                read_back()
                V.tensor_scalar(negm[:, s, :], small[:, 2 * s:2 * s + 2], -1.0, None, ALU.mult).then_inc(scores_ready, 1)

            def pipelined(n, scores, turned, values, between):
                scores(0)
                scores(1)
                for u in range(n):
                    turned(u)
                    if u + 2 < n:
                        scores(u + 2)
                    between(u)
                    values(u)

            V.memset(rel1[BUCKETS:BUCKETS + 1, :], 1.0).then_inc(filled, 1)
            V.memset(rel2[BUCKETS:BUCKETS + 1, :], 1.0).then_inc(filled, 1)
            dve.wait_ge(small_loaded, 16)
            for l in range(DEPTH):
                turn_all_in()
                t0 = C.tile.n
                C.tile.n += 2 * len(TILES1)
                if l == 0:
                    for i, heads in enumerate((HEADS1, NSA_H)):
                        V.tensor_copy(biasrow[0:heads, i, :], aux_in()[0:heads, :]).then_inc(S.aux_evac, 1)
                    read_back()
                    V.memset(small[:, 64:65], 0.0).then_inc(rows_ready, 1)
                    bank = aux_in()
                    evac(V.tensor_copy(bias_c[:, :, :, :].rearrange("p b n h -> p (b n h)"), bank[:, 0:TB * N_CMP * NSA_H]))
                    dve.wait_ge(params_loaded, 16 * PARAMS1)
                    for n in range(DEPTH):
                        for i in range(2):
                            ins = V.tensor_tensor_reduce(out=small[:, 0:64], in0=lamv[:, 2 * i, n, :],
                                                         in1=lamv[:, 2 * i + 1, n, :], scale=1.0, scalar=0.0,
                                                         op0=ALU.mult, op1=ALU.add,
                                                         accum_out=lam[:, 4 + 2 * n + i:5 + 2 * n + i])
                            if n == DEPTH - 1 and i == 1:
                                ins.then_inc(lam_dots, 1)
                            else:
                                step(ins)
                for dst in (q_t, k_t):
                    for b in range(TB):
                        for h in range(2):
                            turn_in(dst[:, 4 * h:4 * h + 4, b * P:(b + 1) * P])
                bank = aux_in()
                evac(V.tensor_tensor(gm_wt[:, :, :], bank[:, :].rearrange("p (h t) -> p h t", h=4), over(triu, 4),
                                     ALU.mult))
                values_ = z[:, 0, :, 256:512]

                def between(u):
                    if u in NORM_AT:
                        dve.wait_ge(S.tile_evac, t0 + 2 * (ORDER1.index(0) + 1))
                        v = values_[:, NORM_AT.index(u), :].rearrange("p (h d) -> p h d", h=4)
                        standardise(v, v, EPS1, vn_ready)
                    if u in MIX_AT:
                        b = MIX_AT.index(u)
                        bank = aux_in()
                        for h in range(4):
                            ins = V.scalar_tensor_tensor(nat[:, b, h * 64:(h + 1) * 64], bank[:, h * 64:(h + 1) * 64],
                                                         gm_bs[:, l, h:h + 1], z[:, 0, b, h * 64:(h + 1) * 64],
                                                         ALU.add, ALU.mult)
                        evac(ins)
                    if u in POOL_AT:
                        g2 = POOL_AT.index(u)
                        bank = aux_in()
                        evac(V.tensor_copy(poolT[:, 2 * g2:2 * g2 + 2, :],
                                           bank[0:64, :].rearrange("p (i t) -> p i t", i=2)))

                dve.wait_ge(bias_loaded, 32)

                def lambdas():
                    dve.wait_ge(lam_exp, 1)
                    for n in range(DEPTH):
                        step(V.tensor_scalar(subln[:, n, :], subln[:, n, :], 1.0 - lam_init(n), None, ALU.mult))
                        step(V.tensor_tensor(lam[:, 2 * n:2 * n + 1], lam[:, 2 * n + 1:2 * n + 2], lam[:, 2 * n:2 * n + 1],
                                             ALU.subtract))
                        step(V.tensor_scalar(lam[:, 2 * n:2 * n + 1], lam[:, 2 * n:2 * n + 1], -lam_init(n), None, ALU.add))

                def scores(u):
                    score_rows(aux_in(), u % 2, bias1[:, u // TB, :], (u % TB + 1) * P, lambda m: m * SEQ)
                    if l == 0 and u == 1:
                        lambdas()

                def turned(u):
                    s, nk = u % 2, (u % TB + 1) * P
                    dve.wait_ge(probs_ready, l * HEADS1 * TB + u + 1)
                    step(V.reciprocal(coef[:, s, 0:2], den[:, s, :]))
                    step(V.tensor_tensor(coef[:, s, 2:3], coef[:, s, 1:2], lam[:, 2 * l:2 * l + 1], ALU.mult))
                    step(V.tensor_scalar(sc[:, s, 0, 0:nk], sc[:, s, 0, 0:nk], coef[:, s, 0:1], None, ALU.mult))
                    V.scalar_tensor_tensor(sc[:, s, 0, 0:nk], sc[:, s, 1, 0:nk], coef[:, s, 2:3],
                                           sc[:, s, 0, 0:nk], ALU.mult, ALU.add).then_inc(attn_ready, 1)
                    turn_in(p_t[:, s, 0:nk].rearrange("p (k q) -> p k q", q=P))

                def values(u):
                    h, b = divmod(u, TB)
                    evac(V.tensor_copy(nat[:, b, 256 + h * P:256 + (h + 1) * P], aux_in()[:, 0:P]))
                    if u >= 2:
                        square(u - 2)

                def square(u):
                    h, b = divmod(u, TB)
                    o = nat[:, b, 256 + h * P:256 + (h + 1) * P]
                    if u >= HEADS1 * TB - 2:
                        read_back()
                    V.tensor_tensor_reduce(out=squares[:, u, :], in0=o, in1=o, scale=1.0, scalar=0.0, op0=ALU.mult,
                                           op1=ALU.add, accum_out=mv[:, b * HEADS1 + h, 1:2]).then_inc(squared, 1)

                pipelined(HEADS1 * TB, scores, turned, values, between)
                for b in range(TB):
                    bank = aux_in()
                    evac(V.tensor_tensor(nat[:, b, 768:1024], bank[:, 0:256], pool_s[:, l, :], ALU.mult))
                square(HEADS1 * TB - 2)
                square(HEADS1 * TB - 1)
                dve.wait_ge(squared, l * HEADS1 * TB + HEADS1 * TB)
                rstd(TB * HEADS1, mv[:, 0:TB * HEADS1, 1], 1.0 / P, EPS1)
                for b in range(TB):
                    for h in range(HEADS1):
                        g = b * HEADS1 + h
                        o = nat[:, b, 256 + h * P:256 + (h + 1) * P]
                        ins = V.scalar_tensor_tensor(o, o, rs_out[:, g:g + 1], subln[:, l, :], ALU.mult, ALU.mult)
                    ins.then_inc(nat_ready, 1)
                turn_all_in()
                add_products(ALPHA)
                layer_norm(2 * l)
                turn_all_in()
                if l == 0:
                    def hidden_in(t, width):
                        for b in range(TB):
                            parts_in([part[:, 4 * t:4 * t + width // P, b * P:(b + 1) * P] for part in hid1_t])

                    step(V.tensor_copy(router_parts[:, :, 0, :], router[:, :, :]))
                    step(V.tensor_tensor(router_parts[:, :, 1, :], router[:, :, :], router_parts[:, :, 0, :],
                                         ALU.subtract))
                    for i, part in enumerate(FF_PARTS):
                        for t, (_, width) in enumerate(part):
                            C.tile.n += 4
                            dve.wait_ge(S.tile_evac, C.tile.n)
                            g = hs[:, t % 2, :, 0:width]
                            V.tensor_tensor(g, g, hu[:, t % 2, :, 0:width], ALU.mult).then_inc(S.gated, 1)
                            C.gated.n += 1
                            if t > 0:
                                hidden_in(t - 1, part[t - 1][1])
                        hidden_in(t, width)
                        add_products(1.0 if i else ALPHA)
                    layer_norm(1)
            V.memset(gates[:, :, :], 0.0)
            V.tensor_scalar(acc[:, :, :], x[:, :, :], ALPHA, None, ALU.mult)
            step(V.memset(rank[:, :, :], -1000.0))
            for b in range(TB):
                bank = aux_in()
                step(V.tensor_copy(logits[:, b, :], bank[:, N_EXP:2 * N_EXP]))
                evac(V.tensor_tensor(logits[:, b, :], logits[:, b, :], bank[:, 0:N_EXP], ALU.add))
            read_back()
            for b in range(TB):
                ins = V.max(top[:, b, :], logits[:, b, :])
            step(ins)
            V.tensor_tensor(small[:, 0:2], top[:, :, 1], top[:, :, 0], ALU.subtract).then_inc(route_dif, 1)
            for b in range(TB):
                ins = V.max_index(topi[:, b, :], top[:, b, :], logits[:, b, :])
            step(ins)
            step(V.tensor_copy(topf[:, :, :], topi[:, :, :]))
            for b in range(TB):
                for i in range(2):
                    ins = V.tensor_scalar(pick[:, b, i, :], iota[:, 0:8], topf[:, b, i:i + 1], None, ALU.is_equal)
            step(ins)
            V.tensor_tensor(mask[:, :, :], pick[:, :, 0, :], pick[:, :, 1, :], ALU.add).then_inc(route_mask, 1)
            dve.wait_ge(route_exp, 1)
            step(V.tensor_scalar(small[:, 10:12], small[:, 8:10], 1.0, None, ALU.add))
            step(V.reciprocal(small[:, 12:14], small[:, 10:12]))
            step(V.tensor_tensor(small[:, 14:16], small[:, 8:10], small[:, 12:14], ALU.mult))
            for b in range(TB):
                ins = V.tensor_scalar(pick[:, b, 1, :], pick[:, b, 1, :], small[:, 14 + b:15 + b], None, ALU.mult)
            step(ins)
            for b in range(TB):
                ins = V.scalar_tensor_tensor(gates[:, b, 0:8], pick[:, b, 0, :], small[:, 12 + b:13 + b],
                                             pick[:, b, 1, :], ALU.mult, ALU.add)
            step(ins)
            bank = aux_in()
            for b in range(TB):
                ins = V.scalar_tensor_tensor(rank[:, b, 0:8], bank[:, b * 8:b * 8 + 8], 1000.0, mask[:, b, :],
                                             ALU.add, ALU.mult)
            step(ins)
            over_cap, place = (excess[:, k, :] for k in range(2))
            evac(V.tensor_scalar(over_cap, bank[:, 16:24], float(CAP), None, ALU.is_gt))
            read_back()
            step(V.tensor_scalar(rank[:, :, 0:8], rank[:, :, 0:8], -1000.0, None, ALU.add))

            def find_extra():
                step(V.memset(place, 0.0))
                for i in range(1, N_EXP):
                    step(V.tensor_tensor(place[:, i:i + 1], place[:, i - 1:i], over_cap[:, i - 1:i], ALU.add))
                for j in range(EXTRA):
                    ins = V.scalar_tensor_tensor(extra_is[:, j, :], place, float(j), over_cap, ALU.is_equal, ALU.mult)
                step(ins)
                for b in range(TB):
                    V.tensor_tensor(extra_of[:, b, :, :], extra_is[:, :, :], over(rank[:, b, 0:8], EXTRA), ALU.mult)
                    V.tensor_tensor(extra_of[:, TB + b, :, :], extra_is[:, :, :], over(gates[:, b, 0:8], EXTRA),
                                    ALU.mult)
                V.tensor_tensor(extra_of[:, 2 * TB, :, :], extra_is[:, :, :], over(iota[:, 0:8], EXTRA), ALU.mult)
                step(V.tensor_reduce(seen[:, 0, :], extra_is[:, :, :], AX.X, ALU.add))
                for b in range(TB):
                    V.tensor_reduce(rank[:, b, N_EXP:ROUNDS], extra_of[:, b, :, :], AX.X, ALU.add)
                    V.tensor_reduce(gates[:, b, N_EXP:ROUNDS], extra_of[:, TB + b, :, :], AX.X, ALU.add)
                V.tensor_reduce(seen[:, 1, :], extra_of[:, 2 * TB, :, :], AX.X, ALU.add)
                step(V.tensor_scalar(seen[:, 2, :], seen[:, 0, :], 1000.0, -1000.0 - CAP, ALU.mult, ALU.add))
                for b in range(TB):
                    ins = V.tensor_tensor(rank[:, b, N_EXP:ROUNDS], rank[:, b, N_EXP:ROUNDS], seen[:, 2, :], ALU.add)
                step(ins)
                V.tensor_copy(extra[:, 0:EXTRA], seen[:, 0, :])
                V.tensor_copy(extra[:, EXTRA:2 * EXTRA], seen[:, 1, :]).then_inc(route_mask, 1)
                dve.wait_ge(route_mask, 2)

            def choose(e):
                col = (lambda v, b: v[:, b, e:e + 1]) if isinstance(e, int) else (
                    lambda v, b: v[:, b, bass.ds(e, 1)])
                for b in range(TB):
                    V.tensor_scalar(sel[:, b, :], iota, col(rank, b), None, ALU.is_equal)
                    ins = V.tensor_scalar(sel_g[:, b, :], iota, col(rank, b), col(gates, b), ALU.is_equal, ALU.mult)
                ins.then_inc(SG[0].picked, 1)

            def gathered():
                for j in range(4):
                    parts_in([part[:, 2 * j:2 * j + 2, :] for part in xg_t])

            def gates_in():
                turn_in(sel_gt)

            def expert(e, _, last):
                start, lead = C.unit.take(MOE_UNITS), EXPERT_HIGHS - 1
                end = start + MOE_UNITS + (0 if last else lead)

                def hidden_in(t):
                    parts_in([part[:, 4 * t:4 * t + 4, :] for part in hide_t])

                for t in range(MOE_TILES):
                    split(start + (t + 1) * KC + lead)
                    n = C.tile.take(2)
                    dve.wait_ge(SG[0].tile_evac, C.tile.at(n) + 2)
                    V.tensor_tensor(hs_e[:, t % 2, :], hs_e[:, t % 2, :], hu_e[:, t % 2, :],
                                    ALU.mult).then_inc(SG[0].gated, 1)
                    C.gated.n += 1
                    if t > 0:
                        hidden_in(t - 1)
                C.tile.take(2)
                C.picked.take()
                choose(e + 1)
                second = start + MOE_TILES * KC
                split(second + GATHER_AT + lead)
                gathered()
                split(min(second + D_FFE // P - 4 + lead, end))
                hidden_in(MOE_TILES - 1)
                split(end)
                for b in range(TB):
                    for h in range(2):
                        y = acc[:, b, h * 512:(h + 1) * 512]
                        evac(V.tensor_tensor(y, y, aux_in()[:, :], ALU.add))
                read_back()
                gates_in()

            choose(0)
            C.picked.n += 1
            C.split.n = C.unit.n = len(STREAM1)
            split(len(STREAM1) + EXPERT_HIGHS - 1)
            gathered()
            gates_in()
            rolled(dve, C, expert, route_mask, extra, EXPERT_HIGHS - 1, (find_extra, N_EXP + 4))
            V.memset(small[:, 21:22], 0.0).then_inc(params_used, 1)
            C, SG[0] = Counts(), S2
            layer_norm(3, acc)

            for l in range(DEPTH):
                if l == 0:
                    dve.wait_ge(nat_ready, TB * (NORM_STAGE[3] + 1))
                rms_norm(4 + 2 * l)
                turn_all_in()
                t0 = C.tile.n
                C.tile.n += 2 * len(ORDER2)
                dve.wait_ge(S2.tile_evac, t0 + 2 * EARLY)
                dve.wait_ge(layer_loaded, 16 * PARAMS2 * (l + 1))
                turn_in(taps[:, :, :])
                step(V.memset(cbuf[:, :], 0.0))
                bank = aux_in()
                for k in range(2):
                    V.tensor_copy(c_t[0:64, 3 * k + 2, 0:CMP_BLOCK], bank[0:64, k * 32:(k + 1) * 32])
                    ins = V.tensor_copy(c_t[64:128, 3 * k + 2, 0:CMP_BLOCK - 1],
                                        bank[0:64, k * 32 + 1:(k + 1) * 32])
                evac(ins)
                for b in range(TB):
                    bank = aux_in()
                    src = bank[0:64, :].rearrange("p (k g t) -> p k g t", k=2, g=2)
                    lo = 1 if b == 0 else 0
                    for k in range(2):
                        V.tensor_copy(c_t[0:64, 3 * k:3 * k + 2, b * P:(b + 1) * P], src[:, k, :, :])
                        ins = V.tensor_copy(c_t[64:128, 3 * k:3 * k + 2, b * P - 1 + lo:(b + 1) * P - 1],
                                            src[:, k, :, lo:P])
                    evac(ins)
                    turn_in(k_t[:, 0:4, b * P:(b + 1) * P])
                    for h in range(2):
                        turn_in(q_t[:, 4 * h:4 * h + 4, b * P:(b + 1) * P])
                for k in range(2):
                    bank = aux_in()
                    evac(V.tensor_copy(hidp[:, k, :], bank[:, 0:45]))
                    read_back()
                    V.memset(small[:, 22:23], 0.0).then_inc(hidc_in, 1)
                bank = aux_in()
                evac(V.tensor_copy(kcmp[:, :, :], bank[0:64, 0:2 * N_CMP].rearrange("p (g n) -> p g n", g=2)))
                bank = aux_in()
                evac(V.tensor_copy(vcmp[:, :, :], bank[0:N_CMP, 0:128].rearrange("p (g d) -> p g d", g=2)))
                bank = aux_in()
                for b in range(TB):
                    n = NSA_H * N_CMP
                    ins = V.tensor_tensor(sc_c[:, b, :, :],
                                          bank[:, b * n:(b + 1) * n].rearrange("p (h n) -> p h n", h=NSA_H),
                                          bias_c[:, b, :, :].rearrange("p n h -> p h n"), ALU.add)
                evac(ins)
                read_back()
                s2 = sc_c[:, :, :, :].rearrange("p b h n -> p (b h) n")
                step(V.tensor_reduce(small[:, 0:16], s2, AX.X, ALU.max))
                step(V.tensor_scalar(small[:, 0:16], small[:, 0:16], -1e29, None, ALU.max))
                V.tensor_tensor(s2, s2, spread(small[:, 0:16], N_CMP), ALU.subtract).then_inc(cmp_scores, 1)
                dve.wait_ge(S2.tile_evac, t0 + 2 * (ORDER2.index(7) + 1))
                for b in range(TB):
                    V.tensor_tensor(z[:, 6, b, :], z[:, 6, b, :], z[:, 7, b, :], ALU.mult).then_inc(conv_in, 1)
                V.memset(u_t[:, :, 0:PAD], 0.0)
                for b in range(TB):
                    turn_in(u_t[:, :, PAD + b * P:PAD + (b + 1) * P])
                read_back()
                V.memset(small[:, 22:23], 0.0).then_inc(conv_ready, 1)

                def convolve(j):
                    for c in range(4):
                        if j > 0:
                            dve.wait_ge(S2.vec, C.own.n - 3)
                            ins = V.scalar_tensor_tensor(y_t[:, c, :], u_t[:, c, j:j + SEQ], taps[:, c, j:j + 1],
                                                         y_t[:, c, :], ALU.mult, ALU.add)
                        else:
                            ins = V.tensor_scalar(y_t[:, c, :], u_t[:, c, j:j + SEQ], taps[:, c, j:j + 1],
                                                  taps[:, c, CONV_W:CONV_W + 1], ALU.mult, ALU.add)
                        C.own.n += 1
                        ins.then_inc(S2.vec, 1)

                convolved = Tally()

                def taps_on(n):
                    for j in range(convolved.n, convolved.n + n):
                        convolve(j)
                    convolved.n += n

                taps_on(TAPS_TURN[0])
                dve.wait_ge(cmp_exp, l + 1)
                step(V.tensor_reduce(small[:, 0:16], s2, AX.X, ALU.add))
                step(V.tensor_scalar(small[:, 0:16], small[:, 0:16], 1e-30, None, ALU.max))
                step(V.reciprocal(small[:, 16:32], small[:, 0:16]))
                step(V.tensor_tensor(small[:, 0:16].rearrange("p (b h) -> p b h", b=TB),
                                     small[:, 16:32].rearrange("p (b h) -> p b h", b=TB),
                                     gates2[:, :, 0:24:3], ALU.mult))
                V.tensor_tensor(s2, s2, spread(small[:, 0:16], N_CMP), ALU.mult).then_inc(cmp_probs, 1)
                for b in range(TB):
                    for h2 in range(2):
                        turn_in(pc_t[:, 4 * h2:4 * h2 + 4, :])
                    evac(V.tensor_copy(o_cmp[:, b, :], aux_in()[:, :]))
                    taps_on(TAPS_TURN[1 + b])

                def between(u):
                    taps_on(TAPS_STEPS[u])

                def scores(u):
                    nk = (u % TB + 1) * P
                    score_rows(aux_in(), u % 2, bias2[:, u // TB, :], nk, lambda m: m * nk)

                def turned(u):
                    h, b = divmod(u, TB)
                    s, nk = u % 2, (b + 1) * P
                    dve.wait_ge(probs_ready, (DEPTH * HEADS1 + l * NSA_H) * TB + u + 1)
                    step(V.reciprocal(coef[:, s, 0:2], den[:, s, :]))
                    step(V.tensor_tensor(coef[:, s, 2:4], coef[:, s, 0:2], gates2[:, b, 3 * h + 1:3 * h + 3], ALU.mult))
                    turn_in(p_t[:, s, 0:2 * nk].rearrange("p (k q) -> p k q", q=P))

                def values(u):
                    h, b = divmod(u, TB)
                    s = u % 2
                    bank = aux_in()
                    o = nat[:, b, h * 64:(h + 1) * 64]
                    step(V.scalar_tensor_tensor(o, bank[:, 0:64], coef[:, s, 2:3], o_cmp[:, b, h * 64:(h + 1) * 64],
                                                ALU.mult, ALU.add))
                    evac(V.scalar_tensor_tensor(o, bank[:, 64:128], coef[:, s, 3:4], o, ALU.mult, ALU.add))

                pipelined(NSA_H * TB, scores, turned, values, between)
                dve.wait_ge(S2.vec, C.own.n)
                dve.wait_ge(pool_taps, (l + 1) * (2 * TAPS_POOL - 1))
                V.tensor_tensor(y_t[:, :, :], y_t[:, :, :],
                                y_pool.rearrange("p b (c t) -> p (b c) t", t=SEQ), ALU.add).then_inc(conv_out, 1)

                t1 = sc[:, 0, 0, :].rearrange("p (h d) -> p h d", h=8)
                t2 = sc[:, 1, 0, :].rearrange("p (h d) -> p h d", h=8)
                dve.wait_ge(S2.tile_evac, t0 + 2 * (ORDER2.index(3) + 1))
                for b in range(TB):
                    qk = z[:, 3, b, :].rearrange("p (h d) -> p h d", h=8)
                    lo, hi = qk[:, :, 0:32], qk[:, :, 32:64]
                    cos, sin = over(rope_cos[:, b, :], 8), over(rope_sin[:, b, :], 8)
                    V.tensor_tensor(t1, hi, sin, ALU.mult)
                    V.tensor_tensor(t2, lo, sin, ALU.mult)
                    V.tensor_tensor(rot[:, b, :, 0:32], lo, cos, ALU.mult)
                    step(V.tensor_tensor(rot[:, b, :, 32:64], hi, cos, ALU.mult))
                    V.tensor_tensor(rot[:, b, :, 0:32], rot[:, b, :, 0:32], t1, ALU.subtract)
                    ins = V.tensor_tensor(rot[:, b, :, 32:64], rot[:, b, :, 32:64], t2, ALU.add)
                    if b == TB - 1:
                        ins.then_inc(rot_ready, 1)
                    else:
                        step(ins)
                for b in range(TB):
                    for h in range(2):
                        turn_in(q_t[:, 4 * h:4 * h + 4, b * P:(b + 1) * P])
                for b in range(TB):
                    turn_in(o_conv[:, b, :].rearrange("p (c d) -> p c d", c=4))

                dve.wait_ge(tables_loaded, 16 * TABLES2 * (l + 1))

                def ret_scores(h):
                    bank = aux_in()
                    evac(V.tensor_tensor(p_t[:, h % 2, 0:3 * P], bank[:, 0:3 * P], decay[:, h, :], ALU.mult))

                def ret_values(h):
                    bank = aux_in()
                    evac(V.tensor_copy(nat[:, :, 512 + h * P:512 + (h + 1) * P],
                                       bank[:, 0:2 * P].rearrange("p (b d) -> p b d", b=TB)))

                ret_scores(0)
                for h in range(RET_H):
                    if h + 1 < RET_H:
                        ret_scores(h + 1)
                    ret_values(h)
                read_back()
                for b in range(TB):
                    parts_in([part[:, :, b * P:(b + 1) * P] for part in br_t[0]])
                dve.wait_ge(S2.tile_evac, t0 + 2 * (ORDER2.index(5) + 1))
                for b in range(TB):
                    ins = V.tensor_tensor(z[:, 5, b, :], z[:, 5, b, :], ret_gn[:, :], ALU.mult)
                step(ins)
                heads = [nat[:, b, 512 + h * P:512 + (h + 1) * P] for b in range(TB) for h in range(RET_H)]
                for g, o in enumerate(heads):
                    ins = V.bn_stats(stats[:, g, 0, :], o)
                step(ins)
                for g in range(len(heads)):
                    ins = V.bn_aggr(mv[:, g, :], stats[:, g, 0, :])
                step(ins)
                rstd(len(heads), mv[:, 0:len(heads), 1], 1.0, EPS2)
                for b in range(TB):
                    for h in range(RET_H):
                        g = b * RET_H + h
                        ins = V.scalar_tensor_tensor(heads[g], heads[g], mv[:, g, 0:1], z[:, 5, b, h * P:(h + 1) * P],
                                                     ALU.subtract, ALU.mult)
                    step(ins)
                    o = nat[:, b, 512:1024].rearrange("p (h d) -> p h d", h=RET_H)
                    V.tensor_tensor(o, o, spread(rs_out[:, b * RET_H:(b + 1) * RET_H], P),
                                    ALU.mult).then_inc(nat_ready, 1)
                for b in range(TB):
                    parts_in([part[:, :, b * P:(b + 1) * P] for part in br_t[1]])
                standardise(o_conv, o_conv, EPS2)
                for b in range(TB):
                    o = o_conv[:, b, :]
                    step(V.tensor_tensor(o, o, conv_ln[:, 0, :], ALU.mult))
                    V.tensor_tensor(o, o, conv_ln[:, 1, :], ALU.add).then_inc(conv_norm, 1)
                for r in range(3):
                    for b in range(TB):
                        C.tile.n += 2
                        dve.wait_ge(S2.tile_evac, C.tile.n)
                        for h in range(2):
                            at = slice(h * 512, (h + 1) * 512)
                            g, product, total = sig[2 * r + h][:, b, :], acc[:, b, at], nat[:, b, at]
                            if r == 0:
                                ins = V.tensor_tensor(total, g, product, ALU.mult)
                            else:
                                ins = V.tensor_tensor(g, g, product, ALU.mult)
                            if h == 1 and r < 2:
                                ins.then_inc(merged, 1)
                        if r == 0:
                            if b == TB - 1:
                                for c in range(TB):
                                    parts_in([part[:, :, c * P:(c + 1) * P] for part in br_t[2]])
                            continue
                        if r == 1:
                            dve.wait_ge(merged, (2 * l + 1) * TB + b + 1)
                        else:
                            step(ins)
                        for h in range(2):
                            at = slice(h * 512, (h + 1) * 512)
                            ins = V.tensor_tensor(nat[:, b, at], nat[:, b, at], sig[2 * r + h][:, b, :], ALU.add)
                        if r == 1:
                            step(ins)
                        else:
                            ins.then_inc(nat_ready, 1)
                turn_all_in()
                add_products(1.0)
                rms_norm(5 + 2 * l)
                turn_all_in()

                def hidden_in(t):
                    for b in range(TB):
                        parts_in([part[:, 4 * t:4 * t + 4, b * P:(b + 1) * P] for part in hid2_t])

                for i, part in enumerate(FF2_PARTS):
                    for t in range(len(part)):
                        C.tile.n += 2
                        dve.wait_ge(S2.tile_evac, C.tile.n)
                        g = hs[:, t % 2, :, :]
                        V.tensor_tensor(g, g, g, ALU.mult).then_inc(gated2, 1)
                        if t > 0:
                            hidden_in(t - 1)
                    hidden_in(t)
                    if i == len(FF2_PARTS) - 1:
                        read_back()
                        V.memset(small[:, 21:22], 0.0).then_inc(params_used, 1)
                    add_products(1.0)
            rms_norm(8)


def buckets(dist):
    n = np.maximum(dist, 0)
    exact = BUCKETS // 2
    far = np.maximum(n, 1).astype(np.float32)
    large = exact + (np.log(far / np.float32(exact)) / np.float32(math.log(MAX_DIST / exact))
                     * np.float32(BUCKETS - exact)).astype(np.int32)
    return np.where(n < exact, n, np.minimum(large, BUCKETS - 1))


def one_hot_buckets(dist):
    rows = (np.arange(BUCKETS).reshape(-1, *[1] * dist.ndim) == buckets(dist)) & (dist >= 0)
    return np.concatenate([rows.astype(np.float32), np.where(dist < 0, NEG, 0.0).astype(np.float32)[None]])


def tables():
    i = np.arange(P)
    half = RET_DK // 2
    inv = 10000.0 ** (-np.arange(half, dtype=np.float32) / np.float32(half))
    ang = (np.arange(SEQ, dtype=np.float32)[:, None] * inv[None, :].astype(np.float32)).astype(np.float32)
    trig = [f(ang.astype(np.float64)).reshape(TB, P, half).transpose(1, 0, 2).reshape(P, TB * half)
            for f in (np.cos, np.sin)]
    small = np.concatenate([np.eye(P), i[:, None] <= i[None, :], i[:, None] < i[None, :],
                            np.broadcast_to(i, (P, P)), *trig], axis=1)
    rows = one_hot_buckets(SEQ - 1 - np.arange(512))
    block_end = CMP_STRIDE * np.arange(N_CMP) + CMP_BLOCK - 1
    dist_c = np.arange(SEQ).reshape(TB, 1, P) - block_end.reshape(1, N_CMP, 1)
    onehot = np.concatenate([rows, one_hot_buckets(dist_c).reshape(BUCKETS + 1, -1)], axis=1)
    t = np.arange(SEQ)
    pool = []
    for w in WINDOWS:
        inside = (t[:, None] <= t[None, :]) & (t[:, None] > t[None, :] - w)
        pool.append(inside / np.minimum(t + 1, w)[None, :] - np.eye(SEQ))
    pool = np.stack(pool).reshape(4, TB, P, SEQ).transpose(2, 1, 0, 3).reshape(P, -1)
    log_g = np.log1p(-np.exp2(-5.0 - np.arange(RET_H)))
    diff = t[None, :] - i[:, None]
    decay = np.where(diff >= 0, np.exp(log_g[:, None, None] * np.maximum(diff, 0)), 0.0) * RET_DK ** -0.5
    decay = np.concatenate([decay, decay[:, :, 0:P]], axis=2).transpose(1, 0, 2).reshape(P, -1)
    named = {"c_small": small, "c_onehot": onehot, "c_pool": pool, "c_decay": decay}
    return {n: np.ascontiguousarray(v, dtype=np.float32) for n, v in named.items()}


def kernel(**inputs):
    import concourse.bacc as bacc
    from concourse.bass_utils import run_bass_kernel_spmd

    nc = bacc.Bacc("TRN2", target_bir_lowering=False, num_devices=1)
    arrays, aps = {}, {}
    for name, a in {**inputs, **tables()}.items():
        a = np.ascontiguousarray(a)
        arrays[f"in_{name}"] = a
        aps[name] = nc.dram_tensor(f"in_{name}", a.shape, mybir.dt.from_np(a.dtype), kind="ExternalInput").ap()
    out = nc.dram_tensor("out_x", (1, SEQ, D), F32, kind="ExternalOutput").ap()
    build(nc, aps, out)
    r = run_bass_kernel_spmd(nc, [arrays], core_ids=[0])
    return r.results[0]["out_x"]
```
